# Optimizing a Trainium2 kernel written in Bass

```python
import jax, jax.numpy as jnp
from jax import lax
import numpy as np

D_MODEL = 1024
BATCH = 1
SEQ = 256
DEPTH = 1

EPS = 1e-6
ROPE_THETA = 500000.0
Q_BLOCK = 128
MLA_HEADS = 8
MLA_Q_LORA = 256
MLA_KV_LORA = 128
MLA_NOPE = 64
MLA_ROPE = 32
MLA_V = 64
DSA_HEADS = 8
DSA_HEAD_DIM = 64
DSA_ROT = DSA_HEAD_DIM // 4
IDX_HEADS = 8
IDX_DIM = 64
IDX_ROT = IDX_DIM // 4
TOPK_MAX = 256
N_EXPERTS = 32
TOP_K = 4
D_FF = 1024
SWIGLU_LIMIT = 7.0
SWIGLU_ALPHA = 1.702
EXPERT_BLOCK = 256
IN_SPLITS = (MLA_Q_LORA, MLA_KV_LORA, MLA_ROPE,
             DSA_HEADS * DSA_HEAD_DIM, DSA_HEAD_DIM, DSA_HEAD_DIM,
             IDX_HEADS * IDX_DIM, IDX_DIM, IDX_HEADS,
             D_MODEL, D_MODEL)
D_IN = 256 + 128 + 32 + 512 + 64 + 64 + 512 + 64 + 8 + D_MODEL + D_MODEL

kernel_name = 'hybrid_mla_dsa_gated_moe_block'

def rms_norm(x, g):
    xf = x.astype(jnp.float32)
    y = xf * lax.rsqrt(jnp.mean(xf * xf, axis=-1, keepdims=True) + EPS)
    return (y * g.astype(jnp.float32)).astype(x.dtype)

def rope_partial(x, pos, rot_dim):
    half = rot_dim // 2
    inv_freq = ROPE_THETA ** (-jnp.arange(half, dtype=jnp.float32) / half)
    ang = pos.astype(jnp.float32)[:, :, None, None] * inv_freq
    cos, sin = jnp.cos(ang), jnp.sin(ang)
    x1 = x[..., :half].astype(jnp.float32)
    x2 = x[..., half:rot_dim].astype(jnp.float32)
    rot = jnp.concatenate([x1 * cos - x2 * sin, x2 * cos + x1 * sin], axis=-1).astype(x.dtype)
    return jnp.concatenate([rot, x[..., rot_dim:]], axis=-1)

def split_cols(z, sizes):
    outs, off = [], 0
    for s in sizes:
        outs.append(z[..., off:off + s])
        off += s
    return outs

def to_blocks(a, nb):
    return a.reshape(a.shape[0], nb, Q_BLOCK, *a.shape[2:]).swapaxes(0, 1)

def from_blocks(o):
    nb, b = o.shape[0], o.shape[1]
    return o.swapaxes(0, 1).reshape(b, nb * Q_BLOCK, -1)

def mla_branch(c_q, c_kv, k_pe, pos, q_norm_g, w_uq, kv_norm_g, w_ukv):
    B, S, _ = c_q.shape
    nb = S // Q_BLOCK
    q = (rms_norm(c_q, q_norm_g) @ w_uq).reshape(B, S, MLA_HEADS, MLA_NOPE + MLA_ROPE)
    q_nope = q[..., :MLA_NOPE]
    q_pe = rope_partial(q[..., MLA_NOPE:], pos, MLA_ROPE)
    kv = (rms_norm(c_kv, kv_norm_g) @ w_ukv).reshape(B, S, MLA_HEADS, MLA_NOPE + MLA_V)
    k_nope, v = kv[..., :MLA_NOPE], kv[..., MLA_NOPE:]
    k_rot = rope_partial(k_pe[:, :, None, :], pos, MLA_ROPE)[:, :, 0]
    key_pos = jnp.arange(S)
    scale = (MLA_NOPE + MLA_ROPE) ** -0.5

    def attend_block(args):
        i, qn, qp = args
        s = (jnp.einsum('bqhd,bkhd->bhqk', qn, k_nope)
             + jnp.einsum('bqhr,bkr->bhqk', qp, k_rot)).astype(jnp.float32) * scale
        q_pos = i * Q_BLOCK + jnp.arange(Q_BLOCK)
        s = jnp.where(key_pos[None, :] <= q_pos[:, None], s, -jnp.inf)
        p = jax.nn.softmax(s, axis=-1).astype(v.dtype)
        return jnp.einsum('bhqk,bkhd->bqhd', p, v)

    out = lax.map(attend_block, (jnp.arange(nb), to_blocks(q_nope, nb), to_blocks(q_pe, nb)))
    return from_blocks(out)

def dsa_branch(q, k, v, q_idx, k_idx, w_idx, pos):
    B, S, _ = q.shape
    nb = S // Q_BLOCK
    topk = min(TOPK_MAX, S // 4)
    q = rope_partial(q.reshape(B, S, DSA_HEADS, DSA_HEAD_DIM), pos, DSA_ROT)
    k = rope_partial(k[:, :, None, :], pos, DSA_ROT)[:, :, 0]
    q_idx = rope_partial(q_idx.reshape(B, S, IDX_HEADS, IDX_DIM), pos, IDX_ROT)
    k_idx = rope_partial(k_idx[:, :, None, :], pos, IDX_ROT)[:, :, 0]
    w_idx = w_idx.astype(jnp.float32) * IDX_HEADS ** -0.5
    key_pos = jnp.arange(S)
    gather_rows = jax.vmap(lambda table, idx: table[idx])

    def attend_block(args):
        i, qb, qib, wib = args
        q_pos = i * Q_BLOCK + jnp.arange(Q_BLOCK)
        causal = key_pos[None, :] <= q_pos[:, None]
        rel = jax.nn.relu(jnp.einsum('bqhd,bkd->bqhk', qib, k_idx).astype(jnp.float32) * IDX_DIM ** -0.5)
        score = jnp.einsum('bqh,bqhk->bqk', wib, rel)
        score = jnp.where(causal[None], score, -jnp.inf)
        _, sel = lax.top_k(score, topk)
        valid = sel <= q_pos[None, :, None]
        k_sel = gather_rows(k, sel)
        v_sel = gather_rows(v, sel)
        s = jnp.einsum('bqhd,bqkd->bhqk', qb, k_sel).astype(jnp.float32) * DSA_HEAD_DIM ** -0.5
        s = jnp.where(valid[:, None], s, -jnp.inf)
        p = jax.nn.softmax(s, axis=-1).astype(v.dtype)
        return jnp.einsum('bhqk,bqkd->bqhd', p, v_sel)

    out = lax.map(attend_block, (jnp.arange(nb), to_blocks(q, nb), to_blocks(q_idx, nb), to_blocks(w_idx, nb)))
    return from_blocks(out)

def moe_ffn(h, router_w, router_b, w_gu, b_gu, w_d, b_d):
    B, S, D = h.shape
    t = h.reshape(B * S, D)
    n_tok = t.shape[0]
    n_assign = n_tok * TOP_K
    n_blk = -(-n_assign // EXPERT_BLOCK) + N_EXPERTS
    logits = (t @ router_w + router_b).astype(jnp.float32)
    top_logit, top_e = lax.top_k(logits, TOP_K)
    gate = jax.nn.softmax(top_logit, axis=-1)
    flat_e = top_e.reshape(-1)
    order = jnp.argsort(flat_e)
    e_sorted = flat_e[order]
    tok_sorted = order // TOP_K
    gate_sorted = gate.reshape(-1)[order]
    counts = jnp.bincount(flat_e, length=N_EXPERTS)
    padded = (counts + EXPERT_BLOCK - 1) // EXPERT_BLOCK * EXPERT_BLOCK
    pad_end = jnp.cumsum(padded)
    pad_start = pad_end - padded
    sort_start = jnp.cumsum(counts) - counts
    dest = pad_start[e_sorted] + jnp.arange(n_assign) - sort_start[e_sorted]
    xbuf = jnp.zeros((n_blk * EXPERT_BLOCK, D), t.dtype).at[dest].set(t[tok_sorted])
    blk_e = jnp.minimum(jnp.searchsorted(pad_end, jnp.arange(n_blk) * EXPERT_BLOCK, side='right'), N_EXPERTS - 1)

    def expert_block(args):
        xb, e = args
        gu = xb @ w_gu[e] + b_gu[e]
        glu = jnp.minimum(gu[:, :D_FF], SWIGLU_LIMIT)
        lin = jnp.clip(gu[:, D_FF:], -SWIGLU_LIMIT, SWIGLU_LIMIT)
        act = glu * jax.nn.sigmoid(SWIGLU_ALPHA * glu) * (lin + 1.0)
        return act @ w_d[e] + b_d[e]

    ybuf = lax.map(expert_block, (xbuf.reshape(n_blk, EXPERT_BLOCK, D), blk_e))
    y = ybuf.reshape(-1, D)[dest] * gate_sorted[:, None].astype(t.dtype)
    out = jax.ops.segment_sum(y, tok_sorted, num_segments=n_tok)
    return out.reshape(B, S, D)

def setup_inputs(seed: int = 0) -> dict:
    key = jax.random.key(seed)
    ks = jax.random.split(key, 20)
    f32 = jnp.float32
    L = DEPTH

    def nrm(k, shape, scale):
        return jax.random.normal(k, shape, f32) * scale

    def gain(k, shape):
        return 1.0 + 0.1 * jax.random.normal(k, shape, f32)

    return {
        'x': nrm(ks[0], (BATCH, SEQ, D_MODEL), 1.0),
        'positions': jnp.tile(jnp.arange(SEQ, dtype=jnp.int32)[None, :], (BATCH, 1)),
        'attn_norm_g': gain(ks[1], (L, D_MODEL)),
        'w_in': nrm(ks[2], (L, D_MODEL, D_IN), D_MODEL ** -0.5),
        'mla_q_norm_g': gain(ks[3], (L, MLA_Q_LORA)),
        'mla_w_uq': nrm(ks[4], (L, MLA_Q_LORA, MLA_HEADS * (MLA_NOPE + MLA_ROPE)), MLA_Q_LORA ** -0.5),
        'mla_kv_norm_g': gain(ks[5], (L, MLA_KV_LORA)),
        'mla_w_ukv': nrm(ks[6], (L, MLA_KV_LORA, MLA_HEADS * (MLA_NOPE + MLA_V)), MLA_KV_LORA ** -0.5),
        'w_branch_mla': nrm(ks[7], (L, MLA_HEADS * MLA_V, D_MODEL), (MLA_HEADS * MLA_V) ** -0.5),
        'w_branch_dsa': nrm(ks[8], (L, DSA_HEADS * DSA_HEAD_DIM, D_MODEL), (DSA_HEADS * DSA_HEAD_DIM) ** -0.5),
        'w_out': nrm(ks[9], (L, D_MODEL, D_MODEL), D_MODEL ** -0.5),
        'ffn_norm_g': gain(ks[10], (L, D_MODEL)),
        'router_w': nrm(ks[11], (L, D_MODEL, N_EXPERTS), D_MODEL ** -0.5),
        'router_b': nrm(ks[12], (L, N_EXPERTS), 0.01),
        'w_gate_up': nrm(ks[13], (L, N_EXPERTS, D_MODEL, 2 * D_FF), D_MODEL ** -0.5),
        'b_gate_up': nrm(ks[14], (L, N_EXPERTS, 2 * D_FF), 0.02),
        'w_down': nrm(ks[15], (L, N_EXPERTS, D_FF, D_MODEL), D_FF ** -0.5),
        'b_down': nrm(ks[16], (L, N_EXPERTS, D_MODEL), 0.02),
        'final_norm_g': gain(ks[17], (D_MODEL,)),
    }

def reference(x, positions, attn_norm_g, w_in, mla_q_norm_g, mla_w_uq, mla_kv_norm_g, mla_w_ukv,
              w_branch_mla, w_branch_dsa, w_out, ffn_norm_g, router_w, router_b,
              w_gate_up, b_gate_up, w_down, b_down, final_norm_g):
    for l in range(DEPTH):
        h = rms_norm(x, attn_norm_g[l])
        z = h @ w_in[l]
        (c_q, c_kv, k_pe, q_b, k_b, v_b, q_idx, k_idx, w_idx, gate_a, gate_b) = split_cols(z, IN_SPLITS)
        y_a = mla_branch(c_q, c_kv, k_pe, positions, mla_q_norm_g[l], mla_w_uq[l], mla_kv_norm_g[l], mla_w_ukv[l])
        y_b = dsa_branch(q_b, k_b, v_b, q_idx, k_idx, w_idx, positions)
        merged = (jax.nn.sigmoid(gate_a) * (y_a @ w_branch_mla[l])
                  + jax.nn.sigmoid(gate_b) * (y_b @ w_branch_dsa[l]))
        x = x + merged @ w_out[l]
        x = x + moe_ffn(rms_norm(x, ffn_norm_g[l]), router_w[l], router_b[l],
                        w_gate_up[l], b_gate_up[l], w_down[l], b_down[l])
    return rms_norm(x, final_norm_g)


_drawn_inputs = setup_inputs


def setup_inputs(seed=0):
    import zlib

    import numpy as np

    out = dict(_drawn_inputs(seed))
    spreads = {}
    factors = {'b_gate_up': 5.161, 'b_down': 5.973}
    for name, (base, spread) in spreads.items():
        noise = np.random.default_rng([zlib.crc32(name.encode()), seed]).standard_normal(out[name].shape)
        drawn = base * np.exp(spread * noise) if base else spread * noise
        out[name] = __import__('jax').numpy.asarray(drawn.astype(out[name].dtype))
    for name, factor in factors.items():
        out[name] = (out[name] * factor).astype(out[name].dtype)
    return out
```

```python
from contextlib import ExitStack

import numpy as np

import concourse.bass as bass
from concourse import mybir

ALU = mybir.AluOpType
ACT = mybir.ActivationFunctionType
AXX = mybir.AxisListType.X
F32 = mybir.dt.float32
F32R = mybir.dt.float32r
I32 = mybir.dt.int32

P = 128
TOKENS, D = 256, 1024
TT = TOKENS // P
EPS = 1e-6
THETA = 500000.0
NEG = -1.0e30
REMOVED = -3.0e38

HEADS = 8
Q_LORA, KV_LORA, NOPE, ROPE, V_DIM = 256, 128, 64, 32, 64
QK = NOPE + ROPE
HD, ROT = 64, 16
TOPK = min(256, TOKENS // 4)
GATES_AT = Q_LORA + KV_LORA + ROPE + 2 * HEADS * HD + 3 * HD + HEADS
D_IN = GATES_AT + 2 * D
C_QB = Q_LORA + KV_LORA + ROPE
C_KB = C_QB + HEADS * HD
C_QI = C_KB + 2 * HD
C_KI = C_QI + HEADS * HD

EXPERTS, EXP_K, FF = 32, 4, 1024
LIMIT, ALPHA = 7.0, 1.702
SLOTS = 64
CHUNKS = TOKENS // SLOTS
TABLE = EXPERTS * (CHUNKS + 1)

KC = D // P
BLK = 512
UNIT = KC * BLK
RING = 6
FRONT_UNITS = 13
UNITS = 6
PIECES = 2 * UNITS
SPLITS = 3
GU_COLS = [0, FF, BLK, FF + BLK]

Z_UNITS = [[(C_QI, 512)], [(C_KB, 128), (C_KI, HD + HEADS)], [(C_QB, 512)], [(0, C_QB)]]

BATCHES = [(0, (0, 2, 4, 6)), (0, (1, 3, 5, 7)),
           (1, (0, 2)), (1, (1, 3)), (1, (4, 6)), (1, (5, 7))]

CONST = {"ident": P, "ident2": SLOTS, "before": P, "ones": P, "slot": P, "causal": P, "invfreq": ROPE // 2}
CONST_AT = {}
for _name, _n in CONST.items():
    CONST_AT[_name] = sum(CONST[k] for k in CONST_AT)


def constants():
    r = np.arange(P)
    part = {
        "ident": np.eye(P),
        "ident2": (r[:, None] % SLOTS == np.arange(SLOTS)[None, :]),
        "before": (r[:, None] < r[None, :]),
        "ones": np.ones((P, P)),
        "slot": np.broadcast_to(r[None, :] % SLOTS, (P, P)),
        "causal": np.where(r[None, :] <= r[:, None], 0.0, NEG),
        "invfreq": np.broadcast_to(
            (np.float32(THETA) ** (-np.arange(ROPE // 2, dtype=np.float32) / np.float32(ROPE // 2))), (P, ROPE // 2)),
    }
    return np.concatenate([part[k].astype(np.float32) for k in CONST], axis=1)


def build(nc, x, positions, attn_norm_g, w_in, mla_q_norm_g, mla_w_uq, mla_kv_norm_g, mla_w_ukv,
          w_branch_mla, w_branch_dsa, w_out, ffn_norm_g, router_w, router_b,
          w_gate_up, b_gate_up, w_down, b_down, final_norm_g, consts, out):
    ctx = ExitStack()
    front = ExitStack()
    with ctx:
        def sb(name, shape, dt=F32, scope=ctx):
            return scope.enter_context(nc.sbuf_tensor(name, shape, dt))

        def sem(name):
            return ctx.enter_context(nc.semaphore(name))

        cst = sb("cst", [P, sum(CONST.values())])
        xs = sb("x_res", [P, TT, D])
        gain = sb("gain", [P, D])
        bias_gu = sb("bias_gu", [P, EXPERTS, 16])
        raw = sb("raw", [P, RING, UNIT])
        stat = sb("stat", [P, 16])
        posc = sb("posc", [P, TT, TABLE])
        gates = sb("gates", [P, TT, TABLE])
        h2 = sb("h2", [P, TT, D])
        n_items = sb("n_items", [P, 1], I32)

        def fb(name, shape, dt=F32):
            return sb(name, shape, dt, front)

        hT = fb("hT", [P, KC, TOKENS])
        area_k = fb("area_k", [P, HEADS * TOKENS])
        z_qi = area_k[:, 0:4 * TOKENS].rearrange("p (t n) -> p t n", t=TT)
        dsaT = area_k[:, 0:4 * TOKENS].rearrange("p (j t) -> p j t", j=4)
        c_qT = area_k[:, 4 * TOKENS:6 * TOKENS].rearrange("p (c t) -> p c t", c=2)
        c_kvT = area_k[:, 6 * TOKENS:7 * TOKENS]
        diag = area_k[:, 7 * TOKENS:8 * TOKENS].rearrange("p (t n) -> p t n", t=TT)
        kmT = area_k[0:QK, :].rearrange("p (h t) -> p h t", h=HEADS)
        z_kv = fb("z_kv", [P, TT, 200])
        z_qb = fb("z_qb", [P, TT, 512])
        z_ml = fb("z_ml", [P, TT, C_QB])
        sgT = fb("sgT", [P, KC, 2, TOKENS])
        qT = fb("qT", [P, 4, TOKENS])
        kT = fb("kT", [P, TOKENS])
        kk = fb("kk", [P, TT, 2, HD])
        score = fb("score", [P, TT, TOKENS])
        work = fb("work", [P, TT, TOKENS])
        pick = fb("pick", [P, 3, TOKENS])
        allow = fb("allow", [P, TT, TOKENS])
        area_p = fb("area_p", [P, 4 * BLK])
        prob = area_p[:, 0:2 * BLK].rearrange("p (b n) -> p b n", b=2)
        probT = area_p[:, 2 * BLK:4 * BLK].rearrange("p (b n) -> p b n", b=2)
        k_ml = area_p[:, 0:TT * HEADS * QK].rearrange("p (t h d) -> p t h d", t=TT, h=HEADS)
        q_ml = fb("q_ml", [P, TT, HEADS, QK])
        v_ml = fb("v_ml", [P, TT, HEADS, V_DIM])
        bgu = h2[0:EXPERTS, :, :].rearrange("p t n -> p (t n)")
        qmT = h2[0:QK, :, :].rearrange("p t n -> p (t n)").rearrange("p (h t) -> p h t", h=HEADS)
        rstd_row = fb("rstd_row", [P, TOKENS])
        g_in = fb("g_in", [P, KC])
        g_q = fb("g_q", [P, 2])
        g_kv = fb("g_kv", [P, 1])
        pos_i = fb("pos_i", [P, TT], I32)
        pos_f = fb("pos_f", [P, TT])
        ang = fb("ang", [P, 2, TT, 16])
        turns = fb("turns", [P, 2, TT, 16])
        trig = fb("trig", [P, 2, TT, 16])
        nsin = fb("nsin", [P, TT, 16])
        ropa = fb("ropa", [P, TT, HEADS, ROT])
        ropb = fb("ropb", [P, TT, HEADS, ROT])
        ropc = fb("ropc", [P, TT, HEADS, ROPE])
        ropd = fb("ropd", [P, TT, HEADS, ROPE])
        w_idx = fb("w_idx", [P, TT, HEADS])
        top8 = fb("top8", [P, TT, 8])
        cnt = fb("cnt", [P, TT])
        mx = fb("mx", [P, 2, 4])
        den = fb("den", [P, 2, 4])
        rw = fb("rw", [P, KC, EXPERTS])
        rb = fb("rb", [P, EXPERTS])
        lg, r_a, r_b, sel, gate, pm = (
            z_ml[:, :, :].rearrange("p t n -> p (t n)")[:, k * TT * EXPERTS:(k + 1) * TT * EXPERTS]
            .rearrange("p (t e) -> p t e", t=TT) for k in range(6))
        r_s = fb("r_s", [P, TT, 4])
        gateT = z_qb[0:EXPERTS, 0, 0:TOKENS]
        q_ml_flat = q_ml[:, :, :, :].rearrange("p t h d -> p (t h d)")
        mlaT = q_ml_flat[:, 0:4 * TOKENS].rearrange("p (j t) -> p j t", j=4)
        bd = q_ml_flat[0:EXPERTS, 0:D]
        front.close()

        hi = sb("w_hi", [P, SPLITS, 4, BLK], F32R)
        lo = sb("w_lo", [P, SPLITS, 4, BLK], F32R)
        xe = sb("x_split", [P, KC, 2, SLOTS], F32R)
        ae = sb("a_split", [P, KC, 2, SLOTS], F32R)
        ev = sb("ev", [P, 2, BLK])
        onehot = sb("onehot", [P, TT, SLOTS])
        gated = sb("gated", [P, TT, P])
        scat = sb("scat", [P, TOKENS])
        gub = sb("gub", [P, 2, 4, SLOTS])
        glu = sb("glu", [P, 4, SLOTS])
        lin = sb("lin", [P, 4, SLOTS])
        sig = sb("sig", [P, 4, SLOTS])
        prod = sb("prod", [P, 4, SLOTS])
        actv = sb("actv", [P, 4, SLOTS])

        B = [ctx.enter_context(nc.psum_tensor(f"bank{i}", [P, BLK], F32)) for i in range(8)]
        ZB, TB, SB, VB = B[0:2], B[2:4], B[4:6], B[6:8]
        ACC, MM, PREP, GUT = B[0:4], B[4:6], B[6], B[7]

        def const(name, rows=P):
            a = CONST_AT[name]
            return cst[0:rows, a:a + CONST[name]]

        ident = const("ident")

        x_in = sem("x_in")
        cst_in = sem("cst_in")
        small_in = sem("small_in")
        SMALL = 16 * 10
        bd_in = sem("bd_in")
        gain_in = sem("gain_in")
        raw_in = [sem(f"raw_in{i}") for i in range(RING)]
        out_done = sem("out_done")
        act_step = sem("act_step")
        dve_step = sem("dve_step")
        pool_step = sem("pool_step")
        x_sq = sem("x_sq")
        x_ms = sem("x_ms")
        x_rt = sem("x_rt")
        diag_ok = sem("diag_ok")
        xT_ps = sem("xT_ps")
        rstd_ps = sem("rstd_ps")
        hT_ok = sem("hT_ok")
        ang_ok = sem("ang_ok")
        trig_ok = sem("trig_ok")
        nsin_ok = sem("nsin_ok")
        bgu_ps = sem("bgu_ps")
        bgu_ok = sem("bgu_ok")
        z_ps = sem("z_ps")
        z_ok = sem("z_ok")
        qi_rot = sem("qi_rot")
        qi_ps = sem("qi_ps")
        qi_ok = sem("qi_ok")
        idx_ps = sem("idx_ps")
        idx_rl = sem("idx_rl")
        idx_ac = sem("idx_ac")
        c_sq = sem("c_sq")
        c_ms = sem("c_ms")
        c_rt = sem("c_rt")
        c_rs = sem("c_rs")
        c_ps = sem("c_ps")
        c_ok = sem("c_ok")
        up_ps = sem("up_ps")
        up_a = sem("up_a")
        up_d = sem("up_d")
        ml_rot = sem("ml_rot")
        qb_rot = sem("qb_rot")
        mT_ps = sem("mT_ps")
        mq_ok = sem("mq_ok")
        mk_ok = sem("mk_ok")
        g_ps = sem("g_ps")
        g_ok = sem("g_ok")
        s_ps = sem("s_ps")
        s_mx = sem("s_mx")
        p_ex = sem("p_ex")
        p_ok = sem("p_ok")
        pT_ps = sem("pT_ps")
        pT_ok = sem("pT_ok")
        pv_ps = sem("pv_ps")
        pv_ok = sem("pv_ok")
        qd_ps = sem("qd_ps")
        qd_ok = sem("qd_ok")
        allow_ok = sem("allow_ok")
        sig_ok = sem("sig_ok")
        br_ps = sem("br_ps")
        br_ok = sem("br_ok")
        wo_ps = sem("wo_ps")
        x1_ok = sem("x1_ok")
        f_sq = sem("f_sq")
        f_ms = sem("f_ms")
        f_rt = sem("f_rt")
        h2_ok = sem("h2_ok")
        h2T_ps = sem("h2T_ps")
        h2T_ok = sem("h2T_ok")
        lg_ps = sem("lg_ps")
        lg_mx = sem("lg_mx")
        lg_ex = sem("lg_ex")
        sel_ok = sem("sel_ok")
        gate_ok = sem("gate_ok")
        pos_ps = sem("pos_ps")
        gT_ps = sem("gT_ps")
        gT_ok = sem("gT_ok")
        n_ok = sem("n_ok")
        prep_ok = sem("prep_ok")
        gath_ps = sem("gath_ps")
        xh_ok = sem("xh_ok")
        xl_ok = sem("xl_ok")
        sc_ps = sem("sc_ps")
        sc_ok = sem("sc_ok")
        hi_ok = sem("hi_ok")
        lo_ok = sem("lo_ok")
        used = sem("used")
        ev_ok = sem("ev_ok")
        ev_used = sem("ev_used")
        gub_ok = sem("gub_ok")
        glu_ok = sem("glu_ok")
        lin_ok = sem("lin_ok")
        sig2_ok = sem("sig2_ok")
        prod_ok = sem("prod_ok")
        actv_ok = sem("actv_ok")
        ah_ok = sem("ah_ok")
        al_ok = sem("al_ok")
        y_ok = sem("y_ok")
        y_sq = sem("y_sq")
        y_ms = sem("y_ms")
        y_rt = sem("y_rt")
        o_ok = sem("o_ok")
        fin_r = sem("fin_r")

        w_in_v = w_in[0].rearrange("(p c) n -> p c n", c=KC)
        w_uq_v = mla_w_uq[0].rearrange("(p c) n -> p c n", c=2)
        w_ukv_v = mla_w_ukv[0]
        w_br_v = [w[0].rearrange("(c p) n -> p c n", p=P) for w in (w_branch_mla, w_branch_dsa)]
        w_out_v = w_out[0].rearrange("(c p) n -> p c n", p=P)
        w_gu_v = w_gate_up[0].rearrange("e (c p) n -> e p c n", p=P)
        w_dn_v = w_down[0].rearrange("e (b p c) n -> e p b c n", b=2, c=4)

        def unit(n):
            return raw[:, n % RING, :]

        def unit3(n, cols=BLK):
            return unit(n)[:, 0:KC * cols].rearrange("p (c n) -> p c n", c=KC)

        U_UP, U_G, U_BR, U_WO = 4, 5, 9, 11
        up_q = unit(U_UP)[:, 0:2 * HEADS * QK].rearrange("p (c n) -> p c n", c=2)
        up_kv = unit(U_UP)[:, 2 * HEADS * QK:2 * HEADS * QK + HEADS * (NOPE + V_DIM)]
        br_w = [unit(U_BR + i)[:, 0:4 * D].rearrange("p (c n) -> p c n", c=4) for i in range(2)]

        EXTRA = [16 if s in (1, U_UP % RING) else 0 for s in range(RING)]

        def landed_front(eng, n):
            eng.wait_ge(raw_in[n % RING], 16 * (n // RING + 1) + EXTRA[n % RING])

        def slot_of(u):
            return (FRONT_UNITS + u) % RING

        def used_up(eng, n):
            if n < U_UP:
                eng.wait_ge(z_ps, 2 * n + 2)
            elif n == U_UP:
                eng.wait_ge(up_ps, 4)
            elif n < U_BR:
                eng.wait_ge(g_ps, 4 * (n - U_G + 1))
            elif n < U_WO:
                eng.wait_ge(br_ps, KC)
            else:
                eng.wait_ge(wo_ps, 3 + n - U_WO)

        LOADS = [1, 1, 1, 1, 2, 2]

        def landed_expert(eng, i, u):
            before = 16 * len([n for n in range(FRONT_UNITS) if n % RING == slot_of(u)]) + EXTRA[slot_of(u)]
            eng.wait_ge(raw_in[slot_of(u)], 16 * LOADS[u] * i + (before + 16 * LOADS[u]))

        h2T = sgT[:, :, :, :].rearrange("p c a t -> p (c a t)")[:, 0:KC * TOKENS].rearrange("p (c t) -> p c t", c=KC)
        mT = hT

        def stepper(eng, signal):
            n = [0]

            def step(ins):
                n[0] += 1
                ins.then_inc(signal, 1)
                eng.wait_ge(signal, n[0])
            return step

        block = ctx.enter_context(nc.Block())

        @block.sync
        def _(sp):
            sp.dma_start(xs[:, :, :], x[0].rearrange("(t p) d -> p t d", p=P)).then_inc(x_in, 16)

            def load_front(n):
                if n >= RING:
                    used_up(sp, n - RING)
                done = raw_in[n % RING]
                if n < 4 and n != 1:
                    c0, w = Z_UNITS[n][0]
                    sp.dma_start(unit3(n, w), w_in_v[:, :, c0:c0 + w]).then_inc(done, 16)
                elif n == 1:
                    at = 0
                    for c0, w in Z_UNITS[1]:
                        sp.dma_start(unit3(1, 200)[:, :, at:at + w], w_in_v[:, :, c0:c0 + w]).then_inc(done, 16)
                        at += w
                elif n == U_UP:
                    sp.dma_start(up_kv, w_ukv_v).then_inc(done, 16)
                    sp.dma_start(up_q, w_uq_v).then_inc(done, 16)
                elif n < U_BR:
                    c0 = GATES_AT + (n - U_G) * BLK
                    sp.dma_start(unit3(n), w_in_v[:, :, c0:c0 + BLK]).then_inc(done, 16)
                elif n < U_WO:
                    sp.dma_start(br_w[n - U_BR], w_br_v[n - U_BR]).then_inc(done, 16)
                else:
                    c0 = (n - U_WO) * BLK
                    sp.dma_start(unit3(n), w_out_v[:, :, c0:c0 + BLK]).then_inc(done, 16)

            def load_expert(e, u):
                to = raw[:, slot_of(u), :].rearrange("p (c n) -> p c n", c=KC)
                if u < 4:
                    c0 = GU_COLS[u]
                    sp.dma_start(to, w_gu_v[e, :, :, c0:c0 + BLK]).then_inc(raw_in[slot_of(u)], 16)
                else:
                    c0 = (u - 4) * BLK
                    for b in range(2):
                        sp.dma_start(to[:, 4 * b:4 * b + 4, :], w_dn_v[e, :, b, :, c0:c0 + BLK])\
                            .then_inc(raw_in[slot_of(u)], 16)

            for n in range(FRONT_UNITS):
                load_front(n)
            for u in range(UNITS):
                used_up(sp, FRONT_UNITS + u - RING)
                load_expert(0, u)
            sp.wait_ge(n_ok, 1)
            items = sp.value_load(n_items[0:1, 0:1], min_val=EXPERTS, max_val=EXPERTS * CHUNKS)
            with sp.Fori(1, items) as i:
                e = sp.snap(i % EXPERTS)
                for u in range(UNITS):
                    sp.wait_ge(lo_ok, PIECES * i + (2 * u + 2 - PIECES))
                    load_expert(e, u)
            for t in range(TT):
                sp.wait_ge(o_ok, t + 1)
                sp.dma_start(out[0, t * P:(t + 1) * P, :], xs[:, t, :]).then_inc(out_done, 16)
            sp.wait_ge(out_done, 16 * TT)

        @block.tensor
        def _(pe):
            def gemm(o, lhs, rhs, n, start=True):
                for c in range(n):
                    mm = pe.matmul(o, lhs(c), rhs(c), start=start and c == 0, stop=c == n - 1)
                return mm

            pe.wait_ge(cst_in, 16)
            pe.wait_ge(x_in, 16)
            for c in range(KC):
                for t in range(TT):
                    a = (c % 2) * TOKENS + t * P
                    tr = pe.transpose(B[2 + c // 2][:, a:a + P], xs[:, t, c:D:KC], ident)
                tr.then_inc(xT_ps, 1)
            pe.wait_ge(diag_ok, TT)
            for t in range(TT):
                mm = pe.matmul(B[6][:, t * P:(t + 1) * P], const("ones"), diag[:, t, :], start=True, stop=True)
            mm.then_inc(rstd_ps, 1)
            pe.wait_ge(small_in, SMALL)
            for u in range(4):
                for c in range(4):
                    a = GU_COLS[u] + c
                    j = (u * 4 + c) * EXPERTS
                    tr = pe.transpose(B[7][:, j:j + EXPERTS], bgu[:, a:GU_COLS[u] + BLK:4], ident[0:EXPERTS, 0:EXPERTS])
            tr.then_inc(bgu_ps, 1)

            z_n = 0
            pe.wait_ge(hT_ok, KC)

            def z_unit(n):
                nonlocal z_n
                w = sum(c for _, c in Z_UNITS[n])
                landed_front(pe, n)
                for t in range(TT):
                    if z_n >= 2:
                        pe.wait_ge(z_ok, z_n - 1)
                    mm = gemm(ZB[t][:, 0:w], lambda c: hT[:, c, t * P:(t + 1) * P],
                              lambda c: unit3(n, w)[:, c, :], KC)
                    mm.then_inc(z_ps, 1)
                    z_n += 1

            def scores(b, q, k, signal):
                t, heads = BATCHES[b % 6]
                w = P * (t + 1)
                for m, h in enumerate(heads):
                    mm = pe.matmul(SB[b % 2][:, m * w:(m + 1) * w], q(h, t), k(h, w), start=True, stop=True)
                mm.then_inc(signal, 1)

            def pair_q(h, t):
                return qT[HD * (h % 2):HD * (h % 2) + HD, h // 2, t * P:(t + 1) * P]

            def pair_k(h, w):
                return kT[HD * (h % 2):HD * (h % 2) + HD, 0:w]

            def turn_pairs(zq, signal):
                for j in range(4):
                    for t in range(TT):
                        a = (j % 2) * TOKENS + t * P
                        tr = pe.transpose(TB[j // 2][:, a:a + P], zq[:, t, j * P:(j + 1) * P], ident)
                    if j % 2:
                        tr.then_inc(signal, 1)
                for t in range(TT):
                    tr = pe.transpose(VB[0][:, t * P:(t + 1) * P], kk[:, t, :, :].rearrange("p a d -> p (a d)"), ident)
                tr.then_inc(signal, 1)

            g_n = 0

            def gate_block():
                nonlocal g_n
                n = U_G + g_n // 4
                if g_n % 4 == 0:
                    landed_front(pe, n)
                if g_n >= 2:
                    pe.wait_ge(g_ok, g_n - 1)
                a = (g_n % 4) * P
                mm = gemm(ZB[g_n % 2][:, 0:TOKENS], lambda c: unit3(n)[:, c, a:a + P], lambda c: hT[:, c, :], KC)
                mm.then_inc(g_ps, 1)
                g_n += 1

            z_unit(0)
            z_unit(1)
            z_unit(2)
            pe.wait_ge(qi_rot, 1)
            pe.wait_ge(hT_ok, KC + 1)
            turn_pairs(z_qi, qi_ps)
            z_unit(3)
            pe.wait_ge(qi_ok, 3)
            for b in range(6):
                if b >= 2:
                    pe.wait_ge(idx_rl, b - 1)
                scores(b, pair_q, pair_k, idx_ps)

            pe.wait_ge(z_ok, 8)
            for c in range(2):
                for t in range(TT):
                    tr = pe.transpose(TB[0][:, c * TOKENS + t * P:c * TOKENS + (t + 1) * P],
                                      z_ml[:, t, c:Q_LORA:2], ident)
            tr.then_inc(c_ps, 1)
            for t in range(TT):
                tr = pe.transpose(TB[1][:, t * P:(t + 1) * P], z_ml[:, t, Q_LORA:Q_LORA + KV_LORA], ident)
            tr.then_inc(c_ps, 1)
            gate_block()
            gate_block()
            landed_front(pe, U_UP)
            pe.wait_ge(c_ok, 2)
            pe.wait_ge(idx_rl, 6)
            n = 0
            for t in range(TT):
                at = slice(t * P, (t + 1) * P)
                if t:
                    pe.wait_ge(up_a, 2)
                gemm(SB[0][:, 0:BLK], lambda c: c_qT[:, c, at], lambda c: up_q[:, c, 0:BLK], 2)
                gemm(SB[1][:, 0:256], lambda c: c_qT[:, c, at], lambda c: up_q[:, c, BLK:768], 2).then_inc(up_ps, 1)
                if t:
                    pe.wait_ge(up_a, 4)
                    pe.wait_ge(up_d, 2)
                for j in range(2):
                    mm = gemm(VB[j][:, :], lambda c: c_kvT[:, at], lambda c: up_kv[:, j * BLK:(j + 1) * BLK], 1)
                mm.then_inc(up_ps, 1)
            gate_block()
            gate_block()
            pe.wait_ge(ml_rot, 1)
            pe.wait_ge(c_ok, 2)
            n = 0
            for j in range(4):
                for src, out_ok in ((q_ml, mq_ok), (k_ml, mk_ok)):
                    if j:
                        pe.wait_ge(out_ok, j)
                    for h in (2 * j, 2 * j + 1):
                        for t in range(TT):
                            a = (h % 2) * TOKENS + t * P
                            tr = pe.transpose(TB[n % 2][0:QK, a:a + P], src[:, t, h, :], ident)
                    tr.then_inc(mT_ps, 1)
                    n += 1
            pe.wait_ge(mq_ok, 4)
            pe.wait_ge(mk_ok, 4)

            def attend(first, q, k, v):
                for b in range(first, first + 6):
                    if b >= 2:
                        pe.wait_ge(s_mx, b - 1)
                    scores(b, q, k, s_ps)
                    gate_block()
                    t, heads = BATCHES[b % 6]
                    pe.wait_ge(p_ok, b + 1)
                    if b >= 2:
                        pe.wait_ge(pT_ok, b - 1)
                    for m in range(4):
                        tr = pe.transpose(TB[b % 2][:, m * P:(m + 1) * P], prob[:, b % 2, m * P:(m + 1) * P], ident)
                    tr.then_inc(pT_ps, 1)
                    pe.wait_ge(pT_ok, b + 1)
                    if b == first and first:
                        pe.wait_ge(pv_ok, 2)
                    if b % 6 == 0:
                        pe.wait_ge(up_d, 4)
                        pe.wait_ge(up_a, 8)
                    for m in range(4):
                        h = heads[m // (t + 1)]
                        kt = m % (t + 1)
                        half = V_DIM * (h % 2)
                        mm = pe.matmul(VB[t][half:half + V_DIM, (h // 2) * P:(h // 2 + 1) * P], v(h, kt),
                                       probT[:, b % 2, m * P:(m + 1) * P], start=kt == 0, stop=kt == t)
                    mm.then_inc(pv_ps, 1)

            attend(0, lambda h, t: qmT[:, h, t * P:(t + 1) * P], lambda h, w: kmT[:, h, 0:w],
                   lambda h, kt: v_ml[:, kt, h, :])
            pe.wait_ge(qb_rot, 1)
            pe.wait_ge(pT_ok, 6)
            pe.wait_ge(pv_ok, 2)
            turn_pairs(z_qb, qd_ps)
            pe.wait_ge(qd_ok, 3)
            attend(6, pair_q, pair_k, lambda h, kt: z_kv[:, kt, HD:2 * HD])

            landed_front(pe, U_BR)
            landed_front(pe, U_BR + 1)
            pe.wait_ge(pv_ok, 4)
            pe.wait_ge(s_mx, 12)
            for mc in range(KC):
                if mc >= 2:
                    pe.wait_ge(br_ok, 2 * (mc - 1) - 1)
                for i, o in enumerate((mlaT, dsaT)):
                    mm = gemm(SB[mc % 2][:, i * TOKENS:(i + 1) * TOKENS],
                              lambda c: br_w[i][:, c, mc * P:(mc + 1) * P], lambda c: o[:, c, :], 4)
                mm.then_inc(br_ps, 1)
            landed_front(pe, U_WO)
            landed_front(pe, U_WO + 1)
            pe.wait_ge(g_ok, 16)
            pe.wait_ge(pT_ok, 12)
            for t in range(TT):
                for n in range(2):
                    for c in range(KC):
                        if t == 0 and n == 0:
                            pe.wait_ge(br_ok, 2 * (c + 1))
                        mm = pe.matmul(B[2 * t + n][:, :], mT[:, c, t * P:(t + 1) * P], unit3(U_WO + n)[:, c, :],
                                       start=c == 0, stop=c == KC - 1)
                    mm.then_inc(wo_ps, 1)
            for t in range(TT):
                pe.wait_ge(h2_ok, t + 1)
                for c in range(KC):
                    tr = pe.transpose(B[4 + 2 * t + c // 4][:, (c % 4) * P:(c % 4 + 1) * P], h2[:, t, c:D:KC], ident)
                    if c % 4 == 3:
                        tr.then_inc(h2T_ps, 1)
            for t in range(TT):
                pe.wait_ge(h2T_ok, 2 * t + 2)
                gemm(B[0][:, t * EXPERTS:(t + 1) * EXPERTS], lambda c: h2T[:, c, t * P:(t + 1) * P],
                     lambda c: rw[:, c, :], KC).then_inc(lg_ps, 1)
            pe.wait_ge(sel_ok, 1)
            ones, before = const("ones"), const("before")
            pe.matmul(B[7][:, 0:32], before, sel[:, 0, :], start=True, stop=True)
            pe.matmul(B[7][:, 32:64], ones, sel[:, 0, :], start=True, stop=False)
            pe.matmul(B[7][:, 32:64], before, sel[:, 1, :], start=False, stop=True)
            pe.matmul(B[7][:, 64:96], ones, sel[:, 0, :], start=True, stop=False)
            pe.matmul(B[7][:, 64:96], ones, sel[:, 1, :], start=False, stop=True).then_inc(pos_ps, 1)
            pe.wait_ge(gate_ok, 1)
            for t in range(TT):
                tr = pe.transpose(B[2][0:EXPERTS, t * P:(t + 1) * P], gate[:, t, :], ident)
            tr.then_inc(gT_ps, 1)
            pe.wait_ge(gT_ok, 1)
            pe.wait_ge(bd_in, 16)
            for t in range(TT):
                for n in range(2):
                    mm = pe.matmul(ACC[2 * t + n][:, :], gateT[:, t * P:(t + 1) * P], bd[:, n * BLK:(n + 1) * BLK],
                                   start=True, stop=True)
                if t == 0:
                    mm.then_inc(ev_used, 2)
            mm.then_inc(used, SPLITS)

            def gather():
                for c in range(KC):
                    for t in range(TT):
                        mm = pe.matmul(PREP[:, c * SLOTS:(c + 1) * SLOTS], h2[:, t, c * P:(c + 1) * P],
                                       onehot[:, t, :], start=t == 0, stop=t == TT - 1)
                mm.then_inc(gath_ps, 1)

            pe.wait_ge(prep_ok, 1)
            gather()
            pe.wait_ge(n_ok, 1)
            items = pe.value_load(n_items[0:1, 0:1], min_val=EXPERTS, max_val=EXPERTS * CHUNKS)
            with pe.Fori(0, items) as i:
                def piece(p):
                    u = p // 2
                    if p % 2 == 0:
                        pe.wait_ge(ev_ok, UNITS * i + (u + 1))
                    x_of = xe if u < 4 else ae
                    pe.wait_ge(hi_ok, PIECES * i + (p + 1))
                    for c in range(4):
                        pe.matmul(MM[u % 2][:, :], x_of[:, 4 * (p % 2) + c, :, :].rearrange("p a s -> p (a s)"),
                                  hi[:, p % SPLITS, c, :], start=p % 2 == 0 and c == 0, stop=False)
                    pe.wait_ge(lo_ok, PIECES * i + (p + 1))
                    for c in range(4):
                        mm = pe.matmul(MM[u % 2][:, :], x_of[:, 4 * (p % 2) + c, :, :].rearrange("p a s -> p (a s)"),
                                       lo[:, p % SPLITS, c, :], start=False, stop=p % 2 == 1 and c == 3)
                    mm.then_inc(used, 1)

                def turn(u):
                    pe.wait_ge(ev_ok, UNITS * i + (2 + u + 1))
                    if u % 2 == 0:
                        pe.wait_ge(gub_ok, 2 * i + (u // 2 + 1))
                    for c in range(4):
                        a = ((u % 2) * 4 + c) * SLOTS
                        mm = pe.matmul(GUT[:, a:a + SLOTS], ev[:, u % 2, c:BLK:4], const("ident2"),
                                       start=True, stop=True)
                    mm.then_inc(ev_used, 1)

                def scatter(n):
                    pe.wait_ge(ev_ok, UNITS * i + (2 + 4 + n + 1))
                    for t in range(TT):
                        mm = pe.matmul(ACC[2 * t + n][:, :], scat[:, t * P:(t + 1) * P], ev[:, n, :],
                                       start=False, stop=True, skip_group_check=True)
                    mm.then_inc(ev_used, 1)

                pe.wait_ge(xl_ok, i + 1)
                piece(0)
                piece(1)
                for t in range(TT):
                    tr = pe.transpose(PREP[:, t * P:(t + 1) * P], gated[:, t, :], ident)
                tr.then_inc(sc_ps, 1)
                piece(2)
                turn(0)
                piece(3)
                piece(4)
                turn(1)
                piece(5)
                piece(6)
                turn(2)
                piece(7)
                turn(3)
                pe.wait_ge(al_ok, 2 * i + 1)
                piece(8)
                pe.wait_ge(al_ok, 2 * i + 2)
                piece(9)
                piece(10)
                pe.wait_ge(sc_ok, i + 1)
                scatter(0)
                piece(11)
                pe.wait_ge(prep_ok, i + 2)
                gather()
                scatter(1)

        @block.scalar
        def _(act):
            step = stepper(act, act_step)
            act.dma_start(cst[:, :], consts).then_inc(cst_in, 16)
            for t in range(TT):
                act.dma_start(pos_i[:, t:t + 1], positions[0, t * P:(t + 1) * P].rearrange("(p a) -> p a", a=1))\
                    .then_inc(small_in, 16)
            act.dma_start(g_in[:, :], attn_norm_g[0].rearrange("(p c) -> p c", c=KC)).then_inc(small_in, 16)
            act.dma_start(g_q[:, :], mla_q_norm_g[0].rearrange("(p c) -> p c", c=2)).then_inc(small_in, 16)
            act.dma_start(g_kv[:, :], mla_kv_norm_g[0].rearrange("(p c) -> p c", c=1)).then_inc(small_in, 16)
            act.dma_start(rw[:, :, :], router_w[0].rearrange("(p c) n -> p c n", c=KC)).then_inc(small_in, 16)
            act.dma_start(rb[:, :], router_b[0].partition_broadcast(P)).then_inc(small_in, 16)
            act.dma_start(bgu, b_gate_up[0]).then_inc(small_in, 16)
            act.dma_start(gain[:, 0:BLK], ffn_norm_g[0, 0:BLK].partition_broadcast(P)).then_inc(small_in, 16)
            act.dma_start(gain[:, BLK:D], ffn_norm_g[0, BLK:D].partition_broadcast(P)).then_inc(small_in, 16)

            act.wait_ge(x_in, 16)
            for t in range(TT):
                step(act.activation(sgT[:, 0:2, :, :].rearrange("p c a t -> p (c a t)"),
                                    xs[:, t, :], ACT.Square, accum_out=stat[:, t:t + 1]))
            act.copy(stat[:, 6:7], stat[:, 1:2]).then_inc(x_sq, 1)
            act.wait_ge(x_ms, 1)
            act.activation(stat[:, 4:6], stat[:, 2:4], ACT.Sqrt).then_inc(x_rt, 1)
            act.wait_ge(ang_ok, 1)
            act.activation(trig[:, :, :, :], ang[:, :, :, :], ACT.Sin).then_inc(trig_ok, 1)

            z_out = [lambda t: z_qi[:, t, :], lambda t: z_kv[:, t, :], lambda t: z_qb[:, t, :], lambda t: z_ml[:, t, :]]

            def z_evac(n):
                w = sum(c for _, c in Z_UNITS[n])
                for t in range(TT):
                    act.wait_ge(z_ps, 2 * n + t + 1)
                    act.copy(z_out[n](t), ZB[t][:, 0:w]).then_inc(z_ok, 1)

            z_evac(0)
            z_evac(1)
            z_evac(2)
            for j in range(2):
                act.wait_ge(qi_ps, j + 1)
                act.copy(qT[:, 2 * j:2 * j + 2, :].rearrange("p j t -> p (j t)"), TB[j][:, :]).then_inc(qi_ok, 1)
            act.wait_ge(qi_ps, 3)
            act.copy(kT[:, :], VB[0][:, 0:TOKENS]).then_inc(qi_ok, 1)
            z_evac(3)
            for b in range(6):
                act.wait_ge(idx_ps, b + 1)
                if b >= 2:
                    act.wait_ge(idx_ac, b - 1)
                act.activation(prob[:, b % 2, :], SB[b % 2][:, :], ACT.Relu, scale=HD ** -0.5).then_inc(idx_rl, 1)
            for t in range(TT):
                step(act.activation(probT[:, 0, 0:Q_LORA], z_ml[:, t, 0:Q_LORA],
                                    ACT.Square, accum_out=stat[:, 7 + t:8 + t]))
                step(act.activation(probT[:, 0, 0:KV_LORA], z_ml[:, t, Q_LORA:Q_LORA + KV_LORA],
                                    ACT.Square, accum_out=stat[:, 9 + t:10 + t]))
            act.copy(stat[:, 6:7], stat[:, 10:11]).then_inc(c_sq, 1)
            act.wait_ge(c_ms, 1)
            act.activation(stat[:, 7:11], stat[:, 7:11], ACT.Sqrt).then_inc(c_rt, 1)

            g_n = 0

            def gate_evac():
                nonlocal g_n
                act.wait_ge(g_ps, g_n + 1)
                act.copy(sgT[:, g_n % KC, g_n // KC, :], ZB[g_n % 2][:, 0:TOKENS]).then_inc(g_ok, 1)
                g_n += 1

            gate_evac()
            gate_evac()
            act.wait_ge(c_rs, 1)
            act.wait_ge(idx_ac, 6)
            for t in range(TT):
                act.wait_ge(up_ps, 2 * t + 1)
                q_flat = q_ml[:, t, :, :].rearrange("p h d -> p (h d)")
                act.activation(q_flat[:, 0:BLK], SB[0][:, :], ACT.Copy, scale=stat[:, 11 + t:12 + t]).then_inc(up_a, 1)
                act.activation(q_flat[:, BLK:768], SB[1][:, 0:256], ACT.Copy, scale=stat[:, 11 + t:12 + t]).then_inc(up_a, 1)
                act.wait_ge(up_ps, 2 * t + 2)
                for j in range(2):
                    src = VB[j][:, :].rearrange("p (h d) -> p h d", h=4)
                    act.activation(k_ml[:, t, 4 * j:4 * j + 4, 0:NOPE], src[:, :, 0:NOPE], ACT.Copy,
                                   scale=stat[:, 13 + t:14 + t]).then_inc(up_a, 1)
            gate_evac()
            gate_evac()
            for j in range(4):
                act.wait_ge(mT_ps, 2 * j + 1)
                act.copy(qmT[:, 2 * j:2 * j + 2, :].rearrange("p h t -> p (h t)"), TB[0][0:QK, :]).then_inc(mq_ok, 1)

            def attend(first):
                for b in range(first, first + 6):
                    t, heads = BATCHES[b % 6]
                    w = P * (t + 1)
                    act.wait_ge(s_mx, b + 1)
                    for m in range(len(heads)):
                        ex = act.activation(prob[:, b % 2, m * w:(m + 1) * w], prob[:, b % 2, m * w:(m + 1) * w], ACT.Exp,
                                            bias=mx[:, b % 2, m:m + 1], accum_out=den[:, b % 2, m:m + 1])
                    ex.then_inc(p_ex, 1)
                    gate_evac()
                    act.wait_ge(pT_ps, b + 1)
                    act.copy(probT[:, b % 2, :], TB[b % 2][:, :]).then_inc(pT_ok, 1)
                    if b % 6 in (1, 5):
                        act.wait_ge(pv_ps, b + 1)
                        to = mlaT if first == 0 else dsaT
                        act.copy(to[:, :, t * P:(t + 1) * P], VB[t][:, :].rearrange("p (j q) -> p j q", j=4)).then_inc(pv_ok, 1)

            attend(0)
            for j in range(2):
                act.wait_ge(qd_ps, j + 1)
                act.copy(qT[:, 2 * j:2 * j + 2, :].rearrange("p j t -> p (j t)"), TB[j][:, :]).then_inc(qd_ok, 1)
            act.wait_ge(qd_ps, 3)
            act.copy(kT[:, :], VB[0][:, 0:TOKENS]).then_inc(qd_ok, 1)
            attend(6)
            act.wait_ge(g_ok, 16)
            for mc in range(0, KC, 2):
                act.activation(sgT[:, mc:mc + 2, :, :], sgT[:, mc:mc + 2, :, :], ACT.Sigmoid).then_inc(sig_ok, 1)
            act.wait_ge(br_ps, KC)
            act.dma_start(bd, b_down[0]).then_inc(bd_in, 16)
            for t in range(TT):
                act.wait_ge(x1_ok, 2 * t + 2)
                step(act.activation(h2[:, t, :], xs[:, t, :], ACT.Square, accum_out=stat[:, t:t + 1]))
                act.copy(stat[:, 6:7], stat[:, t:t + 1]).then_inc(f_sq, 1)
                act.wait_ge(f_ms, t + 1)
                act.activation(stat[:, 4 + t:5 + t], stat[:, 2 + t:3 + t], ACT.Sqrt).then_inc(f_rt, 1)
            act.wait_ge(h2_ok, TT)
            for j in range(2):
                act.dma_start(gain[:, j * BLK:(j + 1) * BLK],
                              final_norm_g[j * BLK:(j + 1) * BLK].partition_broadcast(P)).then_inc(gain_in, 16)
            for j in range(4):
                act.wait_ge(h2T_ps, j + 1)
                t, a = j // 2, (j % 2) * 4
                act.copy(h2T[:, a:a + 4, t * P:(t + 1) * P], B[4 + j][:, :].rearrange("p (c t) -> p c t", c=4)).then_inc(h2T_ok, 1)
            act.wait_ge(lg_mx, 1)
            for t in range(TT):
                ex = act.activation(r_b[:, t, :], lg[:, t, :], ACT.Exp, bias=r_s[:, t, 0:1])
            ex.then_inc(lg_ex, 1)
            act.wait_ge(gT_ps, 1)
            act.copy(gateT, B[2][0:EXPERTS, 0:TOKENS]).then_inc(gT_ok, 1)
            act.wait_ge(used, SPLITS)

            def split_x(n):
                act.wait_ge(gath_ps, n)
                act.copy(xe[:, :, 0, :], PREP[:, :].rearrange("p (c s) -> p c s", c=KC)).then_inc(xh_ok, 1)

            step(act.copy(ev[:, 0, 0:1], stat[:, 0:1]))
            act.copy(ev[:, 0, 1:2], stat[:, 0:1]).then_inc(ev_ok, 2)
            split_x(1)
            act.wait_ge(n_ok, 1)
            items = act.value_load(n_items[0:1, 0:1], min_val=EXPERTS, max_val=EXPERTS * CHUNKS)
            with act.Fori(0, items) as i:
                def high(p):
                    u = p // 2
                    if p % 2 == 0:
                        landed_expert(act, i, u)
                    act.wait_ge(used, PIECES * i + (p + 1))
                    a = (p % 2) * 4 * BLK
                    act.copy(hi[:, p % SPLITS, :, :].rearrange("p c n -> p (c n)"),
                             raw[:, slot_of(u), a:a + 4 * BLK]).then_inc(hi_ok, 1)

                def evac(u):
                    act.wait_ge(used, PIECES * i + (SPLITS + 2 * u + 2))
                    act.wait_ge(ev_used, UNITS * i + (u + 1))
                    act.copy(ev[:, u % 2, :], MM[u % 2][:, :]).then_inc(ev_ok, 1)

                def sigmoid(half):
                    act.wait_ge(glu_ok, 2 * i + (half + 1))
                    act.activation(sig[:, :, :], glu[:, :, :], ACT.Sigmoid, scale=ALPHA).then_inc(sig2_ok, 1)

                def high_act(half):
                    act.wait_ge(actv_ok, 2 * i + (half + 1))
                    act.copy(ae[:, 4 * half:4 * half + 4, 0, :], actv[:, :, :]).then_inc(ah_ok, 1)

                high(0)
                high(1)
                high(2)
                evac(0)
                act.wait_ge(sc_ps, i + 1)
                act.copy(scat[:, :], PREP[:, 0:TOKENS]).then_inc(sc_ok, 1)
                high(3)
                high(4)
                evac(1)
                high(5)
                high(6)
                sigmoid(0)
                evac(2)
                high(7)
                high_act(0)
                high(8)
                evac(3)
                sigmoid(1)
                high(9)
                high_act(1)
                high(10)
                evac(4)
                high(11)
                evac(5)
                split_x(i + 2)
            for t in range(TT):
                act.wait_ge(y_ok, 2 * t + 2)
                act.activation(h2[:, t, :], xs[:, t, :], ACT.Square, accum_out=stat[:, t:t + 1]).then_inc(y_sq, 1)
                act.wait_ge(y_ms, t + 1)
                act.activation(stat[:, 4 + t:5 + t], stat[:, 2 + t:3 + t], ACT.Sqrt).then_inc(y_rt, 1)

        @block.vector
        def _(dve):
            step = stepper(dve, dve_step)

            def rotate(view, heads, half, every, temps, step, eng):
                ta, tb = (x[:, :, 0:heads, 0:2 * half] for x in temps)
                shape = [P, TT, heads, half]
                cos = trig[:, 0, :, 0:16:every].unsqueeze(2).to_broadcast(shape)
                sin = trig[:, 1, :, 0:16:every].unsqueeze(2).to_broadcast(shape)
                neg = nsin[:, :, 0:16:every].unsqueeze(2).to_broadcast(shape)
                x1, x2 = view[:, :, :, 0:half], view[:, :, :, half:2 * half]
                eng.tensor_tensor(ta[:, :, :, 0:half], x1, cos, ALU.mult)
                eng.tensor_tensor(ta[:, :, :, half:2 * half], x2, cos, ALU.mult)
                eng.tensor_tensor(tb[:, :, :, 0:half], x2, neg, ALU.mult)
                step(eng.tensor_tensor(tb[:, :, :, half:2 * half], x1, sin, ALU.mult))
                return eng.tensor_tensor(view, ta, tb, ALU.add)

            dve.wait_ge(small_in, SMALL)
            dve.wait_ge(cst_in, 16)
            step(dve.tensor_copy(pos_f[:, :], pos_i[:, :]))
            for t in range(TT):
                dve.tensor_scalar(ang[:, 1, t, :], const("invfreq"), pos_f[:, t:t + 1], None, ALU.mult)
                last = dve.tensor_scalar(ang[:, 0, t, :], const("invfreq"), pos_f[:, t:t + 1], None, ALU.mult)
            step(last)
            magic = float(1.5 * 2 ** 23)
            dve.tensor_scalar(turns[:, 1], ang[:, 1], 1.0 / (2 * np.pi), None, ALU.mult)
            step(dve.tensor_scalar(turns[:, 0], ang[:, 0], 1.0 / (2 * np.pi), 0.25, ALU.mult, ALU.add))
            step(dve.tensor_scalar(turns[:], turns[:], magic, None, ALU.add))
            step(dve.tensor_scalar(turns[:], turns[:], magic, None, ALU.subtract))
            rest = 2 * np.pi
            for _ in range(3):
                part = float((np.float32(rest).view(np.uint32) & np.uint32(0xFFFFF000)).view(np.float32))
                rest -= part
                step(dve.scalar_tensor_tensor(out=ang[:], in0=turns[:], scalar=-part, in1=ang[:], op0=ALU.mult, op1=ALU.add))
            step(dve.tensor_scalar(ang[:, 0], ang[:, 0], float(np.pi / 2), None, ALU.add))
            dve.tensor_scalar(ang[:], ang[:], 3.1415925, -3.1415925, ALU.min, ALU.max).then_inc(ang_ok, 1)

            dve.wait_ge(x_sq, 1)
            dve.tensor_scalar(stat[:, 2:4], stat[:, 0:2], 1.0 / D, EPS, ALU.mult, ALU.add).then_inc(x_ms, 1)
            dve.wait_ge(x_rt, 1)
            step(dve.reciprocal(stat[:, 0:2], stat[:, 4:6]))
            for t in range(TT):
                dve.tensor_scalar(diag[:, t, :], ident, stat[:, t:t + 1], None, ALU.mult).then_inc(diag_ok, 1)
            dve.wait_ge(rstd_ps, 1)
            step(dve.tensor_copy(rstd_row[:, :], B[6][:, 0:TOKENS]))
            for c in range(KC):
                dve.wait_ge(xT_ps, c + 1)
                a = (c % 2) * TOKENS
                dve.scalar_tensor_tensor(out=hT[:, c, :], in0=B[2 + c // 2][:, a:a + TOKENS], scalar=g_in[:, c:c + 1],
                                         in1=rstd_row[:, :], op0=ALU.mult, op1=ALU.mult).then_inc(hT_ok, 1)
            dve.wait_ge(bgu_ps, 1)
            dve.tensor_copy(bias_gu[:, :, :], B[7][:, :].rearrange("p (j e) -> p e j", e=EXPERTS)).then_inc(hT_ok, 1)
            dve.wait_ge(trig_ok, 1)
            dve.tensor_scalar(nsin[:, :, :], trig[:, 1], -1.0, None, ALU.mult).then_inc(nsin_ok, 1)
            dve.wait_ge(nsin_ok, 1)
            dve.wait_ge(z_ok, 2)
            step(rotate(z_qi[:, :, :].rearrange("p t (h d) -> p t h d", h=HEADS)[:, :, :, 0:ROT], HEADS, ROT // 2, 2, (ropa, ropb), step, dve))
            dve.wait_ge(z_ok, 4)
            step(rotate(z_kv[:, :, 2 * HD:3 * HD].unsqueeze(2)[:, :, :, 0:ROT], 1, ROT // 2, 2, (ropa, ropb), step, dve))
            step(dve.tensor_scalar(w_idx[:, :, :], z_kv[:, :, 3 * HD:3 * HD + HEADS], HEADS ** -0.5, None, ALU.mult))
            dve.tensor_copy(kk[:, :, :, :], z_kv[:, :, 2 * HD:3 * HD].unsqueeze(2).to_broadcast([P, TT, 2, HD])).then_inc(qi_rot, 1)
            for b in range(6):
                t, heads = BATCHES[b]
                w = P * (t + 1)
                dve.wait_ge(idx_rl, b + 1)
                for m, h in enumerate(heads):
                    src = prob[:, b % 2, m * w:(m + 1) * w]
                    if h == 0:
                        ins = dve.tensor_scalar(score[:, t, 0:w], src, w_idx[:, t, h:h + 1], None, ALU.mult)
                    else:
                        ins = dve.scalar_tensor_tensor(out=score[:, t, 0:w], in0=src, scalar=w_idx[:, t, h:h + 1],
                                                       in1=score[:, t, 0:w], op0=ALU.mult, op1=ALU.add)
                    if m < len(heads) - 1:
                        step(ins)
                ins.then_inc(idx_ac, 1)
                dve.wait_ge(idx_ac, b + 1)
            for t in range(TT):
                last = dve.tensor_tensor(score[:, t, t * P:(t + 1) * P], score[:, t, t * P:(t + 1) * P], const("causal"), ALU.add)
            step(last)

            def topk():
                for t in range(TT):
                    w = P * (t + 1)
                    sc, wk = score[:, t, 0:w], work[:, t, 0:w]
                    for r in range(TOPK // 8):
                        step(dve.max(top8[:, t, :], sc if r == 0 else wk))
                        if r < TOPK // 8 - 1:
                            step(dve.match_replace(wk, top8[:, t, :], sc if r == 0 else wk, REMOVED))
                        if r % 3 == 2:
                            yield
                    over, same, count = (pick[:, j, 0:w] for j in range(3))
                    thr = top8[:, t, 7:8]
                    dve.tensor_scalar(over, sc, thr, 0.0, ALU.is_gt, ALU.add, accum_out=cnt[:, t:t + 1])
                    step(dve.tensor_scalar(same, sc, thr, None, ALU.is_equal))
                    dve.tensor_tensor_scan(count, same, same, 0.0, ALU.add, ALU.max)
                    step(dve.tensor_scalar(cnt[:, t:t + 1], cnt[:, t:t + 1], -1.0, float(TOPK), ALU.mult, ALU.add))
                    step(dve.scalar_tensor_tensor(out=same, in0=count, scalar=cnt[:, t:t + 1], in1=same, op0=ALU.is_le, op1=ALU.mult))
                    step(dve.tensor_tensor(over, over, same, ALU.add))
                    step(dve.tensor_scalar(allow[:, t, 0:w], over, -1.0, -NEG, ALU.add, ALU.mult))
                    step(dve.tensor_tensor(allow[:, t, t * P:(t + 1) * P], allow[:, t, t * P:(t + 1) * P], const("causal"), ALU.add))
                    yield

            dve.wait_ge(c_sq, 1)
            step(dve.tensor_scalar(stat[:, 7:9], stat[:, 7:9], 1.0 / Q_LORA, EPS, ALU.mult, ALU.add))
            dve.tensor_scalar(stat[:, 9:11], stat[:, 9:11], 1.0 / KV_LORA, EPS, ALU.mult, ALU.add).then_inc(c_ms, 1)
            for c in range(2):
                dve.wait_ge(c_ps, 1)
                last = dve.tensor_scalar(c_qT[:, c, :], TB[0][:, c * TOKENS:(c + 1) * TOKENS], g_q[:, c:c + 1], None, ALU.mult)
            last.then_inc(c_ok, 1)
            dve.wait_ge(c_ps, 2)
            dve.tensor_scalar(c_kvT[:, :], TB[1][:, 0:TOKENS], g_kv[:, 0:1], None, ALU.mult).then_inc(c_ok, 1)
            dve.wait_ge(c_rt, 1)
            dve.reciprocal(stat[:, 11:15], stat[:, 7:11]).then_inc(c_rs, 1)
            dve.wait_ge(c_rs, 1)
            for t in range(TT):
                dve.wait_ge(up_ps, 2 * t + 2)
                dve.wait_ge(up_a, 4 * t + 4)
                for j in range(2):
                    src = VB[j][:, :].rearrange("p (h d) -> p h d", h=4)
                    dve.tensor_scalar(v_ml[:, t, 4 * j:4 * j + 4, :], src[:, :, NOPE:NOPE + V_DIM],
                                      stat[:, 13 + t:14 + t], None, ALU.mult).then_inc(up_d, 1)
            for j in range(4):
                dve.wait_ge(mT_ps, 2 * j + 2)
                dve.tensor_copy(kmT[:, 2 * j:2 * j + 2, :].rearrange("p h t -> p (h t)"), TB[1][0:QK, :]).then_inc(mk_ok, 1)

            parts = topk()

            def attend(first, scale):
                for b in range(first, first + 6):
                    t, heads = BATCHES[b % 6]
                    w, n = P * (t + 1), len(heads)
                    src = SB[b % 2][:, :].rearrange("p (h k) -> p h k", h=n)
                    pr = prob[:, b % 2, :].rearrange("p (h k) -> p h k", h=n)
                    dve.wait_ge(s_ps, b + 1)
                    if b >= 2:
                        dve.wait_ge(pT_ps, b - 1)
                    if first:
                        mask = allow[:, t, 0:w].unsqueeze(1).to_broadcast([P, n, w])
                        step(dve.scalar_tensor_tensor(out=pr, in0=src, scalar=scale, in1=mask, op0=ALU.mult, op1=ALU.add))
                    else:
                        if t:
                            dve.tensor_scalar(pr[:, :, 0:P], src[:, :, 0:P], scale, None, ALU.mult)
                        mask = const("causal").unsqueeze(1).to_broadcast([P, n, P])
                        step(dve.scalar_tensor_tensor(out=pr[:, :, t * P:w], in0=src[:, :, t * P:w], scalar=scale, in1=mask,
                                                      op0=ALU.mult, op1=ALU.add))
                    step(dve.tensor_reduce(mx[:, b % 2, 0:n], pr, AXX, ALU.max))
                    dve.tensor_scalar(mx[:, b % 2, 0:n], mx[:, b % 2, 0:n], -1.0, None, ALU.mult).then_inc(s_mx, 1)
                    if not first:
                        next(parts, None)
                    dve.wait_ge(p_ex, b + 1)
                    step(dve.reciprocal(den[:, b % 2, 0:n], den[:, b % 2, 0:n]))
                    dve.tensor_tensor(pr, pr, den[:, b % 2, 0:n].unsqueeze(2).to_broadcast([P, n, w]), ALU.mult).then_inc(p_ok, 1)

            attend(0, QK ** -0.5)
            for _ in parts:
                pass
            attend(6, HD ** -0.5)
            for mc in range(KC):
                dve.wait_ge(br_ps, mc + 1)
                dve.wait_ge(sig_ok, mc // 2 + 1)
                sg = sgT[:, mc, :, :].rearrange("p a t -> p (a t)")
                dve.tensor_tensor(sg, sg, SB[mc % 2][:, :], ALU.mult).then_inc(br_ok, 1)
                dve.wait_ge(br_ok, 2 * mc + 1)
                dve.tensor_tensor(mT[:, mc, :], sg[:, 0:TOKENS], sg[:, TOKENS:2 * TOKENS], ALU.add).then_inc(br_ok, 1)
            for t in range(TT):
                for n in range(2):
                    dve.wait_ge(wo_ps, 2 * t + n + 1)
                    at = slice(n * BLK, (n + 1) * BLK)
                    dve.tensor_tensor(xs[:, t, at], xs[:, t, at], B[2 * t + n][:, :], ALU.add).then_inc(x1_ok, 1)
                dve.wait_ge(f_sq, t + 1)
                dve.tensor_scalar(stat[:, 2 + t:3 + t], stat[:, t:t + 1], 1.0 / D, EPS, ALU.mult, ALU.add).then_inc(f_ms, 1)
                dve.wait_ge(f_rt, t + 1)
                step(dve.reciprocal(stat[:, t:t + 1], stat[:, 4 + t:5 + t]))
                dve.scalar_tensor_tensor(out=h2[:, t, :], in0=xs[:, t, :], scalar=stat[:, t:t + 1], in1=gain[:, :],
                                         op0=ALU.mult, op1=ALU.mult).then_inc(h2_ok, 1)
            dve.wait_ge(lg_ps, TT)
            for t in range(TT):
                step(dve.tensor_tensor(lg[:, t, :], B[0][:, t * EXPERTS:(t + 1) * EXPERTS], rb[:, :], ALU.add))
                step(dve.max(top8[:, t, :], lg[:, t, :]))
            for t in range(TT):
                last = dve.tensor_scalar(r_s[:, t, 0:1], top8[:, t, 0:1], -1.0, None, ALU.mult)
            last.then_inc(lg_mx, 1)
            for t in range(TT):
                thr = top8[:, t, EXP_K - 1:EXP_K]
                dve.tensor_scalar(sel[:, t, :], lg[:, t, :], thr, 0.0, ALU.is_gt, ALU.add, accum_out=r_s[:, t, 1:2])
                step(dve.tensor_scalar(r_a[:, t, :], lg[:, t, :], thr, None, ALU.is_equal))
                dve.tensor_tensor_scan(pm[:, t, :], r_a[:, t, :], r_a[:, t, :], 0.0, ALU.add, ALU.max)
                step(dve.tensor_scalar(r_s[:, t, 1:2], r_s[:, t, 1:2], -1.0, float(EXP_K), ALU.mult, ALU.add))
                step(dve.scalar_tensor_tensor(out=r_a[:, t, :], in0=pm[:, t, :], scalar=r_s[:, t, 1:2], in1=r_a[:, t, :],
                                              op0=ALU.is_le, op1=ALU.mult))
            dve.tensor_tensor(sel[:, :, :], sel[:, :, :], r_a[:, :, :], ALU.add).then_inc(sel_ok, 1)
            dve.wait_ge(sel_ok, 1)
            dve.wait_ge(lg_ex, 1)
            step(dve.tensor_tensor(r_b[:, :, :], r_b[:, :, :], sel[:, :, :], ALU.mult))
            step(dve.tensor_reduce(r_s[:, :, 2:3], r_b[:, :, :], AXX, ALU.add))
            step(dve.reciprocal(r_s[:, :, 3:4], r_s[:, :, 2:3]))
            dve.tensor_tensor(gate[:, :, :], r_b[:, :, :], r_s[:, :, 3:4].to_broadcast([P, TT, EXPERTS]), ALU.mult).then_inc(gate_ok, 1)
            dve.wait_ge(gate_ok, 1)
            dve.tensor_copy(gates[:, :, :].rearrange("p t (c e) -> p t c e", e=EXPERTS),
                            gate[:, :, :].unsqueeze(2).to_broadcast([P, TT, CHUNKS + 1, EXPERTS]))
            dve.wait_ge(pos_ps, 1)
            step(dve.scalar_tensor_tensor(out=pm[:, :, :], in0=B[7][:, 0:64].rearrange("p (t e) -> p t e", t=TT), scalar=1.0,
                                          in1=sel[:, :, :], op0=ALU.add, op1=ALU.mult))
            for c in range(CHUNKS + 1):
                last = dve.tensor_scalar(posc[:, :, c * EXPERTS:(c + 1) * EXPERTS], pm[:, :, :], -1.0 - SLOTS * c, None, ALU.add)
            step(last)
            step(dve.tensor_reduce(r_s[:, 0, 0:1], B[7][:, 64:96], AXX, ALU.max))
            for c in range(1, CHUNKS):
                last = dve.tensor_scalar(r_s[:, 0, c:c + 1], r_s[:, 0, 0:1], float(SLOTS * c), float(EXPERTS), ALU.is_gt, ALU.mult)
            step(last)
            step(dve.tensor_reduce(r_s[:, 0, 0:1], r_s[:, 0, 1:4], AXX, ALU.add))
            dve.tensor_scalar(n_items[:, :], r_s[:, 0, 0:1], float(EXPERTS), None, ALU.add).then_inc(n_ok, 1)

            def prepare(i):
                for t in range(TT):
                    dve.tensor_scalar(onehot[:, t, :], const("slot")[:, 0:SLOTS], posc[:, t, bass.ds(i, 1)], None, ALU.is_equal)
                    last = dve.tensor_scalar(gated[:, t, :], const("slot"), posc[:, t, bass.ds(i, 1)],
                                             gates[:, t, bass.ds(i, 1)], ALU.is_equal, ALU.mult)
                last.then_inc(prep_ok, 1)

            def split_x(n):
                dve.wait_ge(xh_ok, n)
                dve.tensor_tensor(xe[:, :, 1, :], PREP[:, :].rearrange("p (c s) -> p c s", c=KC),
                                  xe[:, :, 0, :].bitcast(F32), ALU.subtract).then_inc(xl_ok, 1)

            dve.wait_ge(used, SPLITS)
            dve.wait_ge(n_ok, 1)
            step(dve.memset(gub[:, 0, 0, 0:1], 0.0))
            dve.memset(gub[:, 0, 0, 1:2], 0.0).then_inc(gub_ok, 1)
            prepare(0)
            split_x(1)
            items = dve.value_load(n_items[0:1, 0:1], min_val=EXPERTS, max_val=EXPERTS * CHUNKS)
            with dve.Fori(0, items) as i:
                e = dve.snap(i % EXPERTS)

                def low(p):
                    u = p // 2
                    dve.wait_ge(hi_ok, PIECES * i + (p + 1))
                    a = (p % 2) * 4 * BLK
                    dve.tensor_tensor(lo[:, p % SPLITS, :, :].rearrange("p c n -> p (c n)"),
                                      raw[:, slot_of(u), a:a + 4 * BLK],
                                      hi[:, p % SPLITS, :, :].rearrange("p c n -> p (c n)").bitcast(F32),
                                      ALU.subtract).then_inc(lo_ok, 1)

                def add_bias(half):
                    dve.wait_ge(ev_used, UNITS * i + (2 + 2 * half + 2))
                    dve.tensor_tensor(gub[:, :, :, :].rearrange("p a c s -> p (a c) s"),
                                      GUT[:, :].rearrange("p (j s) -> p j s", s=SLOTS),
                                      bias_gu[:, bass.ds(e, 1), 8 * half:8 * half + 8].rearrange("p a j -> p (a j)")
                                      .unsqueeze(2).to_broadcast([P, 8, SLOTS]), ALU.add).then_inc(gub_ok, 1)
                    dve.wait_ge(gub_ok, 2 * i + (1 + half + 1))
                    dve.tensor_scalar(glu[:, :, :], gub[:, 0], LIMIT, None, ALU.min).then_inc(glu_ok, 1)
                    dve.tensor_scalar(lin[:, :, :], gub[:, 1], LIMIT, -LIMIT, ALU.min, ALU.max).then_inc(lin_ok, 1)

                def product(half):
                    dve.wait_ge(lin_ok, 2 * i + (half + 1))
                    dve.scalar_tensor_tensor(out=prod[:, :, :], in0=lin[:, :, :], scalar=1.0, in1=glu[:, :, :],
                                             op0=ALU.add, op1=ALU.mult).then_inc(prod_ok, 1)

                def low_act(half):
                    dve.wait_ge(ah_ok, 2 * i + (half + 1))
                    dve.tensor_tensor(ae[:, 4 * half:4 * half + 4, 1, :], actv[:, :, :],
                                      ae[:, 4 * half:4 * half + 4, 0, :].bitcast(F32), ALU.subtract).then_inc(al_ok, 1)

                for p in range(6):
                    low(p)
                add_bias(0)
                low(6)
                product(0)
                low(7)
                low_act(0)
                low(8)
                add_bias(1)
                product(1)
                low(9)
                low_act(1)
                low(10)
                dve.wait_ge(sc_ok, i + 1)
                prepare(i + 1)
                low(11)
                split_x(i + 2)
            dve.wait_ge(gain_in, 32)
            dve.wait_ge(ev_used, UNITS * items + 2)
            for t in range(TT):
                for n in range(2):
                    at = slice(n * BLK, (n + 1) * BLK)
                    dve.tensor_tensor(xs[:, t, at], xs[:, t, at], ACC[2 * t + n][:, :], ALU.add).then_inc(y_ok, 1)
                dve.wait_ge(y_sq, t + 1)
                dve.tensor_scalar(stat[:, 2 + t:3 + t], stat[:, t:t + 1], 1.0 / D, EPS, ALU.mult, ALU.add).then_inc(y_ms, 1)
                dve.wait_ge(y_rt, t + 1)
                dve.reciprocal(stat[:, t:t + 1], stat[:, 4 + t:5 + t]).then_inc(fin_r, 1)
                dve.wait_ge(fin_r, t + 1)
                dve.scalar_tensor_tensor(out=xs[:, t, :], in0=xs[:, t, :], scalar=stat[:, t:t + 1], in1=gain[:, :],
                                         op0=ALU.mult, op1=ALU.mult).then_inc(o_ok, 1)

        @block.gpsimd
        def _(pool):
            step = stepper(pool, pool_step)

            def rotate(view, heads, half, every):
                ta, tb = (x[:, :, 0:heads, 0:2 * half] for x in (ropc, ropd))
                shape = [P, TT, heads, half]
                cos = trig[:, 0, :, 0:16:every].unsqueeze(2).to_broadcast(shape)
                sin = trig[:, 1, :, 0:16:every].unsqueeze(2).to_broadcast(shape)
                neg = nsin[:, :, 0:16:every].unsqueeze(2).to_broadcast(shape)
                x1, x2 = view[:, :, :, 0:half], view[:, :, :, half:2 * half]
                pool.tensor_tensor(ta[:, :, :, 0:half], x1, cos, ALU.mult)
                pool.tensor_tensor(ta[:, :, :, half:2 * half], x2, cos, ALU.mult)
                pool.tensor_tensor(tb[:, :, :, 0:half], x2, neg, ALU.mult)
                step(pool.tensor_tensor(tb[:, :, :, half:2 * half], x1, sin, ALU.mult))
                return pool.tensor_tensor(view, ta, tb, ALU.add)

            pool.wait_ge(nsin_ok, 1)
            pool.wait_ge(z_ok, 8)
            pool.wait_ge(c_sq, 1)
            pool.wait_ge(idx_ac, 6)
            step(rotate(z_ml[:, :, Q_LORA + KV_LORA:C_QB].unsqueeze(2), 1, ROPE // 2, 1))
            for t in range(TT):
                last = pool.tensor_copy(k_ml[:, t, :, NOPE:QK],
                                        z_ml[:, t, Q_LORA + KV_LORA:C_QB].unsqueeze(1).to_broadcast([P, HEADS, ROPE]))
            step(last)
            pool.wait_ge(up_a, 8)
            rotate(q_ml[:, :, :, NOPE:QK], HEADS, ROPE // 2, 1).then_inc(ml_rot, 1)
            pool.wait_ge(ml_rot, 1)
            step(rotate(z_qb[:, :, :].rearrange("p t (h d) -> p t h d", h=HEADS)[:, :, :, 0:ROT], HEADS, ROT // 2, 2))
            step(rotate(z_kv[:, :, 0:HD].unsqueeze(2)[:, :, :, 0:ROT], 1, ROT // 2, 2))
            pool.wait_ge(qi_ps, 3)
            for t in range(TT):
                last = pool.tensor_copy(kk[:, t, :, :], z_kv[:, t, 0:HD].unsqueeze(1).to_broadcast([P, 2, HD]))
            last.then_inc(qb_rot, 1)

            pool.wait_ge(n_ok, 1)
            items = pool.value_load(n_items[0:1, 0:1], min_val=EXPERTS, max_val=EXPERTS * CHUNKS)
            with pool.Fori(0, items) as i:
                for half in range(2):
                    pool.wait_ge(prod_ok, 2 * i + (half + 1))
                    pool.wait_ge(sig2_ok, 2 * i + (half + 1))
                    pool.tensor_tensor(actv[:, :, :], prod[:, :, :], sig[:, :, :], ALU.mult).then_inc(actv_ok, 1)


_INS = ['x', 'positions', 'attn_norm_g', 'w_in', 'mla_q_norm_g', 'mla_w_uq', 'mla_kv_norm_g', 'mla_w_ukv',
        'w_branch_mla', 'w_branch_dsa', 'w_out', 'ffn_norm_g', 'router_w', 'router_b',
        'w_gate_up', 'b_gate_up', 'w_down', 'b_down', 'final_norm_g']


def kernel(**inputs):
    import concourse.bacc as _bacc
    from concourse.bass_utils import run_bass_kernel_spmd as _run

    nc = _bacc.Bacc("TRN2", target_bir_lowering=False, num_devices=1)
    arrays, args = {}, []
    for name in _INS + ['consts']:
        a = constants() if name == 'consts' else np.ascontiguousarray(inputs[name])
        arrays[f"in_{name}"] = a
        args.append(nc.dram_tensor(f"in_{name}", a.shape, mybir.dt.from_np(a.dtype), kind="ExternalInput").ap())
    args.append(nc.dram_tensor("out_y", (1, TOKENS, D), F32, kind="ExternalOutput").ap())
    build(nc, *args)
    r = _run(nc, [arrays], core_ids=[0])
    return r.results[0]["out_y"]
```

```python
from contextlib import ExitStack

import numpy as np

import concourse.bass as bass
from concourse import mybir

ALU = mybir.AluOpType
ACT = mybir.ActivationFunctionType
AXX = mybir.AxisListType.X
F32 = mybir.dt.float32
F32R = mybir.dt.float32r
I32 = mybir.dt.int32

P = 128
TOKENS, D = 256, 1024
TT = TOKENS // P
EPS = 1e-6
THETA = 500000.0
NEG = -1.0e30
REMOVED = -3.0e38

HEADS = 8
Q_LORA, KV_LORA, NOPE, ROPE, V_DIM = 256, 128, 64, 32, 64
QK = NOPE + ROPE
HD, ROT = 64, 16
TOPK = min(256, TOKENS // 4)
GATES_AT = Q_LORA + KV_LORA + ROPE + 2 * HEADS * HD + 3 * HD + HEADS
D_IN = GATES_AT + 2 * D
C_QB = Q_LORA + KV_LORA + ROPE
C_KB = C_QB + HEADS * HD
C_QI = C_KB + 2 * HD
C_KI = C_QI + HEADS * HD

EXPERTS, EXP_K, FF = 32, 4, 1024
LIMIT, ALPHA = 7.0, 1.702
SLOTS = 64
CHUNKS = TOKENS // SLOTS
TABLE = EXPERTS * (CHUNKS + 1)

KC = D // P
BLK = 512
UNIT = KC * BLK
RING = 6
FRONT_UNITS = 13
UNITS = 6
PIECES = 2 * UNITS
SPLITS = 3
GU_COLS = [0, FF, BLK, FF + BLK]

Z_UNITS = [[(C_QI, 512)], [(C_KB, 128), (C_KI, HD + HEADS)], [(C_QB, 512)], [(0, C_QB)]]

BATCHES = [(0, (0, 2, 4, 6)), (0, (1, 3, 5, 7)),
           (1, (0, 2)), (1, (1, 3)), (1, (4, 6)), (1, (5, 7))]

CONST = {"ident": P, "ident2": SLOTS, "before": P, "ones": P, "slot": P, "causal": P, "invfreq": ROPE // 2}
CONST_AT = {}
for _name, _n in CONST.items():
    CONST_AT[_name] = sum(CONST[k] for k in CONST_AT)


def constants():
    r = np.arange(P)
    part = {
        "ident": np.eye(P),
        "ident2": (r[:, None] % SLOTS == np.arange(SLOTS)[None, :]),
        "before": (r[:, None] < r[None, :]),
        "ones": np.ones((P, P)),
        "slot": np.broadcast_to(r[None, :] % SLOTS, (P, P)),
        "causal": np.where(r[None, :] <= r[:, None], 0.0, NEG),
        "invfreq": np.broadcast_to(
            (np.float32(THETA) ** (-np.arange(ROPE // 2, dtype=np.float32) / np.float32(ROPE // 2))), (P, ROPE // 2)),
    }
    return np.concatenate([part[k].astype(np.float32) for k in CONST], axis=1)


def build(nc, x, positions, attn_norm_g, w_in, mla_q_norm_g, mla_w_uq, mla_kv_norm_g, mla_w_ukv,
          w_branch_mla, w_branch_dsa, w_out, ffn_norm_g, router_w, router_b,
          w_gate_up, b_gate_up, w_down, b_down, final_norm_g, consts, out):
    ctx = ExitStack()
    front = ExitStack()
    with ctx:
        def sb(name, shape, dt=F32, scope=ctx):
            return scope.enter_context(nc.sbuf_tensor(name, shape, dt))

        def sem(name):
            return ctx.enter_context(nc.semaphore(name))

        cst = sb("cst", [P, sum(CONST.values())])
        xs = sb("x_res", [P, TT, D])
        gain = sb("gain", [P, D])
        bias_gu = sb("bias_gu", [P, EXPERTS, 16])
        raw = sb("raw", [P, RING, UNIT])
        stat = sb("stat", [P, 16])
        posc = sb("posc", [P, TT, TABLE])
        gates = sb("gates", [P, TT, TABLE])
        h2 = sb("h2", [P, TT, D])
        n_items = sb("n_items", [P, 1], I32)

        def fb(name, shape, dt=F32):
            return sb(name, shape, dt, front)

        hT = fb("hT", [P, KC, TOKENS])
        area_k = fb("area_k", [P, HEADS * TOKENS])
        z_qi = area_k[:, 0:4 * TOKENS].rearrange("p (t n) -> p t n", t=TT)
        dsaT = area_k[:, 0:4 * TOKENS].rearrange("p (j t) -> p j t", j=4)
        c_qT = area_k[:, 4 * TOKENS:6 * TOKENS].rearrange("p (c t) -> p c t", c=2)
        c_kvT = area_k[:, 6 * TOKENS:7 * TOKENS]
        diag = area_k[:, 7 * TOKENS:8 * TOKENS].rearrange("p (t n) -> p t n", t=TT)
        kmT = area_k[0:QK, :].rearrange("p (h t) -> p h t", h=HEADS)
        z_kv = fb("z_kv", [P, TT, 200])
        z_qb = fb("z_qb", [P, TT, 512])
        z_ml = fb("z_ml", [P, TT, C_QB])
        sgT = fb("sgT", [P, KC, 2, TOKENS])
        qT = fb("qT", [P, 4, TOKENS])
        kT = fb("kT", [P, TOKENS])
        kk = fb("kk", [P, TT, 2, HD])
        score = fb("score", [P, TT, TOKENS])
        work = fb("work", [P, TT, TOKENS])
        pick = fb("pick", [P, 3, TOKENS])
        allow = fb("allow", [P, TT, TOKENS])
        area_p = fb("area_p", [P, 4 * BLK])
        prob = area_p[:, 0:2 * BLK].rearrange("p (b n) -> p b n", b=2)
        probT = area_p[:, 2 * BLK:4 * BLK].rearrange("p (b n) -> p b n", b=2)
        k_ml = area_p[:, 0:TT * HEADS * QK].rearrange("p (t h d) -> p t h d", t=TT, h=HEADS)
        q_ml = fb("q_ml", [P, TT, HEADS, QK])
        v_ml = fb("v_ml", [P, TT, HEADS, V_DIM])
        bgu = h2[0:EXPERTS, :, :].rearrange("p t n -> p (t n)")
        qmT = h2[0:QK, :, :].rearrange("p t n -> p (t n)").rearrange("p (h t) -> p h t", h=HEADS)
        rstd_row = fb("rstd_row", [P, TOKENS])
        g_in = fb("g_in", [P, KC])
        g_q = fb("g_q", [P, 2])
        g_kv = fb("g_kv", [P, 1])
        pos_i = fb("pos_i", [P, TT], I32)
        pos_f = fb("pos_f", [P, TT])
        ang = fb("ang", [P, 2, TT, 16])
        turns = fb("turns", [P, 2, TT, 16])
        trig = fb("trig", [P, 2, TT, 16])
        nsin = fb("nsin", [P, TT, 16])
        ropa = fb("ropa", [P, TT, HEADS, ROT])
        ropb = fb("ropb", [P, TT, HEADS, ROT])
        ropc = fb("ropc", [P, TT, HEADS, ROPE])
        ropd = fb("ropd", [P, TT, HEADS, ROPE])
        w_idx = fb("w_idx", [P, TT, HEADS])
        top8 = fb("top8", [P, TT, 8])
        cnt = fb("cnt", [P, TT])
        mx = fb("mx", [P, 2, 4])
        den = fb("den", [P, 2, 4])
        rw = fb("rw", [P, KC, EXPERTS])
        rb = fb("rb", [P, EXPERTS])
        lg, r_a, r_b, sel, gate, pm = (
            z_ml[:, :, :].rearrange("p t n -> p (t n)")[:, k * TT * EXPERTS:(k + 1) * TT * EXPERTS]
            .rearrange("p (t e) -> p t e", t=TT) for k in range(6))
        r_s = fb("r_s", [P, TT, 4])
        gateT = z_qb[0:EXPERTS, 0, 0:TOKENS]
        q_ml_flat = q_ml[:, :, :, :].rearrange("p t h d -> p (t h d)")
        mlaT = q_ml_flat[:, 0:4 * TOKENS].rearrange("p (j t) -> p j t", j=4)
        bd = q_ml_flat[0:EXPERTS, 0:D]
        front.close()

        hi = sb("w_hi", [P, SPLITS, 4, BLK], F32R)
        lo = sb("w_lo", [P, SPLITS, 4, BLK], F32R)
        xe = sb("x_split", [P, KC, 2, SLOTS], F32R)
        ae = sb("a_split", [P, KC, 2, SLOTS], F32R)
        ev = sb("ev", [P, 2, BLK])
        onehot = sb("onehot", [P, TT, SLOTS])
        gated = sb("gated", [P, TT, P])
        scat = sb("scat", [P, TOKENS])
        gub = sb("gub", [P, 2, 4, SLOTS])
        glu = sb("glu", [P, 4, SLOTS])
        lin = sb("lin", [P, 4, SLOTS])
        sig = sb("sig", [P, 4, SLOTS])
        prod = sb("prod", [P, 4, SLOTS])
        actv = sb("actv", [P, 4, SLOTS])

        B = [ctx.enter_context(nc.psum_tensor(f"bank{i}", [P, BLK], F32)) for i in range(8)]
        ZB, TB, SB, VB = B[0:2], B[2:4], B[4:6], B[6:8]
        ACC, MM, PREP, GUT = B[0:4], B[4:6], B[6], B[7]

        def const(name, rows=P):
            a = CONST_AT[name]
            return cst[0:rows, a:a + CONST[name]]

        ident = const("ident")

        x_in = [sem(f"x_in{t}") for t in range(TT)]
        cst_in = sem("cst_in")
        early_in = sem("early_in")
        small_in = sem("small_in")
        SMALL = 16 * 5
        bd_in = sem("bd_in")
        gain_in = sem("gain_in")
        final_in = sem("final_in")
        raw_in = [sem(f"raw_in{i}") for i in range(RING)]
        out_done = sem("out_done")
        act_step = sem("act_step")
        dve_step = sem("dve_step")
        pool_step = sem("pool_step")
        x_sq = sem("x_sq")
        x_ms = sem("x_ms")
        x_rt = sem("x_rt")
        diag_ok = sem("diag_ok")
        xT_ps = sem("xT_ps")
        rstd_ps = sem("rstd_ps")
        hT_ok = sem("hT_ok")
        ang_ok = sem("ang_ok")
        trig_ok = sem("trig_ok")
        nsin_ok = sem("nsin_ok")
        bgu_ps = sem("bgu_ps")
        bgu_ok = sem("bgu_ok")
        z_ps = sem("z_ps")
        z_ok = sem("z_ok")
        qi_rot = sem("qi_rot")
        qi_ps = sem("qi_ps")
        qi_ok = sem("qi_ok")
        idx_ps = sem("idx_ps")
        idx_rl = sem("idx_rl")
        idx_ac = sem("idx_ac")
        c_sq = sem("c_sq")
        c_ms = sem("c_ms")
        c_rt = sem("c_rt")
        c_rs = sem("c_rs")
        c_ps = sem("c_ps")
        c_ok = sem("c_ok")
        up_ps = sem("up_ps")
        up_a = sem("up_a")
        up_d = sem("up_d")
        ml_rot = sem("ml_rot")
        qb_rot = sem("qb_rot")
        mT_ps = sem("mT_ps")
        mq_ok = sem("mq_ok")
        mk_ok = sem("mk_ok")
        g_ps = sem("g_ps")
        g_ok = sem("g_ok")
        s_ps = sem("s_ps")
        s_mx = sem("s_mx")
        p_ex = sem("p_ex")
        p_ok = sem("p_ok")
        pT_ps = sem("pT_ps")
        pT_ok = sem("pT_ok")
        pv_ps = sem("pv_ps")
        pv_ok = sem("pv_ok")
        qd_ps = sem("qd_ps")
        qd_ok = sem("qd_ok")
        allow_ok = sem("allow_ok")
        sig_ok = sem("sig_ok")
        br_ps = sem("br_ps")
        br_ok = sem("br_ok")
        wo_ps = sem("wo_ps")
        x1_ok = sem("x1_ok")
        f_sq = sem("f_sq")
        f_ms = sem("f_ms")
        f_rt = sem("f_rt")
        h2_ok = sem("h2_ok")
        h2T_ps = sem("h2T_ps")
        h2T_ok = sem("h2T_ok")
        lg_ps = sem("lg_ps")
        lg_mx = sem("lg_mx")
        lg_ex = sem("lg_ex")
        sel_ok = sem("sel_ok")
        gate_ok = sem("gate_ok")
        pos_ps = sem("pos_ps")
        gT_ps = sem("gT_ps")
        gT_ok = sem("gT_ok")
        n_ok = sem("n_ok")
        prep_ok = sem("prep_ok")
        gath_ps = sem("gath_ps")
        xh_ok = sem("xh_ok")
        xl_ok = sem("xl_ok")
        sc_ps = sem("sc_ps")
        sc_ok = sem("sc_ok")
        hi_ok = sem("hi_ok")
        lo_ok = sem("lo_ok")
        used = sem("used")
        ev_ok = sem("ev_ok")
        ev_used = sem("ev_used")
        gub_ok = sem("gub_ok")
        glu_ok = sem("glu_ok")
        lin_ok = sem("lin_ok")
        sig2_ok = sem("sig2_ok")
        prod_ok = sem("prod_ok")
        actv_ok = sem("actv_ok")
        ah_ok = sem("ah_ok")
        al_ok = sem("al_ok")
        y_ok = sem("y_ok")
        y_sq = sem("y_sq")
        y_ms = sem("y_ms")
        y_rt = sem("y_rt")
        o_ok = sem("o_ok")
        fin_r = sem("fin_r")

        w_in_v = w_in[0].rearrange("(p c) n -> p c n", c=KC)
        w_uq_v = mla_w_uq[0].rearrange("(p c) n -> p c n", c=2)
        w_ukv_v = mla_w_ukv[0]
        w_br_v = [w[0].rearrange("(c p) n -> p c n", p=P) for w in (w_branch_mla, w_branch_dsa)]
        w_out_v = w_out[0].rearrange("(c p) n -> p c n", p=P)
        w_gu_v = w_gate_up[0].rearrange("e (c p) n -> e p c n", p=P)
        w_dn_v = w_down[0].rearrange("e (b p c) n -> e b p (c n)", b=2, c=4)

        def unit(n):
            return raw[:, n % RING, :]

        def unit3(n, cols=BLK):
            return unit(n)[:, 0:KC * cols].rearrange("p (c n) -> p c n", c=KC)

        U_UP, U_G, U_BR, U_WO = 4, 5, 9, 11
        up_q = unit(U_UP)[:, 0:2 * HEADS * QK].rearrange("p (c n) -> p c n", c=2)
        up_kv = unit(U_UP)[:, 2 * HEADS * QK:2 * HEADS * QK + HEADS * (NOPE + V_DIM)]
        br_w = [unit(U_BR + i)[:, 0:4 * D].rearrange("p (c n) -> p c n", c=4) for i in range(2)]

        EXTRA = [16 if s in (1, U_UP % RING) else 0 for s in range(RING)]

        def landed_front(eng, n):
            eng.wait_ge(raw_in[n % RING], 16 * (n // RING + 1) + EXTRA[n % RING])

        def slot_of(u):
            return (FRONT_UNITS + u) % RING

        def used_up(eng, n):
            if n < U_UP:
                eng.wait_ge(z_ps, 2 * n + 2)
            elif n == U_UP:
                eng.wait_ge(up_ps, 4)
            elif n < U_BR:
                eng.wait_ge(g_ps, 4 * (n - U_G + 1))
            elif n < U_WO:
                eng.wait_ge(br_ps, KC)
            else:
                eng.wait_ge(wo_ps, 3 + n - U_WO)

        def landed_expert(eng, i, u):
            before = 16 * len([n for n in range(FRONT_UNITS) if n % RING == slot_of(u)]) + EXTRA[slot_of(u)]
            eng.wait_ge(raw_in[slot_of(u)], 16 * i + (before + 16))

        def piece_of(p):
            a = raw[:, slot_of(p // 2), :]
            if p < 8:
                return a.rearrange("p (h c n) -> p h c n", h=2, c=4)[:, p % 2]
            return a.rearrange("p (c h n) -> p c h n", c=4, h=2)[:, :, p % 2]

        def pieces_until(u):
            return 2 * u + 2 if u < 4 else 11 + u - 4

        h2T = sgT[:, :, :, :].rearrange("p c a t -> p (c a t)")[:, 0:KC * TOKENS].rearrange("p (c t) -> p c t", c=KC)
        mT = hT

        def stepper(eng, signal):
            n = [0]

            def step(ins):
                n[0] += 1
                ins.then_inc(signal, 1)
                eng.wait_ge(signal, n[0])
            return step

        block = ctx.enter_context(nc.Block())

        @block.sync
        def _(sp):
            for t in range(TT):
                sp.dma_start(xs[:, t, :], x[0, t * P:(t + 1) * P, :]).then_inc(x_in[t], 16)
            sp.dma_start(cst[:, :], consts).then_inc(cst_in, 16)
            sp.dma_start(g_in[:, :], attn_norm_g[0].rearrange("(p c) -> p c", c=KC)).then_inc(early_in, 16)
            for t in range(TT):
                sp.dma_start(pos_i[:, t:t + 1], positions[0, t * P:(t + 1) * P].rearrange("(p a) -> p a", a=1))\
                    .then_inc(early_in, 16)

            def load_front(n):
                if n >= RING:
                    used_up(sp, n - RING)
                done = raw_in[n % RING]
                if n < 4 and n != 1:
                    c0, w = Z_UNITS[n][0]
                    sp.dma_start(unit3(n, w), w_in_v[:, :, c0:c0 + w]).then_inc(done, 16)
                elif n == 1:
                    at = 0
                    for c0, w in Z_UNITS[1]:
                        sp.dma_start(unit3(1, 200)[:, :, at:at + w], w_in_v[:, :, c0:c0 + w]).then_inc(done, 16)
                        at += w
                elif n == U_UP:
                    sp.dma_start(up_kv, w_ukv_v).then_inc(done, 16)
                    sp.dma_start(up_q, w_uq_v).then_inc(done, 16)
                elif n < U_BR:
                    c0 = GATES_AT + (n - U_G) * BLK
                    sp.dma_start(unit3(n), w_in_v[:, :, c0:c0 + BLK]).then_inc(done, 16)
                elif n < U_WO:
                    sp.dma_start(br_w[n - U_BR], w_br_v[n - U_BR]).then_inc(done, 16)
                else:
                    c0 = (n - U_WO) * BLK
                    sp.dma_start(unit3(n), w_out_v[:, :, c0:c0 + BLK]).then_inc(done, 16)

            def load_expert(e, u):
                if u < 4:
                    c0 = GU_COLS[u]
                    to = raw[:, slot_of(u), :].rearrange("p (c n) -> p c n", c=KC)
                    sp.dma_start(to, w_gu_v[e, :, :, c0:c0 + BLK]).then_inc(raw_in[slot_of(u)], 16)
                else:
                    sp.dma_start(raw[:, slot_of(u), :], w_dn_v[e, u - 4]).then_inc(raw_in[slot_of(u)], 16)

            load_front(0)
            load_front(1)
            sp.dma_start(bgu, b_gate_up[0]).then_inc(small_in, 16)
            sp.dma_start(g_q[:, :], mla_q_norm_g[0].rearrange("(p c) -> p c", c=2)).then_inc(small_in, 16)
            sp.dma_start(g_kv[:, :], mla_kv_norm_g[0].rearrange("(p c) -> p c", c=1)).then_inc(small_in, 16)
            sp.dma_start(rw[:, :, :], router_w[0].rearrange("(p c) n -> p c n", c=KC)).then_inc(small_in, 16)
            sp.dma_start(rb[:, :], router_b[0].partition_broadcast(P)).then_inc(small_in, 16)
            load_front(2)
            load_front(3)
            for j in range(2):
                sp.dma_start(gain[:, j * BLK:(j + 1) * BLK],
                             ffn_norm_g[0, j * BLK:(j + 1) * BLK].partition_broadcast(P)).then_inc(gain_in, 16)
            for n in range(4, FRONT_UNITS):
                load_front(n)
            for u in range(UNITS):
                used_up(sp, FRONT_UNITS + u - RING)
                load_expert(0, u)
            sp.wait_ge(n_ok, 1)
            items = sp.value_load(n_items[0:1, 0:1], min_val=EXPERTS, max_val=EXPERTS * CHUNKS)
            with sp.Fori(1, items) as i:
                e = sp.snap(i % EXPERTS)
                for u in range(UNITS):
                    sp.wait_ge(lo_ok, PIECES * i + (2 * u + 2 - PIECES))
                    load_expert(e, u)
            for t in range(TT):
                sp.wait_ge(o_ok, t + 1)
                sp.dma_start(out[0, t * P:(t + 1) * P, :], xs[:, t, :]).then_inc(out_done, 16)
            sp.wait_ge(out_done, 16 * TT)

        @block.tensor
        def _(pe):
            def gemm(o, lhs, rhs, n, start=True):
                for c in range(n):
                    mm = pe.matmul(o, lhs(c), rhs(c), start=start and c == 0, stop=c == n - 1)
                return mm

            pe.wait_ge(cst_in, 16)
            pe.wait_ge(x_in[0], 16)
            pe.wait_ge(x_in[1], 16)
            for c in range(KC):
                for t in range(TT):
                    a = (c % 2) * TOKENS + t * P
                    tr = pe.transpose(B[2 + c // 2][:, a:a + P], xs[:, t, c:D:KC], ident)
                tr.then_inc(xT_ps, 1)
            pe.wait_ge(diag_ok, TT)
            for t in range(TT):
                mm = pe.matmul(B[6][:, t * P:(t + 1) * P], const("ones"), diag[:, t, :], start=True, stop=True)
            mm.then_inc(rstd_ps, 1)
            z_n = 0

            def z_unit(n):
                nonlocal z_n
                w = sum(c for _, c in Z_UNITS[n])
                landed_front(pe, n)
                for t in range(TT):
                    if z_n >= 2:
                        pe.wait_ge(z_ok, z_n - 1)
                    for c in range(KC):
                        if z_n == 0:
                            pe.wait_ge(hT_ok, c + 1)
                        mm = pe.matmul(ZB[t][:, 0:w], hT[:, c, t * P:(t + 1) * P], unit3(n, w)[:, c, :],
                                       start=c == 0, stop=c == KC - 1)
                    mm.then_inc(z_ps, 1)
                    z_n += 1

            def scores(b, q, k, signal):
                t, heads = BATCHES[b % 6]
                w = P * (t + 1)
                for m, h in enumerate(heads):
                    mm = pe.matmul(SB[b % 2][:, m * w:(m + 1) * w], q(h, t), k(h, w), start=True, stop=True)
                mm.then_inc(signal, 1)

            def pair_q(h, t):
                return qT[HD * (h % 2):HD * (h % 2) + HD, h // 2, t * P:(t + 1) * P]

            def pair_k(h, w):
                return kT[HD * (h % 2):HD * (h % 2) + HD, 0:w]

            def turn_pairs(zq, signal):
                for j in range(4):
                    for t in range(TT):
                        a = (j % 2) * TOKENS + t * P
                        tr = pe.transpose(TB[j // 2][:, a:a + P], zq[:, t, j * P:(j + 1) * P], ident)
                    if j % 2:
                        tr.then_inc(signal, 1)
                for t in range(TT):
                    tr = pe.transpose(VB[0][:, t * P:(t + 1) * P], kk[:, t, :, :].rearrange("p a d -> p (a d)"), ident)
                tr.then_inc(signal, 1)

            g_n = 0

            def gate_block():
                nonlocal g_n
                n = U_G + g_n // 4
                if g_n % 4 == 0:
                    landed_front(pe, n)
                if g_n >= 2:
                    pe.wait_ge(g_ok, g_n - 1)
                else:
                    pe.wait_ge(z_ok, 7 + g_n)
                a = (g_n % 4) * P
                mm = gemm(ZB[g_n % 2][:, 0:TOKENS], lambda c: unit3(n)[:, c, a:a + P], lambda c: hT[:, c, :], KC)
                mm.then_inc(g_ps, 1)
                g_n += 1

            z_unit(0)
            z_unit(1)
            pe.wait_ge(small_in, SMALL)
            for u in range(4):
                for c in range(4):
                    a = GU_COLS[u] + c
                    j = (u * 4 + c) * EXPERTS
                    tr = pe.transpose(B[7][:, j:j + EXPERTS], bgu[:, a:GU_COLS[u] + BLK:4], ident[0:EXPERTS, 0:EXPERTS])
            tr.then_inc(bgu_ps, 1)
            z_unit(2)
            pe.wait_ge(qi_rot, 1)
            turn_pairs(z_qi, qi_ps)
            z_unit(3)
            pe.wait_ge(qi_ok, 3)
            for b in range(6):
                if b >= 2:
                    pe.wait_ge(idx_rl, b - 1)
                scores(b, pair_q, pair_k, idx_ps)
                if b in (1, 3):
                    gate_block()
            pe.wait_ge(qb_rot, 1)
            turn_pairs(z_qb, qd_ps)
            gate_block()

            pe.wait_ge(z_ok, 8)
            pe.wait_ge(qd_ok, 3)
            for c in range(2):
                for t in range(TT):
                    tr = pe.transpose(TB[0][:, c * TOKENS + t * P:c * TOKENS + (t + 1) * P],
                                      z_ml[:, t, c:Q_LORA:2], ident)
            tr.then_inc(c_ps, 1)
            for t in range(TT):
                tr = pe.transpose(TB[1][:, t * P:(t + 1) * P], z_ml[:, t, Q_LORA:Q_LORA + KV_LORA], ident)
            tr.then_inc(c_ps, 1)
            gate_block()
            pe.wait_ge(bgu_ok, 1)
            landed_front(pe, U_UP)
            pe.wait_ge(c_ok, 2)
            pe.wait_ge(idx_rl, 6)
            n = 0
            for t in range(TT):
                at = slice(t * P, (t + 1) * P)
                if t:
                    pe.wait_ge(up_a, 2)
                gemm(SB[0][:, 0:BLK], lambda c: c_qT[:, c, at], lambda c: up_q[:, c, 0:BLK], 2)
                gemm(SB[1][:, 0:256], lambda c: c_qT[:, c, at], lambda c: up_q[:, c, BLK:768], 2).then_inc(up_ps, 1)
                if t:
                    pe.wait_ge(up_a, 4)
                    pe.wait_ge(up_d, 2)
                for j in range(2):
                    mm = gemm(VB[j][:, :], lambda c: c_kvT[:, at], lambda c: up_kv[:, j * BLK:(j + 1) * BLK], 1)
                mm.then_inc(up_ps, 1)
            gate_block()
            gate_block()
            pe.wait_ge(ml_rot, 1)
            pe.wait_ge(c_ok, 2)
            n = 0
            for j in range(4):
                for src, out_ok in ((q_ml, mq_ok), (k_ml, mk_ok)):
                    if j:
                        pe.wait_ge(out_ok, j)
                    for h in (2 * j, 2 * j + 1):
                        for t in range(TT):
                            a = (h % 2) * TOKENS + t * P
                            tr = pe.transpose(TB[n % 2][0:QK, a:a + P], src[:, t, h, :], ident)
                    tr.then_inc(mT_ps, 1)
                    n += 1
            pe.wait_ge(mq_ok, 4)
            pe.wait_ge(mk_ok, 4)

            def scores_of(b):
                if b >= 2:
                    pe.wait_ge(s_mx, b - 1)
                if b < 6:
                    scores(b, lambda h, t: qmT[:, h, t * P:(t + 1) * P], lambda h, w: kmT[:, h, 0:w], s_ps)
                else:
                    scores(b, pair_q, pair_k, s_ps)

            def turn_probs(b):
                pe.wait_ge(p_ok, b + 1)
                if b >= 2:
                    pe.wait_ge(pT_ok, b - 1)
                for m in range(4):
                    tr = pe.transpose(TB[b % 2][:, m * P:(m + 1) * P], prob[:, b % 2, m * P:(m + 1) * P], ident)
                tr.then_inc(pT_ps, 1)

            def values(b):
                t, heads = BATCHES[b % 6]
                pe.wait_ge(pT_ok, b + 1)
                if b in (6, 8):
                    pe.wait_ge(pv_ok, t + 1)
                for m in range(4):
                    h = heads[m // (t + 1)]
                    kt = m % (t + 1)
                    half = V_DIM * (h % 2)
                    v = v_ml[:, kt, h, :] if b < 6 else z_kv[:, kt, HD:2 * HD]
                    mm = pe.matmul(VB[t][half:half + V_DIM, (h // 2) * P:(h // 2 + 1) * P], v,
                                   probT[:, b % 2, m * P:(m + 1) * P], start=kt == 0, stop=kt == t)
                mm.then_inc(pv_ps, 1)

            pe.wait_ge(up_d, 4)
            pe.wait_ge(up_a, 8)
            scores_of(0)
            for b in range(12):
                if b < 11:
                    scores_of(b + 1)
                if b:
                    values(b - 1)
                if g_n < 16:
                    gate_block()
                turn_probs(b)
            values(11)

            landed_front(pe, U_BR)
            landed_front(pe, U_BR + 1)
            pe.wait_ge(pv_ok, 4)
            pe.wait_ge(s_mx, 12)
            for mc in range(KC):
                if mc >= 2:
                    pe.wait_ge(br_ok, 2 * (mc - 1) - 1)
                for i, o in enumerate((mlaT, dsaT)):
                    mm = gemm(SB[mc % 2][:, i * TOKENS:(i + 1) * TOKENS],
                              lambda c: br_w[i][:, c, mc * P:(mc + 1) * P], lambda c: o[:, c, :], 4)
                mm.then_inc(br_ps, 1)
            landed_front(pe, U_WO)
            landed_front(pe, U_WO + 1)
            pe.wait_ge(g_ok, 16)
            pe.wait_ge(pT_ok, 12)
            for t in range(TT):
                for n in range(2):
                    for c in range(KC):
                        if t == 0 and n == 0:
                            pe.wait_ge(br_ok, 2 * (c + 1))
                        mm = pe.matmul(B[2 * t + n][:, :], mT[:, c, t * P:(t + 1) * P], unit3(U_WO + n)[:, c, :],
                                       start=c == 0, stop=c == KC - 1)
                    mm.then_inc(wo_ps, 1)
            for t in range(TT):
                pe.wait_ge(h2_ok, t + 1)
                for c in range(KC):
                    tr = pe.transpose(B[4 + 2 * t + c // 4][:, (c % 4) * P:(c % 4 + 1) * P], h2[:, t, c:D:KC], ident)
                    if c % 4 == 3:
                        tr.then_inc(h2T_ps, 1)
            for t in range(TT):
                pe.wait_ge(h2T_ok, 2 * t + 2)
                gemm(B[0][:, t * EXPERTS:(t + 1) * EXPERTS], lambda c: h2T[:, c, t * P:(t + 1) * P],
                     lambda c: rw[:, c, :], KC).then_inc(lg_ps, 1)
            pe.wait_ge(sel_ok, 1)
            ones, before = const("ones"), const("before")
            pe.matmul(B[7][:, 0:32], before, sel[:, 0, :], start=True, stop=True)
            pe.matmul(B[7][:, 32:64], ones, sel[:, 0, :], start=True, stop=False)
            pe.matmul(B[7][:, 32:64], before, sel[:, 1, :], start=False, stop=True)
            pe.matmul(B[7][:, 64:96], ones, sel[:, 0, :], start=True, stop=False)
            pe.matmul(B[7][:, 64:96], ones, sel[:, 1, :], start=False, stop=True).then_inc(pos_ps, 1)
            pe.wait_ge(gate_ok, 1)
            for t in range(TT):
                tr = pe.transpose(B[2][0:EXPERTS, t * P:(t + 1) * P], gate[:, t, :], ident)
            tr.then_inc(gT_ps, 1)
            pe.wait_ge(gT_ok, 1)
            pe.wait_ge(bd_in, 16)
            for t in range(TT):
                for n in range(2):
                    mm = pe.matmul(ACC[2 * t + n][:, :], gateT[:, t * P:(t + 1) * P], bd[:, n * BLK:(n + 1) * BLK],
                                   start=True, stop=True)
                if t == 0:
                    mm.then_inc(ev_used, 2)
            mm.then_inc(used, SPLITS)

            def gather():
                for c in range(KC):
                    for t in range(TT):
                        mm = pe.matmul(PREP[:, c * SLOTS:(c + 1) * SLOTS], h2[:, t, c * P:(c + 1) * P],
                                       onehot[:, t, :], start=t == 0, stop=t == TT - 1)
                mm.then_inc(gath_ps, 1)

            pe.wait_ge(prep_ok, 1)
            gather()
            pe.wait_ge(n_ok, 1)
            items = pe.value_load(n_items[0:1, 0:1], min_val=EXPERTS, max_val=EXPERTS * CHUNKS)

            def scatter(n, i):
                pe.wait_ge(ev_ok, UNITS * i + (2 + 4 + n + 1 - UNITS))
                for t in range(TT):
                    mm = pe.matmul(ACC[2 * t + n][:, :], scat[:, t * P:(t + 1) * P], ev[:, n, :],
                                   start=False, stop=True, skip_group_check=True)
                mm.then_inc(ev_used, 1)

            def item(i, first):
                def piece(p):
                    down = p >= 8
                    if down:
                        bank, chunk, begin, end = p % 2, 4 * ((p - 8) // 2), p < 10, p >= 10
                    else:
                        bank, chunk, begin, end = p // 2 % 2, 4 * (p % 2), p % 2 == 0, p % 2 == 1
                    if begin:
                        unit_no = p - 4 if down else p // 2
                        pe.wait_ge(ev_ok, UNITS * i + (unit_no + 1))
                    x_of = ae if down else xe
                    pe.wait_ge(hi_ok, PIECES * i + (p + 1))
                    for c in range(4):
                        pe.matmul(MM[bank][:, :], x_of[:, chunk + c, :, :].rearrange("p a s -> p (a s)"),
                                  hi[:, p % SPLITS, c, :], start=begin and c == 0, stop=False)
                    pe.wait_ge(lo_ok, PIECES * i + (p + 1))
                    for c in range(4):
                        mm = pe.matmul(MM[bank][:, :], x_of[:, chunk + c, :, :].rearrange("p a s -> p (a s)"),
                                       lo[:, p % SPLITS, c, :], start=False, stop=end and c == 3)
                    mm.then_inc(used, 1)

                def turn(u):
                    pe.wait_ge(ev_ok, UNITS * i + (2 + u + 1))
                    if u % 2 == 0:
                        pe.wait_ge(gub_ok, 2 * i + (u // 2 + 1))
                    for c in range(4):
                        a = ((u % 2) * 4 + c) * SLOTS
                        mm = pe.matmul(GUT[:, a:a + SLOTS], ev[:, u % 2, c:BLK:4], const("ident2"),
                                       start=True, stop=True)
                    mm.then_inc(ev_used, 1)

                pe.wait_ge(xl_ok, i + 1)
                piece(0)
                if not first:
                    scatter(0, i)
                piece(1)
                if not first:
                    scatter(1, i)
                piece(2)
                turn(0)
                for t in range(TT):
                    tr = pe.transpose(PREP[:, t * P:(t + 1) * P], gated[:, t, :], ident)
                tr.then_inc(sc_ps, 1)
                piece(3)
                piece(4)
                turn(1)
                piece(5)
                piece(6)
                turn(2)
                piece(7)
                pe.wait_ge(al_ok, 2 * i + 1)
                piece(8)
                turn(3)
                piece(9)
                pe.wait_ge(prep_ok, i + 2)
                pe.wait_ge(sc_ok, i + 1)
                gather()
                pe.wait_ge(al_ok, 2 * i + 2)
                piece(10)
                piece(11)

            item(0, True)
            with pe.Fori(1, items) as i:
                item(i, False)
            scatter(0, items)
            scatter(1, items)

        @block.scalar
        def _(act):
            step = stepper(act, act_step)
            for t in range(TT):
                act.wait_ge(x_in[t], 16)
                step(act.activation(sgT[:, 0:2, :, :].rearrange("p c a t -> p (c a t)"),
                                    xs[:, t, :], ACT.Square, accum_out=stat[:, t:t + 1]))
            act.copy(stat[:, 6:7], stat[:, 1:2]).then_inc(x_sq, 1)
            act.wait_ge(x_ms, 1)
            act.activation(stat[:, 4:6], stat[:, 2:4], ACT.Sqrt).then_inc(x_rt, 1)
            act.wait_ge(ang_ok, 1)
            act.activation(trig[:, :, :, :], ang[:, :, :, :], ACT.Sin).then_inc(trig_ok, 1)

            z_out = [lambda t: z_qi[:, t, :], lambda t: z_kv[:, t, :], lambda t: z_qb[:, t, :], lambda t: z_ml[:, t, :]]

            def z_evac(n):
                w = sum(c for _, c in Z_UNITS[n])
                for t in range(TT):
                    act.wait_ge(z_ps, 2 * n + t + 1)
                    act.copy(z_out[n](t), ZB[t][:, 0:w]).then_inc(z_ok, 1)

            z_evac(0)
            z_evac(1)
            z_evac(2)
            for j in range(2):
                act.wait_ge(qi_ps, j + 1)
                act.copy(qT[:, 2 * j:2 * j + 2, :].rearrange("p j t -> p (j t)"), TB[j][:, :]).then_inc(qi_ok, 1)
            act.wait_ge(qi_ps, 3)
            act.copy(kT[:, :], VB[0][:, 0:TOKENS]).then_inc(qi_ok, 1)
            z_evac(3)
            g_n = 0

            def gate_evac():
                nonlocal g_n
                act.wait_ge(g_ps, g_n + 1)
                act.copy(sgT[:, g_n % KC, g_n // KC, :], ZB[g_n % 2][:, 0:TOKENS]).then_inc(g_ok, 1)
                g_n += 1

            for b in range(6):
                act.wait_ge(idx_ps, b + 1)
                if b >= 2:
                    act.wait_ge(idx_ac, b - 1)
                act.activation(prob[:, b % 2, :], SB[b % 2][:, :], ACT.Relu, scale=HD ** -0.5).then_inc(idx_rl, 1)
                if b in (1, 3):
                    gate_evac()
            for j in range(2):
                act.wait_ge(qd_ps, j + 1)
                act.copy(qT[:, 2 * j:2 * j + 2, :].rearrange("p j t -> p (j t)"), TB[j][:, :]).then_inc(qd_ok, 1)
            act.wait_ge(qd_ps, 3)
            act.copy(kT[:, :], VB[0][:, 0:TOKENS]).then_inc(qd_ok, 1)
            for t in range(TT):
                step(act.activation(probT[:, 0, 0:Q_LORA], z_ml[:, t, 0:Q_LORA],
                                    ACT.Square, accum_out=stat[:, 7 + t:8 + t]))
                step(act.activation(probT[:, 0, 0:KV_LORA], z_ml[:, t, Q_LORA:Q_LORA + KV_LORA],
                                    ACT.Square, accum_out=stat[:, 9 + t:10 + t]))
            act.copy(stat[:, 6:7], stat[:, 10:11]).then_inc(c_sq, 1)
            act.wait_ge(c_ms, 1)
            act.activation(stat[:, 7:11], stat[:, 7:11], ACT.Sqrt).then_inc(c_rt, 1)

            gate_evac()
            gate_evac()
            act.wait_ge(c_rs, 1)
            act.wait_ge(idx_ac, 6)
            for t in range(TT):
                act.wait_ge(up_ps, 2 * t + 1)
                q_flat = q_ml[:, t, :, :].rearrange("p h d -> p (h d)")
                act.activation(q_flat[:, 0:BLK], SB[0][:, :], ACT.Copy, scale=stat[:, 11 + t:12 + t]).then_inc(up_a, 1)
                act.activation(q_flat[:, BLK:768], SB[1][:, 0:256], ACT.Copy, scale=stat[:, 11 + t:12 + t]).then_inc(up_a, 1)
                act.wait_ge(up_ps, 2 * t + 2)
                for j in range(2):
                    src = VB[j][:, :].rearrange("p (h d) -> p h d", h=4)
                    act.activation(k_ml[:, t, 4 * j:4 * j + 4, 0:NOPE], src[:, :, 0:NOPE], ACT.Copy,
                                   scale=stat[:, 13 + t:14 + t]).then_inc(up_a, 1)
            gate_evac()
            gate_evac()
            for j in range(4):
                act.wait_ge(mT_ps, 2 * j + 1)
                act.copy(qmT[:, 2 * j:2 * j + 2, :].rearrange("p h t -> p (h t)"), TB[0][0:QK, :]).then_inc(mq_ok, 1)

            def exps(b):
                t, heads = BATCHES[b % 6]
                w = P * (t + 1)
                act.wait_ge(s_mx, b + 1)
                for m in range(len(heads)):
                    ex = act.activation(prob[:, b % 2, m * w:(m + 1) * w], prob[:, b % 2, m * w:(m + 1) * w], ACT.Exp,
                                        bias=mx[:, b % 2, m:m + 1], accum_out=den[:, b % 2, m:m + 1])
                ex.then_inc(p_ex, 1)

            def out_of(b):
                if b % 6 in (1, 5):
                    act.wait_ge(pv_ps, b + 1)
                    t = BATCHES[b % 6][0]
                    to = mlaT if b < 6 else dsaT
                    act.copy(to[:, :, t * P:(t + 1) * P], VB[t][:, :].rearrange("p (j q) -> p j q", j=4)).then_inc(pv_ok, 1)

            exps(0)
            for b in range(12):
                if b < 11:
                    exps(b + 1)
                if b:
                    out_of(b - 1)
                if g_n < 16:
                    gate_evac()
                act.wait_ge(pT_ps, b + 1)
                act.copy(probT[:, b % 2, :], TB[b % 2][:, :]).then_inc(pT_ok, 1)
            out_of(11)
            act.wait_ge(g_ok, 16)
            for mc in range(0, KC, 2):
                act.activation(sgT[:, mc:mc + 2, :, :], sgT[:, mc:mc + 2, :, :], ACT.Sigmoid).then_inc(sig_ok, 1)
            act.wait_ge(br_ps, KC)
            act.dma_start(bd, b_down[0]).then_inc(bd_in, 16)
            for t in range(TT):
                act.wait_ge(x1_ok, 2 * t + 2)
                step(act.activation(h2[:, t, :], xs[:, t, :], ACT.Square, accum_out=stat[:, t:t + 1]))
                act.copy(stat[:, 6:7], stat[:, t:t + 1]).then_inc(f_sq, 1)
                act.wait_ge(f_ms, t + 1)
                act.activation(stat[:, 4 + t:5 + t], stat[:, 2 + t:3 + t], ACT.Sqrt).then_inc(f_rt, 1)
            act.wait_ge(h2_ok, TT)
            for j in range(2):
                act.dma_start(gain[:, j * BLK:(j + 1) * BLK],
                              final_norm_g[j * BLK:(j + 1) * BLK].partition_broadcast(P)).then_inc(final_in, 16)
            for j in range(4):
                act.wait_ge(h2T_ps, j + 1)
                t, a = j // 2, (j % 2) * 4
                act.copy(h2T[:, a:a + 4, t * P:(t + 1) * P], B[4 + j][:, :].rearrange("p (c t) -> p c t", c=4)).then_inc(h2T_ok, 1)
            act.wait_ge(lg_mx, 1)
            for t in range(TT):
                ex = act.activation(r_b[:, t, :], lg[:, t, :], ACT.Exp, bias=r_s[:, t, 0:1])
            ex.then_inc(lg_ex, 1)
            act.wait_ge(gT_ps, 1)
            act.copy(gateT, B[2][0:EXPERTS, 0:TOKENS]).then_inc(gT_ok, 1)
            act.wait_ge(used, SPLITS)

            def split_x(n):
                act.wait_ge(gath_ps, n)
                act.copy(xe[:, :, 0, :], PREP[:, :].rearrange("p (c s) -> p c s", c=KC)).then_inc(xh_ok, 1)

            step(act.copy(ev[:, 0, 0:1], stat[:, 0:1]))
            act.copy(ev[:, 0, 1:2], stat[:, 0:1]).then_inc(ev_ok, 2)
            split_x(1)
            act.wait_ge(n_ok, 1)
            items = act.value_load(n_items[0:1, 0:1], min_val=EXPERTS, max_val=EXPERTS * CHUNKS)

            def evac(u, i, back=0):
                act.wait_ge(used, PIECES * i + (SPLITS + pieces_until(u) - PIECES * back))
                if u < 4:
                    act.wait_ge(ev_used, UNITS * i + (u + 1))
                act.copy(ev[:, u % 2, :], MM[u % 2][:, :]).then_inc(ev_ok, 1)

            def item(i, first):
                def high(p):
                    if p % 2 == 0:
                        landed_expert(act, i, p // 2)
                    act.wait_ge(used, PIECES * i + (p + 1))
                    act.copy(hi[:, p % SPLITS, :, :], piece_of(p)).then_inc(hi_ok, 1)

                def sigmoid(half):
                    act.wait_ge(glu_ok, 2 * i + (half + 1))
                    act.activation(sig[:, :, :], glu[:, :, :], ACT.Sigmoid, scale=ALPHA).then_inc(sig2_ok, 1)

                def high_act(half):
                    act.wait_ge(actv_ok, 2 * i + (half + 1))
                    act.copy(ae[:, 4 * half:4 * half + 4, 0, :], actv[:, :, :]).then_inc(ah_ok, 1)

                high(0)
                if not first:
                    evac(4, i, 1)
                high(1)
                if not first:
                    evac(5, i, 1)
                high(2)
                high(3)
                evac(0, i)
                high(4)
                act.wait_ge(sc_ps, i + 1)
                act.copy(scat[:, :], PREP[:, 0:TOKENS]).then_inc(sc_ok, 1)
                high(5)
                evac(1, i)
                high(6)
                high(7)
                evac(2, i)
                sigmoid(0)
                high(8)
                high_act(0)
                high(9)
                evac(3, i)
                high(10)
                sigmoid(1)
                high(11)
                high_act(1)
                split_x(i + 2)

            item(0, True)
            with act.Fori(1, items) as i:
                item(i, False)
            evac(4, items, 1)
            evac(5, items, 1)
            for t in range(TT):
                act.wait_ge(y_ok, 2 * t + 2)
                act.activation(h2[:, t, :], xs[:, t, :], ACT.Square, accum_out=stat[:, t:t + 1]).then_inc(y_sq, 1)
                act.wait_ge(y_ms, t + 1)
                act.activation(stat[:, 4 + t:5 + t], stat[:, 2 + t:3 + t], ACT.Sqrt).then_inc(y_rt, 1)

        @block.vector
        def _(dve):
            step = stepper(dve, dve_step)

            def rotate(view, heads, half, every, temps, step, eng):
                ta, tb = (x[:, :, 0:heads, 0:2 * half] for x in temps)
                shape = [P, TT, heads, half]
                cos = trig[:, 0, :, 0:16:every].unsqueeze(2).to_broadcast(shape)
                sin = trig[:, 1, :, 0:16:every].unsqueeze(2).to_broadcast(shape)
                neg = nsin[:, :, 0:16:every].unsqueeze(2).to_broadcast(shape)
                x1, x2 = view[:, :, :, 0:half], view[:, :, :, half:2 * half]
                eng.tensor_tensor(ta[:, :, :, 0:half], x1, cos, ALU.mult)
                eng.tensor_tensor(ta[:, :, :, half:2 * half], x2, cos, ALU.mult)
                eng.tensor_tensor(tb[:, :, :, 0:half], x2, neg, ALU.mult)
                step(eng.tensor_tensor(tb[:, :, :, half:2 * half], x1, sin, ALU.mult))
                return eng.tensor_tensor(view, ta, tb, ALU.add)

            dve.wait_ge(x_sq, 1)
            dve.tensor_scalar(stat[:, 2:4], stat[:, 0:2], 1.0 / D, EPS, ALU.mult, ALU.add).then_inc(x_ms, 1)
            dve.wait_ge(x_rt, 1)
            step(dve.reciprocal(stat[:, 0:2], stat[:, 4:6]))
            dve.wait_ge(cst_in, 16)
            for t in range(TT):
                dve.tensor_scalar(diag[:, t, :], ident, stat[:, t:t + 1], None, ALU.mult).then_inc(diag_ok, 1)
            dve.wait_ge(rstd_ps, 1)
            dve.wait_ge(early_in, 48)
            step(dve.tensor_copy(rstd_row[:, :], B[6][:, 0:TOKENS]))
            for c in range(KC):
                dve.wait_ge(xT_ps, c + 1)
                a = (c % 2) * TOKENS
                dve.scalar_tensor_tensor(out=hT[:, c, :], in0=B[2 + c // 2][:, a:a + TOKENS], scalar=g_in[:, c:c + 1],
                                         in1=rstd_row[:, :], op0=ALU.mult, op1=ALU.mult).then_inc(hT_ok, 1)
            dve.wait_ge(early_in, 48)
            step(dve.tensor_copy(pos_f[:, :], pos_i[:, :]))
            for t in range(TT):
                dve.tensor_scalar(ang[:, 1, t, :], const("invfreq"), pos_f[:, t:t + 1], None, ALU.mult)
                last = dve.tensor_scalar(ang[:, 0, t, :], const("invfreq"), pos_f[:, t:t + 1], None, ALU.mult)
            step(last)
            magic = float(1.5 * 2 ** 23)
            dve.tensor_scalar(turns[:, 1], ang[:, 1], 1.0 / (2 * np.pi), None, ALU.mult)
            step(dve.tensor_scalar(turns[:, 0], ang[:, 0], 1.0 / (2 * np.pi), 0.25, ALU.mult, ALU.add))
            step(dve.tensor_scalar(turns[:], turns[:], magic, None, ALU.add))
            step(dve.tensor_scalar(turns[:], turns[:], magic, None, ALU.subtract))
            rest = 2 * np.pi
            for _ in range(3):
                part = float((np.float32(rest).view(np.uint32) & np.uint32(0xFFFFF000)).view(np.float32))
                rest -= part
                step(dve.scalar_tensor_tensor(out=ang[:], in0=turns[:], scalar=-part, in1=ang[:], op0=ALU.mult, op1=ALU.add))
            step(dve.tensor_scalar(ang[:, 0], ang[:, 0], float(np.pi / 2), None, ALU.add))
            dve.tensor_scalar(ang[:], ang[:], 3.1415925, -3.1415925, ALU.min, ALU.max).then_inc(ang_ok, 1)

            dve.wait_ge(trig_ok, 1)
            dve.tensor_scalar(nsin[:, :, :], trig[:, 1], -1.0, None, ALU.mult).then_inc(nsin_ok, 1)
            dve.wait_ge(nsin_ok, 1)
            dve.wait_ge(z_ok, 2)
            step(rotate(z_qi[:, :, :].rearrange("p t (h d) -> p t h d", h=HEADS)[:, :, :, 0:ROT], HEADS, ROT // 2, 2, (ropa, ropb), step, dve))
            dve.wait_ge(z_ok, 4)
            step(rotate(z_kv[:, :, 2 * HD:3 * HD].unsqueeze(2)[:, :, :, 0:ROT], 1, ROT // 2, 2, (ropa, ropb), step, dve))
            step(dve.tensor_scalar(w_idx[:, :, :], z_kv[:, :, 3 * HD:3 * HD + HEADS], HEADS ** -0.5, None, ALU.mult))
            dve.tensor_copy(kk[:, :, :, :], z_kv[:, :, 2 * HD:3 * HD].unsqueeze(2).to_broadcast([P, TT, 2, HD])).then_inc(qi_rot, 1)
            dve.wait_ge(bgu_ps, 1)
            dve.tensor_copy(bias_gu[:, :, :], B[7][:, :].rearrange("p (j e) -> p e j", e=EXPERTS)).then_inc(bgu_ok, 1)
            for b in range(6):
                t, heads = BATCHES[b]
                w = P * (t + 1)
                dve.wait_ge(idx_rl, b + 1)
                for m, h in enumerate(heads):
                    src = prob[:, b % 2, m * w:(m + 1) * w]
                    if h == 0:
                        ins = dve.tensor_scalar(score[:, t, 0:w], src, w_idx[:, t, h:h + 1], None, ALU.mult)
                    else:
                        ins = dve.scalar_tensor_tensor(out=score[:, t, 0:w], in0=src, scalar=w_idx[:, t, h:h + 1],
                                                       in1=score[:, t, 0:w], op0=ALU.mult, op1=ALU.add)
                    if m < len(heads) - 1:
                        step(ins)
                ins.then_inc(idx_ac, 1)
                dve.wait_ge(idx_ac, b + 1)
            for t in range(TT):
                last = dve.tensor_tensor(score[:, t, t * P:(t + 1) * P], score[:, t, t * P:(t + 1) * P], const("causal"), ALU.add)
            step(last)

            def topk():
                for t in range(TT):
                    w = P * (t + 1)
                    sc, wk = score[:, t, 0:w], work[:, t, 0:w]
                    for r in range(TOPK // 8):
                        step(dve.max(top8[:, t, :], sc if r == 0 else wk))
                        if r < TOPK // 8 - 1:
                            step(dve.match_replace(wk, top8[:, t, :], sc if r == 0 else wk, REMOVED))
                        if r % 3 == 2:
                            yield
                    over, same, count = (pick[:, j, 0:w] for j in range(3))
                    thr = top8[:, t, 7:8]
                    dve.tensor_scalar(over, sc, thr, 0.0, ALU.is_gt, ALU.add, accum_out=cnt[:, t:t + 1])
                    step(dve.tensor_scalar(same, sc, thr, None, ALU.is_equal))
                    dve.tensor_tensor_scan(count, same, same, 0.0, ALU.add, ALU.max)
                    step(dve.tensor_scalar(cnt[:, t:t + 1], cnt[:, t:t + 1], -1.0, float(TOPK), ALU.mult, ALU.add))
                    step(dve.scalar_tensor_tensor(out=same, in0=count, scalar=cnt[:, t:t + 1], in1=same, op0=ALU.is_le, op1=ALU.mult))
                    step(dve.tensor_tensor(over, over, same, ALU.add))
                    step(dve.tensor_scalar(allow[:, t, 0:w], over, -1.0, -NEG, ALU.add, ALU.mult))
                    step(dve.tensor_tensor(allow[:, t, t * P:(t + 1) * P], allow[:, t, t * P:(t + 1) * P], const("causal"), ALU.add))
                    yield

            dve.wait_ge(c_sq, 1)
            step(dve.tensor_scalar(stat[:, 7:9], stat[:, 7:9], 1.0 / Q_LORA, EPS, ALU.mult, ALU.add))
            dve.tensor_scalar(stat[:, 9:11], stat[:, 9:11], 1.0 / KV_LORA, EPS, ALU.mult, ALU.add).then_inc(c_ms, 1)
            for c in range(2):
                dve.wait_ge(c_ps, 1)
                last = dve.tensor_scalar(c_qT[:, c, :], TB[0][:, c * TOKENS:(c + 1) * TOKENS], g_q[:, c:c + 1], None, ALU.mult)
            last.then_inc(c_ok, 1)
            dve.wait_ge(c_ps, 2)
            dve.tensor_scalar(c_kvT[:, :], TB[1][:, 0:TOKENS], g_kv[:, 0:1], None, ALU.mult).then_inc(c_ok, 1)
            dve.wait_ge(c_rt, 1)
            dve.reciprocal(stat[:, 11:15], stat[:, 7:11]).then_inc(c_rs, 1)
            dve.wait_ge(c_rs, 1)
            parts = topk()
            for _ in range(3):
                next(parts)
            for t in range(TT):
                dve.wait_ge(up_ps, 2 * t + 2)
                dve.wait_ge(up_a, 4 * t + 4)
                for j in range(2):
                    src = VB[j][:, :].rearrange("p (h d) -> p h d", h=4)
                    dve.tensor_scalar(v_ml[:, t, 4 * j:4 * j + 4, :], src[:, :, NOPE:NOPE + V_DIM],
                                      stat[:, 13 + t:14 + t], None, ALU.mult).then_inc(up_d, 1)
            for j in range(4):
                dve.wait_ge(mT_ps, 2 * j + 2)
                dve.tensor_copy(kmT[:, 2 * j:2 * j + 2, :].rearrange("p h t -> p (h t)"), TB[1][0:QK, :]).then_inc(mk_ok, 1)

            def masked(b):
                t, heads = BATCHES[b % 6]
                w, n = P * (t + 1), len(heads)
                scale = (QK if b < 6 else HD) ** -0.5
                src = SB[b % 2][:, :].rearrange("p (h k) -> p h k", h=n)
                pr = prob[:, b % 2, :].rearrange("p (h k) -> p h k", h=n)
                dve.wait_ge(s_ps, b + 1)
                if b >= 2:
                    dve.wait_ge(pT_ps, b - 1)
                if b >= 6:
                    mask = allow[:, t, 0:w].unsqueeze(1).to_broadcast([P, n, w])
                    step(dve.scalar_tensor_tensor(out=pr, in0=src, scalar=scale, in1=mask, op0=ALU.mult, op1=ALU.add))
                else:
                    if t:
                        dve.tensor_scalar(pr[:, :, 0:P], src[:, :, 0:P], scale, None, ALU.mult)
                    mask = const("causal").unsqueeze(1).to_broadcast([P, n, P])
                    step(dve.scalar_tensor_tensor(out=pr[:, :, t * P:w], in0=src[:, :, t * P:w], scalar=scale, in1=mask,
                                                  op0=ALU.mult, op1=ALU.add))
                step(dve.tensor_reduce(mx[:, b % 2, 0:n], pr, AXX, ALU.max))
                dve.tensor_scalar(mx[:, b % 2, 0:n], mx[:, b % 2, 0:n], -1.0, None, ALU.mult).then_inc(s_mx, 1)

            def normalised(b):
                t, heads = BATCHES[b % 6]
                w, n = P * (t + 1), len(heads)
                pr = prob[:, b % 2, :].rearrange("p (h k) -> p h k", h=n)
                dve.wait_ge(p_ex, b + 1)
                step(dve.reciprocal(den[:, b % 2, 0:n], den[:, b % 2, 0:n]))
                dve.tensor_tensor(pr, pr, den[:, b % 2, 0:n].unsqueeze(2).to_broadcast([P, n, w]), ALU.mult).then_inc(p_ok, 1)

            masked(0)
            for b in range(12):
                if b == 5:
                    for _ in parts:
                        pass
                if b < 11:
                    masked(b + 1)
                normalised(b)
                next(parts, None)
            for mc in range(KC):
                dve.wait_ge(br_ps, mc + 1)
                dve.wait_ge(sig_ok, mc // 2 + 1)
                sg = sgT[:, mc, :, :].rearrange("p a t -> p (a t)")
                dve.tensor_tensor(sg, sg, SB[mc % 2][:, :], ALU.mult).then_inc(br_ok, 1)
                dve.wait_ge(br_ok, 2 * mc + 1)
                dve.tensor_tensor(mT[:, mc, :], sg[:, 0:TOKENS], sg[:, TOKENS:2 * TOKENS], ALU.add).then_inc(br_ok, 1)
            for t in range(TT):
                for n in range(2):
                    dve.wait_ge(wo_ps, 2 * t + n + 1)
                    at = slice(n * BLK, (n + 1) * BLK)
                    dve.tensor_tensor(xs[:, t, at], xs[:, t, at], B[2 * t + n][:, :], ALU.add).then_inc(x1_ok, 1)
                dve.wait_ge(gain_in, 32)
                dve.wait_ge(f_sq, t + 1)
                dve.tensor_scalar(stat[:, 2 + t:3 + t], stat[:, t:t + 1], 1.0 / D, EPS, ALU.mult, ALU.add).then_inc(f_ms, 1)
                dve.wait_ge(f_rt, t + 1)
                step(dve.reciprocal(stat[:, t:t + 1], stat[:, 4 + t:5 + t]))
                dve.scalar_tensor_tensor(out=h2[:, t, :], in0=xs[:, t, :], scalar=stat[:, t:t + 1], in1=gain[:, :],
                                         op0=ALU.mult, op1=ALU.mult).then_inc(h2_ok, 1)
            dve.wait_ge(lg_ps, TT)
            for t in range(TT):
                step(dve.tensor_tensor(lg[:, t, :], B[0][:, t * EXPERTS:(t + 1) * EXPERTS], rb[:, :], ALU.add))
                step(dve.max(top8[:, t, :], lg[:, t, :]))
            for t in range(TT):
                last = dve.tensor_scalar(r_s[:, t, 0:1], top8[:, t, 0:1], -1.0, None, ALU.mult)
            last.then_inc(lg_mx, 1)
            for t in range(TT):
                thr = top8[:, t, EXP_K - 1:EXP_K]
                dve.tensor_scalar(sel[:, t, :], lg[:, t, :], thr, 0.0, ALU.is_gt, ALU.add, accum_out=r_s[:, t, 1:2])
                step(dve.tensor_scalar(r_a[:, t, :], lg[:, t, :], thr, None, ALU.is_equal))
                dve.tensor_tensor_scan(pm[:, t, :], r_a[:, t, :], r_a[:, t, :], 0.0, ALU.add, ALU.max)
                step(dve.tensor_scalar(r_s[:, t, 1:2], r_s[:, t, 1:2], -1.0, float(EXP_K), ALU.mult, ALU.add))
                step(dve.scalar_tensor_tensor(out=r_a[:, t, :], in0=pm[:, t, :], scalar=r_s[:, t, 1:2], in1=r_a[:, t, :],
                                              op0=ALU.is_le, op1=ALU.mult))
            dve.tensor_tensor(sel[:, :, :], sel[:, :, :], r_a[:, :, :], ALU.add).then_inc(sel_ok, 1)
            dve.wait_ge(sel_ok, 1)
            dve.wait_ge(lg_ex, 1)
            step(dve.tensor_tensor(r_b[:, :, :], r_b[:, :, :], sel[:, :, :], ALU.mult))
            step(dve.tensor_reduce(r_s[:, :, 2:3], r_b[:, :, :], AXX, ALU.add))
            step(dve.reciprocal(r_s[:, :, 3:4], r_s[:, :, 2:3]))
            dve.tensor_tensor(gate[:, :, :], r_b[:, :, :], r_s[:, :, 3:4].to_broadcast([P, TT, EXPERTS]), ALU.mult).then_inc(gate_ok, 1)
            dve.wait_ge(gate_ok, 1)
            dve.tensor_copy(gates[:, :, :].rearrange("p t (c e) -> p t c e", e=EXPERTS),
                            gate[:, :, :].unsqueeze(2).to_broadcast([P, TT, CHUNKS + 1, EXPERTS]))
            dve.wait_ge(pos_ps, 1)
            step(dve.scalar_tensor_tensor(out=pm[:, :, :], in0=B[7][:, 0:64].rearrange("p (t e) -> p t e", t=TT), scalar=1.0,
                                          in1=sel[:, :, :], op0=ALU.add, op1=ALU.mult))
            for c in range(CHUNKS + 1):
                last = dve.tensor_scalar(posc[:, :, c * EXPERTS:(c + 1) * EXPERTS], pm[:, :, :], -1.0 - SLOTS * c, None, ALU.add)
            step(last)
            step(dve.tensor_reduce(r_s[:, 0, 0:1], B[7][:, 64:96], AXX, ALU.max))
            for c in range(1, CHUNKS):
                last = dve.tensor_scalar(r_s[:, 0, c:c + 1], r_s[:, 0, 0:1], float(SLOTS * c), float(EXPERTS), ALU.is_gt, ALU.mult)
            step(last)
            step(dve.tensor_reduce(r_s[:, 0, 0:1], r_s[:, 0, 1:4], AXX, ALU.add))
            dve.tensor_scalar(n_items[:, :], r_s[:, 0, 0:1], float(EXPERTS), None, ALU.add).then_inc(n_ok, 1)

            def prepare(i):
                for t in range(TT):
                    dve.tensor_scalar(onehot[:, t, :], const("slot")[:, 0:SLOTS], posc[:, t, bass.ds(i, 1)], None, ALU.is_equal)
                    last = dve.tensor_scalar(gated[:, t, :], const("slot"), posc[:, t, bass.ds(i, 1)],
                                             gates[:, t, bass.ds(i, 1)], ALU.is_equal, ALU.mult)
                last.then_inc(prep_ok, 1)

            def split_x(n):
                dve.wait_ge(xh_ok, n)
                dve.tensor_tensor(xe[:, :, 1, :], PREP[:, :].rearrange("p (c s) -> p c s", c=KC),
                                  xe[:, :, 0, :].bitcast(F32), ALU.subtract).then_inc(xl_ok, 1)

            dve.wait_ge(used, SPLITS)
            dve.wait_ge(n_ok, 1)
            step(dve.memset(gub[:, 0, 0, 0:1], 0.0))
            dve.memset(gub[:, 0, 0, 1:2], 0.0).then_inc(gub_ok, 1)
            prepare(0)
            split_x(1)
            items = dve.value_load(n_items[0:1, 0:1], min_val=EXPERTS, max_val=EXPERTS * CHUNKS)

            def item(i):
                e = i % EXPERTS if isinstance(i, int) else dve.snap(i % EXPERTS)

                def low(p):
                    dve.wait_ge(hi_ok, PIECES * i + (p + 1))
                    dve.tensor_tensor(lo[:, p % SPLITS, :, :], piece_of(p), hi[:, p % SPLITS, :, :].bitcast(F32),
                                      ALU.subtract).then_inc(lo_ok, 1)

                def add_bias(half):
                    dve.wait_ge(ev_used, UNITS * i + (2 + 2 * half + 2))
                    dve.tensor_tensor(gub[:, :, :, :].rearrange("p a c s -> p (a c) s"),
                                      GUT[:, :].rearrange("p (j s) -> p j s", s=SLOTS),
                                      bias_gu[:, bass.ds(e, 1), 8 * half:8 * half + 8].rearrange("p a j -> p (a j)")
                                      .unsqueeze(2).to_broadcast([P, 8, SLOTS]), ALU.add).then_inc(gub_ok, 1)
                    dve.wait_ge(gub_ok, 2 * i + (1 + half + 1))
                    dve.tensor_scalar(glu[:, :, :], gub[:, 0], LIMIT, None, ALU.min).then_inc(glu_ok, 1)
                    dve.tensor_scalar(lin[:, :, :], gub[:, 1], LIMIT, -LIMIT, ALU.min, ALU.max).then_inc(lin_ok, 1)

                def product(half):
                    dve.wait_ge(lin_ok, 2 * i + (half + 1))
                    dve.scalar_tensor_tensor(out=prod[:, :, :], in0=lin[:, :, :], scalar=1.0, in1=glu[:, :, :],
                                             op0=ALU.add, op1=ALU.mult).then_inc(prod_ok, 1)

                def low_act(half):
                    dve.wait_ge(ah_ok, 2 * i + (half + 1))
                    dve.tensor_tensor(ae[:, 4 * half:4 * half + 4, 1, :], actv[:, :, :],
                                      ae[:, 4 * half:4 * half + 4, 0, :].bitcast(F32), ALU.subtract).then_inc(al_ok, 1)

                for p in range(5):
                    low(p)
                dve.wait_ge(sc_ok, i + 1)
                prepare(i + 1)
                low(5)
                low(6)
                add_bias(0)
                product(0)
                low(7)
                low_act(0)
                low(8)
                low(9)
                add_bias(1)
                product(1)
                low(10)
                low_act(1)
                low(11)
                split_x(i + 2)

            item(0)
            with dve.Fori(1, items) as i:
                item(i)
            dve.wait_ge(final_in, 32)
            dve.wait_ge(ev_used, UNITS * items + 2)
            for t in range(TT):
                for n in range(2):
                    at = slice(n * BLK, (n + 1) * BLK)
                    dve.tensor_tensor(xs[:, t, at], xs[:, t, at], ACC[2 * t + n][:, :], ALU.add).then_inc(y_ok, 1)
                dve.wait_ge(y_sq, t + 1)
                dve.tensor_scalar(stat[:, 2 + t:3 + t], stat[:, t:t + 1], 1.0 / D, EPS, ALU.mult, ALU.add).then_inc(y_ms, 1)
                dve.wait_ge(y_rt, t + 1)
                dve.reciprocal(stat[:, t:t + 1], stat[:, 4 + t:5 + t]).then_inc(fin_r, 1)
                dve.wait_ge(fin_r, t + 1)
                dve.scalar_tensor_tensor(out=xs[:, t, :], in0=xs[:, t, :], scalar=stat[:, t:t + 1], in1=gain[:, :],
                                         op0=ALU.mult, op1=ALU.mult).then_inc(o_ok, 1)

        @block.gpsimd
        def _(pool):
            step = stepper(pool, pool_step)

            def rotate(view, heads, half, every):
                ta, tb = (x[:, :, 0:heads, 0:2 * half] for x in (ropc, ropd))
                shape = [P, TT, heads, half]
                cos = trig[:, 0, :, 0:16:every].unsqueeze(2).to_broadcast(shape)
                sin = trig[:, 1, :, 0:16:every].unsqueeze(2).to_broadcast(shape)
                neg = nsin[:, :, 0:16:every].unsqueeze(2).to_broadcast(shape)
                x1, x2 = view[:, :, :, 0:half], view[:, :, :, half:2 * half]
                pool.tensor_tensor(ta[:, :, :, 0:half], x1, cos, ALU.mult)
                pool.tensor_tensor(ta[:, :, :, half:2 * half], x2, cos, ALU.mult)
                pool.tensor_tensor(tb[:, :, :, 0:half], x2, neg, ALU.mult)
                step(pool.tensor_tensor(tb[:, :, :, half:2 * half], x1, sin, ALU.mult))
                return pool.tensor_tensor(view, ta, tb, ALU.add)

            pool.wait_ge(nsin_ok, 1)
            pool.wait_ge(z_ok, 6)
            step(rotate(z_qb[:, :, :].rearrange("p t (h d) -> p t h d", h=HEADS)[:, :, :, 0:ROT], HEADS, ROT // 2, 2))
            step(rotate(z_kv[:, :, 0:HD].unsqueeze(2)[:, :, :, 0:ROT], 1, ROT // 2, 2))
            pool.wait_ge(qi_ps, 3)
            for t in range(TT):
                last = pool.tensor_copy(kk[:, t, :, :], z_kv[:, t, 0:HD].unsqueeze(1).to_broadcast([P, 2, HD]))
            last.then_inc(qb_rot, 1)
            pool.wait_ge(z_ok, 8)
            pool.wait_ge(c_sq, 1)
            pool.wait_ge(idx_ac, 6)
            step(rotate(z_ml[:, :, Q_LORA + KV_LORA:C_QB].unsqueeze(2), 1, ROPE // 2, 1))
            for t in range(TT):
                last = pool.tensor_copy(k_ml[:, t, :, NOPE:QK],
                                        z_ml[:, t, Q_LORA + KV_LORA:C_QB].unsqueeze(1).to_broadcast([P, HEADS, ROPE]))
            step(last)
            pool.wait_ge(up_a, 8)
            rotate(q_ml[:, :, :, NOPE:QK], HEADS, ROPE // 2, 1).then_inc(ml_rot, 1)

            pool.wait_ge(n_ok, 1)
            items = pool.value_load(n_items[0:1, 0:1], min_val=EXPERTS, max_val=EXPERTS * CHUNKS)
            with pool.Fori(0, items) as i:
                for half in range(2):
                    pool.wait_ge(prod_ok, 2 * i + (half + 1))
                    pool.wait_ge(sig2_ok, 2 * i + (half + 1))
                    pool.tensor_tensor(actv[:, :, :], prod[:, :, :], sig[:, :, :], ALU.mult).then_inc(actv_ok, 1)


_INS = ['x', 'positions', 'attn_norm_g', 'w_in', 'mla_q_norm_g', 'mla_w_uq', 'mla_kv_norm_g', 'mla_w_ukv',
        'w_branch_mla', 'w_branch_dsa', 'w_out', 'ffn_norm_g', 'router_w', 'router_b',
        'w_gate_up', 'b_gate_up', 'w_down', 'b_down', 'final_norm_g']


def kernel(**inputs):
    import concourse.bacc as _bacc
    from concourse.bass_utils import run_bass_kernel_spmd as _run

    nc = _bacc.Bacc("TRN2", target_bir_lowering=False, num_devices=1)
    arrays, args = {}, []
    for name in _INS + ['consts']:
        a = constants() if name == 'consts' else np.ascontiguousarray(inputs[name])
        arrays[f"in_{name}"] = a
        args.append(nc.dram_tensor(f"in_{name}", a.shape, mybir.dt.from_np(a.dtype), kind="ExternalInput").ap())
    args.append(nc.dram_tensor("out_y", (1, TOKENS, D), F32, kind="ExternalOutput").ap())
    build(nc, *args)
    r = _run(nc, [arrays], core_ids=[0])
    return r.results[0]["out_y"]
```

```python
from contextlib import ExitStack

import numpy as np

import concourse.bass as bass
from concourse import mybir

ALU = mybir.AluOpType
ACT = mybir.ActivationFunctionType
AXX = mybir.AxisListType.X
F32 = mybir.dt.float32
F32R = mybir.dt.float32r
I32 = mybir.dt.int32

P = 128
TOKENS, D = 256, 1024
TT = TOKENS // P
EPS = 1e-6
THETA = 500000.0
NEG = -1.0e30
REMOVED = -3.0e38

HEADS = 8
Q_LORA, KV_LORA, NOPE, ROPE, V_DIM = 256, 128, 64, 32, 64
QK = NOPE + ROPE
HD, ROT = 64, 16
TOPK = min(256, TOKENS // 4)
GATES_AT = Q_LORA + KV_LORA + ROPE + 2 * HEADS * HD + 3 * HD + HEADS
D_IN = GATES_AT + 2 * D
C_QB = Q_LORA + KV_LORA + ROPE
C_KB = C_QB + HEADS * HD
C_QI = C_KB + 2 * HD
C_KI = C_QI + HEADS * HD

EXPERTS, EXP_K, FF = 32, 4, 1024
LIMIT, ALPHA = 7.0, 1.702
SLOTS = 64
CHUNKS = TOKENS // SLOTS
TABLE = EXPERTS * (CHUNKS + 1)

KC = D // P
BLK = 512
UNIT = KC * BLK
RING = 6
FRONT_UNITS = 13
UNITS = 6
PIECES = 2 * UNITS
SPLITS = 4
GU_COLS = [0, FF, BLK, FF + BLK]

Z_UNITS = [[(C_KB, 128), (C_KI, HD + HEADS)], [(C_QI, 512)], [(C_QB, 512)], [(0, C_QB)]]

BATCHES = [(0, (0, 2, 4, 6)), (0, (1, 3, 5, 7)),
           (1, (0, 2)), (1, (1, 3)), (1, (4, 6)), (1, (5, 7))]

WARM = (4, 10, 6, 4)

GATES_IDX = (3,)
GATES_ATT = (0, 1, 2, 3, 4, 5, 6, 7, 8, 9, 10)

CONST = {"ident": P, "ident2": SLOTS, "before": P, "ones": P, "slot": P, "causal": P, "invfreq": ROPE // 2}
CONST_AT = {}
for _name, _n in CONST.items():
    CONST_AT[_name] = sum(CONST[k] for k in CONST_AT)


def constants():
    r = np.arange(P)
    part = {
        "ident": np.eye(P),
        "ident2": (r[:, None] % SLOTS == np.arange(SLOTS)[None, :]),
        "before": (r[:, None] < r[None, :]),
        "ones": np.ones((P, P)),
        "slot": np.broadcast_to(r[None, :] % SLOTS, (P, P)),
        "causal": np.where(r[None, :] <= r[:, None], 0.0, NEG),
        "invfreq": np.broadcast_to(
            (np.float32(THETA) ** (-np.arange(ROPE // 2, dtype=np.float32) / np.float32(ROPE // 2))), (P, ROPE // 2)),
    }
    return np.concatenate([part[k].astype(np.float32) for k in CONST], axis=1)


def build(nc, x, positions, attn_norm_g, w_in, mla_q_norm_g, mla_w_uq, mla_kv_norm_g, mla_w_ukv,
          w_branch_mla, w_branch_dsa, w_out, ffn_norm_g, router_w, router_b,
          w_gate_up, b_gate_up, w_down, b_down, final_norm_g, consts, out):
    ctx = ExitStack()
    front = ExitStack()
    with ctx:
        def sb(name, shape, dt=F32, scope=ctx):
            return scope.enter_context(nc.sbuf_tensor(name, shape, dt))

        def sem(name):
            return ctx.enter_context(nc.semaphore(name))

        cst = sb("cst", [P, sum(CONST.values())])
        xs = sb("x_res", [P, TT, D])
        gain = sb("gain", [P, D])
        bias_gu = sb("bias_gu", [P, EXPERTS, 16])
        raw = sb("raw", [P, RING, UNIT])
        stat = sb("stat", [P, 16])
        posc = sb("posc", [P, TT, TABLE])
        gates = sb("gates", [P, TT, TABLE])
        h2 = sb("h2", [P, TT, D])
        n_items = sb("n_items", [P, 1], I32)
        gateT = sb("gateT", [EXPERTS, TOKENS])
        bd = gain[0:EXPERTS, :]

        def fb(name, shape, dt=F32):
            return sb(name, shape, dt, front)

        area_k = fb("area_k", [P, HEADS * TOKENS])
        z_qi = area_k[:, 0:4 * TOKENS].rearrange("p (t n) -> p t n", t=TT)
        dsaT = area_k[:, 0:4 * TOKENS].rearrange("p (j t) -> p j t", j=4)
        c_qT = area_k[:, 4 * TOKENS:6 * TOKENS].rearrange("p (c t) -> p c t", c=2)
        c_kvT = area_k[:, 6 * TOKENS:7 * TOKENS]
        diag = area_k[:, 7 * TOKENS:8 * TOKENS].rearrange("p (t n) -> p t n", t=TT)
        kmT = area_k[0:QK, :].rearrange("p (h t) -> p h t", h=HEADS)
        area_p = fb("area_p", [P, 4 * BLK])
        prob = area_p[:, 0:2 * BLK].rearrange("p (b n) -> p b n", b=2)
        probT = area_p[:, 2 * BLK:4 * BLK].rearrange("p (b n) -> p b n", b=2)
        k_ml = area_p[:, 0:TT * HEADS * QK].rearrange("p (t h d) -> p t h d", t=TT, h=HEADS)
        q_ml = fb("q_ml", [P, TT, HEADS, QK])
        q_ml_flat = q_ml[:, :, :, :].rearrange("p t h d -> p (t h d)")
        mlaT = q_ml_flat[:, 0:4 * TOKENS].rearrange("p (j t) -> p j t", j=4)
        v_ml = fb("v_ml", [P, TT, HEADS, V_DIM])
        z_kv = fb("z_kv", [P, TT, 200])
        z_qb = fb("z_qb", [P, TT, 512])
        qT = fb("qT", [P, 4, TOKENS])
        kT = fb("kT", [P, TOKENS])
        kk = fb("kk", [P, TT, 2, HD])
        score = fb("score", [P, TT, TOKENS])
        work = fb("work", [P, TT, TOKENS])
        pick = fb("pick", [P, 3, TOKENS])
        allow = fb("allow", [P, TT, TOKENS])
        ropa = fb("ropa", [P, TT, HEADS, ROT])
        ropb = fb("ropb", [P, TT, HEADS, ROT])
        ropc = fb("ropc", [P, TT, HEADS, ROPE])
        ropd = fb("ropd", [P, TT, HEADS, ROPE])
        z_ml = fb("z_ml", [P, TT, C_QB])
        rstd_row = fb("rstd_row", [P, TOKENS])
        sgT = fb("sgT", [P, KC, 2, TOKENS])
        hT = fb("hT", [P, KC, TOKENS])
        bgu = h2[0:EXPERTS, :, :].rearrange("p t n -> p (t n)")
        qmT = h2[0:QK, :, :].rearrange("p t n -> p (t n)").rearrange("p (h t) -> p h t", h=HEADS)
        g_in = fb("g_in", [P, KC])
        g_ffn = fb("g_ffn", [P, KC])
        g_q = fb("g_q", [P, 2])
        g_kv = fb("g_kv", [P, 1])
        pos_i = fb("pos_i", [P, TT], I32)
        pos_f = fb("pos_f", [P, TT])
        ang = fb("ang", [P, 2, TT, 16])
        turns = fb("turns", [P, 2, TT, 16])
        trig = fb("trig", [P, 2, TT, 16])
        nsin = fb("nsin", [P, TT, 16])
        w_idx = fb("w_idx", [P, TT, HEADS])
        top8 = fb("top8", [P, TT, 8])
        cnt = fb("cnt", [P, TT])
        mx = fb("mx", [P, 2, 4])
        den = fb("den", [P, 2, 4])
        rw = fb("rw", [P, KC, EXPERTS])
        rb = fb("rb", [P, EXPERTS])
        at_r = 4288 // 4
        lg, r_a, r_b, sel, gate, pm = (
            hT[:, :, :].rearrange("p c n -> p (c n)")[:, at_r + k * TT * EXPERTS:at_r + (k + 1) * TT * EXPERTS]
            .rearrange("p (t e) -> p t e", t=TT) for k in range(6))
        r_s = fb("r_s", [P, TT, 4])
        front.close()

        hi = sb("w_hi", [P, SPLITS, 4, BLK], F32R)
        lo = sb("w_lo", [P, SPLITS, 4, BLK], F32R)
        xe = sb("x_split", [P, KC, 2, SLOTS], F32R)
        ae = sb("a_split", [P, KC, 2, SLOTS], F32R)
        sig = sb("sig", [P, 4, SLOTS])
        ev = sb("ev", [P, 2, BLK])
        gub = sb("gub", [P, 2, 4, SLOTS])
        onehot = sb("onehot", [P, TT, SLOTS])
        gated = sb("gated", [P, TT, P])
        scat = sb("scat", [P, TOKENS])
        glu, lin = gub[:, 0], gub[:, 1]

        B = [ctx.enter_context(nc.psum_tensor(f"bank{i}", [P, BLK], F32)) for i in range(8)]
        ZB, TB, SB, VB = B[0:2], B[2:4], B[4:6], B[6:8]
        TURN = TB + SB
        ACC, MM, PREP, GUT = B[0:4], B[4:6], B[6], B[7]

        def const(name, rows=P):
            a = CONST_AT[name]
            return cst[0:rows, a:a + CONST[name]]

        ident = const("ident")

        x_in = [sem(f"x_in{t}") for t in range(TT)]
        cst_in = sem("cst_in")
        early_in = sem("early_in")
        small_in = sem("small_in")
        SMALL = 16 * 6
        bd_in = sem("bd_in")
        sums_ok = sem("sums_ok")
        gain_in = sem("gain_in")
        final_in = sem("final_in")
        raw_in = [sem(f"raw_in{i}") for i in range(RING)]
        out_done = sem("out_done")
        act_step = sem("act_step")
        dve_step = sem("dve_step")
        pool_step = sem("pool_step")
        one_ok = sem("one_ok")
        x_sq = sem("x_sq")
        x_ms = sem("x_ms")
        x_rt = sem("x_rt")
        diag_ok = sem("diag_ok")
        xT_ps = sem("xT_ps")
        rstd_ps = sem("rstd_ps")
        hT_ok = sem("hT_ok")
        ang_ok = sem("ang_ok")
        trig_ok = sem("trig_ok")
        nsin_ok = sem("nsin_ok")
        bgu_ps = sem("bgu_ps")
        bgu_ok = sem("bgu_ok")
        z_ps = sem("z_ps")
        z_ok = sem("z_ok")
        qi_rot = sem("qi_rot")
        qi_ps = sem("qi_ps")
        qi_ok = sem("qi_ok")
        idx_ps = sem("idx_ps")
        idx_rl = sem("idx_rl")
        idx_ac = sem("idx_ac")
        c_sq = sem("c_sq")
        c_ms = sem("c_ms")
        c_rt = sem("c_rt")
        c_rs = sem("c_rs")
        c_ps = sem("c_ps")
        c_ok = sem("c_ok")
        up_ps = sem("up_ps")
        up_a = sem("up_a")
        up_d = sem("up_d")
        ml_rot = sem("ml_rot")
        qb_rot = sem("qb_rot")
        mT_ps = sem("mT_ps")
        mq_ok = sem("mq_ok")
        mk_ok = sem("mk_ok")
        g_ps = sem("g_ps")
        g_ok = sem("g_ok")
        s_ps = sem("s_ps")
        s_mx = sem("s_mx")
        p_ex = sem("p_ex")
        p_ok = sem("p_ok")
        pT_ps = sem("pT_ps")
        pT_ok = sem("pT_ok")
        pv_ps = sem("pv_ps")
        pv_ok = sem("pv_ok")
        qd_ps = sem("qd_ps")
        qd_ok = sem("qd_ok")
        sig_ok = sem("sig_ok")
        br_ps = sem("br_ps")
        br_ok = sem("br_ok")
        wo_ps = sem("wo_ps")
        x1_ok = sem("x1_ok")
        f_sq = sem("f_sq")
        f_ms = sem("f_ms")
        f_rt = sem("f_rt")
        h2_ok = sem("h2_ok")
        x1T_ps = sem("x1T_ps")
        x1T_ok = sem("x1T_ok")
        x1T_last = sem("x1T_last")
        rw_ok = sem("rw_ok")
        lg_ps = sem("lg_ps")
        lg_mx = sem("lg_mx")
        lg_ex = sem("lg_ex")
        sel_ok = sem("sel_ok")
        gate_ok = sem("gate_ok")
        pos_ps = sem("pos_ps")
        gT_ps = sem("gT_ps")
        gT_ok = sem("gT_ok")
        n_ok = sem("n_ok")
        prep_ok = sem("prep_ok")
        gath_ps = sem("gath_ps")
        xh_ok = sem("xh_ok")
        xl_ok = sem("xl_ok")
        sc_ps = sem("sc_ps")
        sc_ok = sem("sc_ok")
        hi_ok = sem("hi_ok")
        lo_ok = sem("lo_ok")
        used = sem("used")
        ev_ok = sem("ev_ok")
        ev_used = sem("ev_used")
        gub_ok = sem("gub_ok")
        glu_ok = sem("glu_ok")
        lin_ok = sem("lin_ok")
        sig2_ok = sem("sig2_ok")
        prod_ok = sem("prod_ok")
        actv_ok = sem("actv_ok")
        ah_ok = sem("ah_ok")
        al_ok = sem("al_ok")
        y_ok = sem("y_ok")
        y_sq = sem("y_sq")
        y_ms = sem("y_ms")
        y_rt = sem("y_rt")
        o_ok = sem("o_ok")
        fin_r = sem("fin_r")

        w_in_v = w_in[0].rearrange("(p c) n -> p c n", c=KC)
        w_uq_v = mla_w_uq[0].rearrange("(p c) n -> p c n", c=2)
        w_ukv_v = mla_w_ukv[0]
        w_br_v = [w[0].rearrange("(c p) n -> p c n", p=P) for w in (w_branch_mla, w_branch_dsa)]
        w_out_v = w_out[0].rearrange("(c p) n -> p c n", p=P)
        w_gu_v = w_gate_up[0].rearrange("e (c p) n -> e p c n", p=P)
        w_dn_v = w_down[0].rearrange("e (b p c) n -> e b p (c n)", b=2, c=4)

        def unit(n):
            return raw[:, n % RING, :]

        def unit3(n, cols=BLK):
            return unit(n)[:, 0:KC * cols].rearrange("p (c n) -> p c n", c=KC)

        U_UP, U_G, U_BR, U_WO = 4, 5, 9, 11
        up_q = unit(U_UP)[:, 0:2 * HEADS * QK].rearrange("p (c n) -> p c n", c=2)
        up_kv = unit(U_UP)[:, 2 * HEADS * QK:2 * HEADS * QK + HEADS * (NOPE + V_DIM)]
        br_w = [unit(U_BR + i)[:, 0:4 * D].rearrange("p (c n) -> p c n", c=4) for i in range(2)]

        EXTRA = [16 if s in (0, U_UP % RING) else 0 for s in range(RING)]

        def landed_front(eng, n):
            eng.wait_ge(raw_in[n % RING], 16 * (n // RING + 1) + EXTRA[n % RING])

        def slot_of(u):
            return (FRONT_UNITS + u) % RING

        def used_up(eng, n):
            if n < U_UP:
                eng.wait_ge(z_ps, 2 * n + 2)
            elif n == U_UP:
                eng.wait_ge(up_ps, 4)
            elif n < U_BR:
                eng.wait_ge(g_ps, 4 * (n - U_G + 1))
            elif n < U_WO:
                eng.wait_ge(br_ps, KC)
            else:
                eng.wait_ge(wo_ps, 3 + n - U_WO)

        def landed_expert(eng, i, u):
            before = 16 * len([n for n in range(FRONT_UNITS) if n % RING == slot_of(u)]) + EXTRA[slot_of(u)]
            eng.wait_ge(raw_in[slot_of(u)], 16 * i + (before + 16))

        def piece_of(p):
            a = raw[:, slot_of(p // 2), :]
            if p < 8:
                return a.rearrange("p (h c n) -> p h c n", h=2, c=4)[:, p % 2]
            return a.rearrange("p (c h n) -> p c h n", c=4, h=2)[:, :, p % 2]

        def pieces_until(u):
            return 2 * u + 2 if u < 4 else 11 + u - 4

        x1T = sgT[:, :, :, :].rearrange("p c a t -> p (c a t)")[:, KC * TOKENS:2 * KC * TOKENS].rearrange("p (c t) -> p c t", c=KC)
        mT = hT

        def stepper(eng, signal):
            n = [0]

            def step(ins):
                n[0] += 1
                ins.then_inc(signal, 1)
                eng.wait_ge(signal, n[0])
            return step

        block = ctx.enter_context(nc.Block())

        @block.sync
        def _(sp):
            sp.dma_start(cst[:, :], consts).then_inc(cst_in, 16)
            for t in range(TT):
                sp.dma_start(xs[:, t, :], x[0, t * P:(t + 1) * P, :]).then_inc(x_in[t], 16)
            sp.dma_start(g_in[:, :], attn_norm_g[0].rearrange("(p c) -> p c", c=KC)).then_inc(early_in, 16)
            for t in range(TT):
                sp.dma_start(pos_i[:, t:t + 1], positions[0, t * P:(t + 1) * P].rearrange("(p a) -> p a", a=1))\
                    .then_inc(early_in, 16)

            def load_front(n):
                if n >= RING:
                    used_up(sp, n - RING)
                done = raw_in[n % RING]
                if 0 < n < 4:
                    c0, w = Z_UNITS[n][0]
                    sp.dma_start(unit3(n, w), w_in_v[:, :, c0:c0 + w]).then_inc(done, 16)
                elif n == 0:
                    at = 0
                    for c0, w in Z_UNITS[0]:
                        sp.dma_start(unit3(0, 200)[:, :, at:at + w], w_in_v[:, :, c0:c0 + w]).then_inc(done, 16)
                        at += w
                elif n == U_UP:
                    sp.dma_start(up_kv, w_ukv_v).then_inc(done, 16)
                    sp.dma_start(up_q, w_uq_v).then_inc(done, 16)
                elif n < U_BR:
                    c0 = GATES_AT + (n - U_G) * BLK
                    sp.dma_start(unit3(n), w_in_v[:, :, c0:c0 + BLK]).then_inc(done, 16)
                elif n < U_WO:
                    sp.dma_start(br_w[n - U_BR], w_br_v[n - U_BR]).then_inc(done, 16)
                else:
                    c0 = (n - U_WO) * BLK
                    sp.dma_start(unit3(n), w_out_v[:, :, c0:c0 + BLK]).then_inc(done, 16)

            def load_expert(e, u):
                if u < 4:
                    c0 = GU_COLS[u]
                    to = raw[:, slot_of(u), :].rearrange("p (c n) -> p c n", c=KC)
                    sp.dma_start(to, w_gu_v[e, :, :, c0:c0 + BLK]).then_inc(raw_in[slot_of(u)], 16)
                else:
                    sp.dma_start(raw[:, slot_of(u), :], w_dn_v[e, u - 4]).then_inc(raw_in[slot_of(u)], 16)

            load_front(0)
            load_front(1)
            sp.dma_start(bgu, b_gate_up[0]).then_inc(small_in, 16)
            sp.dma_start(g_q[:, :], mla_q_norm_g[0].rearrange("(p c) -> p c", c=2)).then_inc(small_in, 16)
            sp.dma_start(g_kv[:, :], mla_kv_norm_g[0].rearrange("(p c) -> p c", c=1)).then_inc(small_in, 16)
            sp.dma_start(rw[:, :, :], router_w[0].rearrange("(p c) n -> p c n", c=KC)).then_inc(small_in, 16)
            sp.dma_start(g_ffn[:, :], ffn_norm_g[0].rearrange("(p c) -> p c", c=KC)).then_inc(small_in, 16)
            sp.dma_start(rb[:, :], router_b[0].partition_broadcast(P)).then_inc(small_in, 16)
            load_front(2)
            load_front(3)
            for j in range(2):
                sp.dma_start(gain[:, j * BLK:(j + 1) * BLK],
                             ffn_norm_g[0, j * BLK:(j + 1) * BLK].partition_broadcast(P)).then_inc(gain_in, 16)
            for n in range(4, FRONT_UNITS):
                load_front(n)
            for u in range(UNITS):
                used_up(sp, FRONT_UNITS + u - RING)
                load_expert(0, u)
            for u in range(UNITS):
                sp.wait_ge(lo_ok, 2 * u + 2)
                load_expert(1, u)
            sp.wait_ge(n_ok, 1)
            items = sp.value_load(n_items[0:1, 0:1], min_val=EXPERTS, max_val=EXPERTS * CHUNKS)
            with sp.Fori(2, items) as i:
                e = sp.snap(i % EXPERTS)
                for u in range(UNITS):
                    sp.wait_ge(lo_ok, PIECES * i + (2 * u + 2 - PIECES))
                    load_expert(e, u)
            for t in range(TT):
                for n in range(2):
                    at = slice(n * BLK, (n + 1) * BLK)
                    sp.wait_ge(o_ok, 2 * t + n + 1)
                    sp.dma_start(out[0, t * P:(t + 1) * P, at], xs[:, t, at]).then_inc(out_done, 16)
            sp.wait_ge(out_done, 16 * 2 * TT)

        @block.tensor
        def _(pe):
            def gemm(o, lhs, rhs, n, start=True):
                for c in range(n):
                    mm = pe.matmul(o, lhs(c), rhs(c), start=start and c == 0, stop=c == n - 1)
                return mm

            def turned(o, src):
                return pe.transpose(o, src, ident)

            pe.wait_ge(cst_in, 16)
            for t in range(TT):
                pe.wait_ge(x_in[t], 16)
                for c in range(KC):
                    a = (c % 2) * TOKENS + t * P
                    tr = turned(B[2 + c // 2][:, a:a + P], xs[:, t, c:D:KC])
                    if t == TT - 1:
                        tr.then_inc(xT_ps, 1)
            pe.wait_ge(diag_ok, TT)
            for t in range(TT):
                mm = pe.matmul(B[6][:, t * P:(t + 1) * P], const("ones"), diag[:, t, :], start=True, stop=True)
            mm.then_inc(rstd_ps, 1)
            z_n = 0

            def z_unit(n):
                nonlocal z_n
                w = sum(c for _, c in Z_UNITS[n])
                landed_front(pe, n)
                for t in range(TT):
                    if z_n >= 2:
                        pe.wait_ge(z_ok, z_n - 1)
                    for c in range(KC):
                        if z_n == 0:
                            pe.wait_ge(hT_ok, c + 1)
                        mm = pe.matmul(ZB[t][:, 0:w], hT[:, c, t * P:(t + 1) * P], unit3(n, w)[:, c, :],
                                       start=c == 0, stop=c == KC - 1)
                    mm.then_inc(z_ps, 1)
                    z_n += 1

            def scores(b, q, k, signal):
                t, heads = BATCHES[b % 6]
                w = P * (t + 1)
                for m, h in enumerate(heads):
                    mm = pe.matmul(SB[b % 2][:, m * w:(m + 1) * w], q(h, t), k(h, w), start=True, stop=True)
                mm.then_inc(signal, 1)

            def pair_q(h, t):
                return qT[HD * (h % 2):HD * (h % 2) + HD, h // 2, t * P:(t + 1) * P]

            def pair_k(h, w):
                return kT[HD * (h % 2):HD * (h % 2) + HD, 0:w]

            def turn_pairs(zq, signal):
                for j in range(4):
                    for t in range(TT):
                        a = (j % 2) * TOKENS + t * P
                        tr = turned(TB[j // 2][:, a:a + P], zq[:, t, j * P:(j + 1) * P])
                    if j % 2:
                        tr.then_inc(signal, 1)
                for t in range(TT):
                    tr = turned(VB[0][:, t * P:(t + 1) * P], kk[:, t, :, :].rearrange("p a d -> p (a d)"))
                tr.then_inc(signal, 1)

            g_n = 0

            def gate_block():
                nonlocal g_n
                n = U_G + g_n // 4
                if g_n % 4 == 0:
                    landed_front(pe, n)
                if g_n >= 2:
                    pe.wait_ge(g_ok, g_n - 1)
                else:
                    pe.wait_ge(z_ok, 7 + g_n)
                a = (g_n % 4) * P
                mm = gemm(ZB[g_n % 2][:, 0:TOKENS], lambda c: unit3(n)[:, c, a:a + P], lambda c: hT[:, c, :], KC)
                mm.then_inc(g_ps, 1)
                g_n += 1

            z_unit(0)
            z_unit(1)
            pe.wait_ge(small_in, SMALL)
            for u in range(4):
                for c in range(4):
                    a = GU_COLS[u] + c
                    j = (u * 4 + c) * EXPERTS
                    tr = pe.transpose(B[7][:, j:j + EXPERTS], bgu[:, a:GU_COLS[u] + BLK:4], ident[0:EXPERTS, 0:EXPERTS])
            tr.then_inc(bgu_ps, 1)
            z_unit(2)
            pe.wait_ge(qi_rot, 1)
            turn_pairs(z_qi, qi_ps)
            z_unit(3)
            pe.wait_ge(qi_ok, 3)
            for b in range(6):
                if b >= 2:
                    pe.wait_ge(idx_rl, b - 1)
                scores(b, pair_q, pair_k, idx_ps)
                if b in GATES_IDX:
                    gate_block()
            pe.wait_ge(qb_rot, 1)
            turn_pairs(z_qb, qd_ps)
            gate_block()

            pe.wait_ge(z_ok, 8)
            pe.wait_ge(qd_ok, 3)
            for c in range(2):
                for t in range(TT):
                    tr = turned(TB[0][:, c * TOKENS + t * P:c * TOKENS + (t + 1) * P],
                                      z_ml[:, t, c:Q_LORA:2])
            tr.then_inc(c_ps, 1)
            for t in range(TT):
                tr = turned(TB[1][:, t * P:(t + 1) * P], z_ml[:, t, Q_LORA:Q_LORA + KV_LORA])
            tr.then_inc(c_ps, 1)
            gate_block()
            pe.wait_ge(bgu_ok, 1)
            landed_front(pe, U_UP)
            pe.wait_ge(c_ok, 2)
            pe.wait_ge(idx_rl, 6)
            for t in range(TT):
                at = slice(t * P, (t + 1) * P)
                if t:
                    pe.wait_ge(up_a, 2)
                gemm(SB[0][:, 0:BLK], lambda c: c_qT[:, c, at], lambda c: up_q[:, c, 0:BLK], 2)
                gemm(SB[1][:, 0:256], lambda c: c_qT[:, c, at], lambda c: up_q[:, c, BLK:768], 2).then_inc(up_ps, 1)
                if t:
                    pe.wait_ge(up_a, 4)
                    pe.wait_ge(up_d, 2)
                for j in range(2):
                    mm = gemm(VB[j][:, :], lambda c: c_kvT[:, at], lambda c: up_kv[:, j * BLK:(j + 1) * BLK], 1)
                mm.then_inc(up_ps, 1)
            gate_block()
            gate_block()
            pe.wait_ge(ml_rot, 1)
            pe.wait_ge(c_ok, 2)
            pe.wait_ge(up_a, 8)
            for j in range(4):
                for i, (src, out_ok) in enumerate(((q_ml, mq_ok), (k_ml, mk_ok))):
                    if j >= 2:
                        pe.wait_ge(out_ok, j - 1)
                    for h in (2 * j, 2 * j + 1):
                        for t in range(TT):
                            a = (h % 2) * TOKENS + t * P
                            tr = turned(TURN[(2 * j + i) % 4][0:QK, a:a + P], src[:, t, h, :])
                    tr.then_inc(mT_ps, 1)
            pe.wait_ge(mq_ok, 4)
            pe.wait_ge(mk_ok, 4)

            def scores_of(b):
                if b >= 2:
                    pe.wait_ge(s_mx, b - 1)
                if b < 6:
                    scores(b, lambda h, t: qmT[:, h, t * P:(t + 1) * P], lambda h, w: kmT[:, h, 0:w], s_ps)
                else:
                    scores(b, pair_q, pair_k, s_ps)

            def turn_probs(b):
                pe.wait_ge(p_ok, b + 1)
                if b >= 2:
                    pe.wait_ge(pT_ok, b - 1)
                for m in range(4):
                    tr = turned(TB[b % 2][:, m * P:(m + 1) * P], prob[:, b % 2, m * P:(m + 1) * P])
                tr.then_inc(pT_ps, 1)

            def values(b):
                t, heads = BATCHES[b % 6]
                pe.wait_ge(pT_ok, b + 1)
                if b in (6, 8):
                    pe.wait_ge(pv_ok, t + 1)
                for m in range(4):
                    h = heads[m // (t + 1)]
                    kt = m % (t + 1)
                    half = V_DIM * (h % 2)
                    v = v_ml[:, kt, h, :] if b < 6 else z_kv[:, kt, HD:2 * HD]
                    mm = pe.matmul(VB[t][half:half + V_DIM, (h // 2) * P:(h // 2 + 1) * P], v,
                                   probT[:, b % 2, m * P:(m + 1) * P], start=kt == 0, stop=kt == t)
                mm.then_inc(pv_ps, 1)

            pe.wait_ge(up_d, 4)
            pe.wait_ge(up_a, 8)
            scores_of(0)
            for b in range(12):
                if b < 11:
                    scores_of(b + 1)
                if b:
                    values(b - 1)
                if b in GATES_ATT:
                    gate_block()
                turn_probs(b)
            def branch(i, mc):
                o = (mlaT, dsaT)[i]
                return gemm(SB[mc % 2][:, i * TOKENS:(i + 1) * TOKENS],
                            lambda c: br_w[i][:, c, mc * P:(mc + 1) * P], lambda c: o[:, c, :], 4)

            landed_front(pe, U_BR)
            pe.wait_ge(pv_ok, 2)
            pe.wait_ge(s_mx, 12)
            branch(0, 0)
            values(11)
            branch(0, 1)
            landed_front(pe, U_BR + 1)
            pe.wait_ge(pv_ok, 4)
            for mc in range(KC):
                if mc >= 2:
                    pe.wait_ge(br_ok, 2 * (mc - 1) - 1)
                    branch(0, mc)
                branch(1, mc).then_inc(br_ps, 1)
            landed_front(pe, U_WO)
            landed_front(pe, U_WO + 1)
            pe.wait_ge(g_ok, 16)
            pe.wait_ge(pT_ok, 12)
            def project(t, n):
                for c in range(KC):
                    if t == 0 and n == 0:
                        pe.wait_ge(br_ok, 2 * (c + 1))
                    mm = pe.matmul(B[2 * t + n][:, :], mT[:, c, t * P:(t + 1) * P], unit3(U_WO + n)[:, c, :],
                                   start=c == 0, stop=c == KC - 1)
                    if t == 0 and n == 0 and c == 0:
                        mm.then_inc(used, SPLITS)
                mm.then_inc(wo_ps, 1)

            def turn_x1(t):
                pe.wait_ge(x1_ok, 2 * t + 2)
                for c in range(KC):
                    tr = turned(B[4 + 2 * t + c // 4][:, (c % 4) * P:(c % 4 + 1) * P], xs[:, t, c:D:KC])
                    if c % 4 == 3:
                        tr.then_inc(x1T_ps, 1)

            def logits(t):
                gemm(B[3 * t][:, 0:EXPERTS], lambda c: x1T[:, c, t * P:(t + 1) * P],
                     lambda c: rw[:, c, :], KC).then_inc(lg_ps, 1)

            def stay_warm(n):
                for _ in range(n):
                    pe.matmul(B[1][:, :], hi[:, 0, 0, 0:P], hi[:, 0, 0, :], start=True, stop=True)

            project(0, 0)
            project(0, 1)
            project(1, 0)
            turn_x1(0)
            project(1, 1)
            pe.wait_ge(x1T_ok, 2)
            pe.wait_ge(rw_ok, 1)
            logits(0)
            stay_warm(WARM[0])
            turn_x1(1)
            pe.wait_ge(x1T_ok, 3)
            pe.wait_ge(x1T_last, 1)
            logits(1)
            stay_warm(WARM[1])
            pe.wait_ge(sel_ok, TT)
            ones, before = const("ones"), const("before")
            pe.matmul(B[7][:, 0:32], before, sel[:, 0, :], start=True, stop=True).then_inc(ev_used, 2)
            pe.matmul(B[7][:, 32:64], ones, sel[:, 0, :], start=True, stop=False)
            pe.matmul(B[7][:, 32:64], before, sel[:, 1, :], start=False, stop=True)
            pe.matmul(B[7][:, 64:96], ones, sel[:, 0, :], start=True, stop=False)
            pe.matmul(B[7][:, 64:96], ones, sel[:, 1, :], start=False, stop=True).then_inc(pos_ps, 1)
            pe.wait_ge(gate_ok, 1)
            for t in range(TT):
                tr = pe.transpose(B[2][0:EXPERTS, t * P:(t + 1) * P], gate[:, t, :], ident)
            tr.then_inc(gT_ps, 1)
            def gather():
                for c in range(KC):
                    for t in range(TT):
                        mm = pe.matmul(PREP[:, c * SLOTS:(c + 1) * SLOTS], h2[:, t, c * P:(c + 1) * P],
                                       onehot[:, t, :], start=t == 0, stop=t == TT - 1)
                mm.then_inc(gath_ps, 1)

            stay_warm(WARM[2])
            pe.wait_ge(prep_ok, 1)
            pe.wait_ge(h2_ok, TT)
            gather()
            stay_warm(WARM[3])
            pe.wait_ge(n_ok, 1)
            items = pe.value_load(n_items[0:1, 0:1], min_val=EXPERTS, max_val=EXPERTS * CHUNKS)

            def scatter(n, i):
                pe.wait_ge(ev_ok, UNITS * i + (2 + 4 + n + 1 - UNITS))
                for t in range(TT):
                    mm = pe.matmul(ACC[2 * t + n][:, :], scat[:, t * P:(t + 1) * P], ev[:, n, :],
                                   start=False, stop=True, skip_group_check=True)
                mm.then_inc(ev_used, 1)

            def start_sums():
                pe.wait_ge(gT_ok, 1)
                pe.wait_ge(bd_in, 16)
                for t in range(TT):
                    for n in range(2):
                        mm = pe.matmul(ACC[2 * t + n][:, :], gateT[:, t * P:(t + 1) * P], bd[:, n * BLK:(n + 1) * BLK],
                                       start=True, stop=True)
                mm.then_inc(sums_ok, 1)

            def item(i, first):
                def piece(p):
                    down = p >= 8
                    if down:
                        bank, chunk, begin, end = p % 2, 4 * ((p - 8) // 2), p < 10, p >= 10
                    else:
                        bank, chunk, begin, end = p // 2 % 2, 4 * (p % 2), p % 2 == 0, p % 2 == 1
                    if begin:
                        unit_no = p - 4 if down else p // 2
                        pe.wait_ge(ev_ok, UNITS * i + (unit_no + 1))
                    x_of = ae if down else xe
                    pe.wait_ge(hi_ok, PIECES * i + (p + 1))
                    for c in range(4):
                        pe.matmul(MM[bank][:, :], x_of[:, chunk + c, :, :].rearrange("p a s -> p (a s)"),
                                  hi[:, p % SPLITS, c, :], start=begin and c == 0, stop=False)
                    pe.wait_ge(lo_ok, PIECES * i + (p + 1))
                    for c in range(4):
                        mm = pe.matmul(MM[bank][:, :], x_of[:, chunk + c, :, :].rearrange("p a s -> p (a s)"),
                                       lo[:, p % SPLITS, c, :], start=False, stop=end and c == 3)
                    mm.then_inc(used, 1)

                def turn(u):
                    pe.wait_ge(ev_ok, UNITS * i + (2 + u + 1))
                    if u % 2 == 0:
                        pe.wait_ge(gub_ok, 2 * i + (u // 2 + 1))
                    for c in range(4):
                        a = ((u % 2) * 4 + c) * SLOTS
                        mm = pe.matmul(GUT[:, a:a + SLOTS], ev[:, u % 2, c:BLK:4], const("ident2"),
                                       start=True, stop=True)
                    mm.then_inc(ev_used, 1)

                pe.wait_ge(xl_ok, i + 1)
                piece(0)
                if not first:
                    scatter(0, i)
                piece(1)
                if not first:
                    scatter(1, i)
                piece(2)
                turn(0)
                for t in range(TT):
                    tr = turned(PREP[:, t * P:(t + 1) * P], gated[:, t, :])
                tr.then_inc(sc_ps, 1)
                piece(3)
                piece(4)
                turn(1)
                piece(5)
                if first:
                    start_sums()
                piece(6)
                turn(2)
                piece(7)
                pe.wait_ge(al_ok, 2 * i + 1)
                piece(8)
                turn(3)
                piece(9)
                pe.wait_ge(prep_ok, i + 2)
                pe.wait_ge(sc_ok, i + 1)
                gather()
                pe.wait_ge(al_ok, 2 * i + 2)
                piece(10)
                piece(11)

            item(0, True)
            with pe.Fori(1, items) as i:
                item(i, False)
            scatter(0, items)
            scatter(1, items)

        @block.scalar
        def _(act):
            step = stepper(act, act_step)
            act.wait_ge(one_ok, 1)
            step(act.activation(stat[:, 15:16], stat[:, 14:15], ACT.Sqrt))
            for t in range(TT):
                act.wait_ge(x_in[t], 16)
                step(act.activation(sgT[:, 0:2, :, :].rearrange("p c a t -> p (c a t)"),
                                    xs[:, t, :], ACT.Square, accum_out=stat[:, t:t + 1]))
            act.copy(stat[:, 6:7], stat[:, 1:2]).then_inc(x_sq, 1)
            act.wait_ge(x_ms, 1)
            act.activation(stat[:, 4:6], stat[:, 2:4], ACT.Sqrt).then_inc(x_rt, 1)
            act.wait_ge(ang_ok, 1)
            act.activation(trig[:, :, :, :], ang[:, :, :, :], ACT.Sin).then_inc(trig_ok, 1)

            z_out = [lambda t: z_kv[:, t, :], lambda t: z_qi[:, t, :], lambda t: z_qb[:, t, :], lambda t: z_ml[:, t, :]]

            def z_evac(n):
                w = sum(c for _, c in Z_UNITS[n])
                for t in range(TT):
                    act.wait_ge(z_ps, 2 * n + t + 1)
                    act.copy(z_out[n](t), ZB[t][:, 0:w]).then_inc(z_ok, 1)

            z_evac(0)
            z_evac(1)
            z_evac(2)
            for j in range(2):
                act.wait_ge(qi_ps, j + 1)
                act.copy(qT[:, 2 * j:2 * j + 2, :].rearrange("p j t -> p (j t)"), TB[j][:, :]).then_inc(qi_ok, 1)
            act.wait_ge(qi_ps, 3)
            act.copy(kT[:, :], VB[0][:, 0:TOKENS]).then_inc(qi_ok, 1)
            z_evac(3)
            g_n = 0

            def gate_evac():
                nonlocal g_n
                act.wait_ge(g_ps, g_n + 1)
                act.copy(sgT[:, g_n % KC, g_n // KC, :], ZB[g_n % 2][:, 0:TOKENS]).then_inc(g_ok, 1)
                g_n += 1

            for b in range(6):
                act.wait_ge(idx_ps, b + 1)
                if b >= 2:
                    act.wait_ge(idx_ac, b - 1)
                act.activation(prob[:, b % 2, :], SB[b % 2][:, :], ACT.Relu, scale=HD ** -0.5).then_inc(idx_rl, 1)
                if b in GATES_IDX:
                    gate_evac()
            for j in range(2):
                act.wait_ge(qd_ps, j + 1)
                act.copy(qT[:, 2 * j:2 * j + 2, :].rearrange("p j t -> p (j t)"), TB[j][:, :]).then_inc(qd_ok, 1)
            act.wait_ge(qd_ps, 3)
            act.copy(kT[:, :], VB[0][:, 0:TOKENS]).then_inc(qd_ok, 1)
            for t in range(TT):
                step(act.activation(probT[:, 0, 0:Q_LORA], z_ml[:, t, 0:Q_LORA],
                                    ACT.Square, accum_out=stat[:, 7 + t:8 + t]))
                step(act.activation(probT[:, 0, 0:KV_LORA], z_ml[:, t, Q_LORA:Q_LORA + KV_LORA],
                                    ACT.Square, accum_out=stat[:, 9 + t:10 + t]))
            act.copy(stat[:, 6:7], stat[:, 10:11]).then_inc(c_sq, 1)
            act.wait_ge(c_ms, 1)
            act.activation(stat[:, 7:11], stat[:, 7:11], ACT.Sqrt).then_inc(c_rt, 1)

            gate_evac()
            gate_evac()
            act.wait_ge(c_rs, 1)
            act.wait_ge(idx_ac, 6)
            for t in range(TT):
                act.wait_ge(up_ps, 2 * t + 1)
                q_flat = q_ml[:, t, :, :].rearrange("p h d -> p (h d)")
                act.activation(q_flat[:, 0:BLK], SB[0][:, :], ACT.Copy, scale=stat[:, 11 + t:12 + t]).then_inc(up_a, 1)
                act.activation(q_flat[:, BLK:768], SB[1][:, 0:256], ACT.Copy, scale=stat[:, 11 + t:12 + t]).then_inc(up_a, 1)
                act.wait_ge(up_ps, 2 * t + 2)
                for j in range(2):
                    src = VB[j][:, :].rearrange("p (h d) -> p h d", h=4)
                    act.activation(k_ml[:, t, 4 * j:4 * j + 4, 0:NOPE], src[:, :, 0:NOPE], ACT.Copy,
                                   scale=stat[:, 13 + t:14 + t]).then_inc(up_a, 1)
            gate_evac()
            gate_evac()
            for j in range(4):
                act.wait_ge(mT_ps, 2 * j + 1)
                act.copy(qmT[:, 2 * j:2 * j + 2, :].rearrange("p h t -> p (h t)"), TURN[2 * j % 4][0:QK, :]).then_inc(mq_ok, 1)

            def exps(b):
                t, heads = BATCHES[b % 6]
                w = P * (t + 1)
                act.wait_ge(s_mx, b + 1)
                for m in range(len(heads)):
                    ex = act.activation(prob[:, b % 2, m * w:(m + 1) * w], prob[:, b % 2, m * w:(m + 1) * w], ACT.Exp,
                                        bias=mx[:, b % 2, m:m + 1], accum_out=den[:, b % 2, m:m + 1])
                ex.then_inc(p_ex, 1)

            def out_of(b):
                if b % 6 in (1, 5):
                    act.wait_ge(pv_ps, b + 1)
                    t = BATCHES[b % 6][0]
                    to = mlaT if b < 6 else dsaT
                    act.copy(to[:, :, t * P:(t + 1) * P], VB[t][:, :].rearrange("p (j q) -> p j q", j=4)).then_inc(pv_ok, 1)

            exps(0)
            for b in range(12):
                if b < 11:
                    exps(b + 1)
                if b:
                    out_of(b - 1)
                if b in GATES_ATT:
                    gate_evac()
                act.wait_ge(pT_ps, b + 1)
                act.copy(probT[:, b % 2, :], TB[b % 2][:, :]).then_inc(pT_ok, 1)
            out_of(11)
            act.wait_ge(g_ok, 16)
            for mc in range(0, KC, 2):
                act.activation(sgT[:, mc:mc + 2, :, :], sgT[:, mc:mc + 2, :, :], ACT.Sigmoid).then_inc(sig_ok, 1)
            def high(i, p):
                if p % 2 == 0:
                    landed_expert(act, i, p // 2)
                act.wait_ge(used, PIECES * i + (p + 1))
                act.copy(hi[:, p % SPLITS, :, :], piece_of(p)).then_inc(hi_ok, 1)

            def x1T_out(j):
                t, a = j // 2, (j % 2) * 4
                act.wait_ge(x1T_ps, j + 1)
                act.copy(x1T[:, a:a + 4, t * P:(t + 1) * P], B[4 + j][:, :].rearrange("p (c t) -> p c t", c=4)).then_inc(x1T_ok, 1)

            for t in range(TT):
                act.wait_ge(x1_ok, 2 * t + 2)
                step(act.activation(h2[:, t, :], xs[:, t, :], ACT.Square, accum_out=stat[:, t:t + 1]))
                act.copy(stat[:, 6:7], stat[:, t:t + 1]).then_inc(f_sq, 1)
                if t == 1:
                    x1T_out(2)
                act.wait_ge(f_ms, t + 1)
                act.activation(stat[:, 4 + t:5 + t], stat[:, 2 + t:3 + t], ACT.Sqrt).then_inc(f_rt, 1)
                if t == 0:
                    for p in range(SPLITS):
                        high(0, p)
                    x1T_out(0)
                    x1T_out(1)
            for t in range(TT):
                act.wait_ge(lg_mx, t + 1)
                act.activation(r_b[:, t, :], lg[:, t, :], ACT.Exp, bias=r_s[:, t, 0:1]).then_inc(lg_ex, 1)
            act.wait_ge(h2_ok, TT)
            act.dma_start(bd, b_down[0]).then_inc(bd_in, 16)
            act.wait_ge(gT_ps, 1)
            act.copy(gateT[:, :], B[2][0:EXPERTS, 0:TOKENS]).then_inc(gT_ok, 1)
            def split_x(n):
                act.wait_ge(gath_ps, n)
                act.copy(xe[:, :, 0, :], PREP[:, :].rearrange("p (c s) -> p c s", c=KC)).then_inc(xh_ok, 1)

            act.copy(stat[:, 6:7], stat[:, 0:1]).then_inc(ev_ok, 2)
            split_x(1)
            act.wait_ge(n_ok, 1)
            items = act.value_load(n_items[0:1, 0:1], min_val=EXPERTS, max_val=EXPERTS * CHUNKS)

            def evac(u, i, back=0):
                act.wait_ge(used, PIECES * i + (SPLITS + pieces_until(u) - PIECES * back))
                if u < 4:
                    act.wait_ge(ev_used, UNITS * i + (u + 1))
                act.copy(ev[:, u % 2, :], MM[u % 2][:, :]).then_inc(ev_ok, 1)

            def item(i, first):
                def sigmoid(half):
                    act.wait_ge(glu_ok, 2 * i + (half + 1))
                    act.activation(sig[:, :, :], glu, ACT.Sigmoid, scale=ALPHA).then_inc(sig2_ok, 1)

                def high_act(half):
                    act.wait_ge(actv_ok, 2 * i + (half + 1))
                    act.copy(ae[:, 4 * half:4 * half + 4, 0, :], sig[:, :, :]).then_inc(ah_ok, 1)

                if not first:
                    high(i, 0)
                    evac(4, i, 1)
                    high(i, 1)
                    evac(5, i, 1)
                    high(i, 2)
                    high(i, 3)
                if first:
                    high(i, 4)
                    evac(0, i)
                    high(i, 5)
                    high(i, 6)
                else:
                    evac(0, i)
                    high(i, 4)
                    high(i, 5)
                act.wait_ge(sc_ps, i + 1)
                act.copy(scat[:, :], PREP[:, 0:TOKENS]).then_inc(sc_ok, 1)
                evac(1, i)
                if not first:
                    high(i, 6)
                high(i, 7)
                evac(2, i)
                sigmoid(0)
                high(i, 8)
                high_act(0)
                high(i, 9)
                evac(3, i)
                high(i, 10)
                sigmoid(1)
                high(i, 11)
                high_act(1)
                split_x(i + 2)

            item(0, True)
            act.wait_ge(sums_ok, 1)
            for j in range(2):
                act.dma_start(gain[:, j * BLK:(j + 1) * BLK],
                              final_norm_g[j * BLK:(j + 1) * BLK].partition_broadcast(P)).then_inc(final_in, 16)
            with act.Fori(1, items) as i:
                item(i, False)
            evac(4, items, 1)
            evac(5, items, 1)
            step(act.activation(stat[:, 15:16], const("ones")[:, 0:1], ACT.Sqrt))
            for t in range(TT):
                act.wait_ge(y_ok, 3 + t)
                act.activation(h2[:, t, :], xs[:, t, :], ACT.Square, accum_out=stat[:, t:t + 1]).then_inc(y_sq, 1)
                act.wait_ge(y_ms, t + 1)
                act.activation(stat[:, 4 + t:5 + t], stat[:, 2 + t:3 + t], ACT.Sqrt).then_inc(y_rt, 1)

        @block.vector
        def _(dve):
            step = stepper(dve, dve_step)

            def rotate(view, heads, half, every):
                ta, tb = (x[:, :, 0:heads, 0:2 * half] for x in (ropa, ropb))
                shape = [P, TT, heads, half]
                cos = trig[:, 0, :, 0:16:every].unsqueeze(2).to_broadcast(shape)
                sin = trig[:, 1, :, 0:16:every].unsqueeze(2).to_broadcast(shape)
                neg = nsin[:, :, 0:16:every].unsqueeze(2).to_broadcast(shape)
                x1, x2 = view[:, :, :, 0:half], view[:, :, :, half:2 * half]
                dve.tensor_tensor(ta[:, :, :, 0:half], x1, cos, ALU.mult)
                dve.tensor_tensor(ta[:, :, :, half:2 * half], x2, cos, ALU.mult)
                dve.tensor_tensor(tb[:, :, :, 0:half], x2, neg, ALU.mult)
                step(dve.tensor_tensor(tb[:, :, :, half:2 * half], x1, sin, ALU.mult))
                return dve.tensor_tensor(view, ta, tb, ALU.add)

            dve.memset(stat[:, 14:15], 1.0).then_inc(one_ok, 1)
            dve.wait_ge(x_sq, 1)
            dve.tensor_scalar(stat[:, 2:4], stat[:, 0:2], 1.0 / D, EPS, ALU.mult, ALU.add).then_inc(x_ms, 1)
            dve.wait_ge(x_rt, 1)
            step(dve.reciprocal(stat[:, 0:2], stat[:, 4:6]))
            dve.wait_ge(cst_in, 16)
            for t in range(TT):
                dve.tensor_scalar(diag[:, t, :], ident, stat[:, t:t + 1], None, ALU.mult).then_inc(diag_ok, 1)
            dve.wait_ge(rstd_ps, 1)
            dve.wait_ge(early_in, 48)
            step(dve.tensor_copy(rstd_row[:, :], B[6][:, 0:TOKENS]))
            for c in range(KC):
                dve.wait_ge(xT_ps, c + 1)
                a = (c % 2) * TOKENS
                dve.scalar_tensor_tensor(out=hT[:, c, :], in0=B[2 + c // 2][:, a:a + TOKENS], scalar=g_in[:, c:c + 1],
                                         in1=rstd_row[:, :], op0=ALU.mult, op1=ALU.mult).then_inc(hT_ok, 1)
            dve.wait_ge(early_in, 48)
            step(dve.tensor_copy(pos_f[:, :], pos_i[:, :]))
            for t in range(TT):
                dve.tensor_scalar(ang[:, 1, t, :], const("invfreq"), pos_f[:, t:t + 1], None, ALU.mult)
                last = dve.tensor_scalar(ang[:, 0, t, :], const("invfreq"), pos_f[:, t:t + 1], None, ALU.mult)
            step(last)
            magic = float(1.5 * 2 ** 23)
            dve.tensor_scalar(turns[:, 1], ang[:, 1], 1.0 / (2 * np.pi), None, ALU.mult)
            step(dve.tensor_scalar(turns[:, 0], ang[:, 0], 1.0 / (2 * np.pi), 0.25, ALU.mult, ALU.add))
            step(dve.tensor_scalar(turns[:], turns[:], magic, None, ALU.add))
            step(dve.tensor_scalar(turns[:], turns[:], magic, None, ALU.subtract))
            rest = 2 * np.pi
            for _ in range(3):
                part = float((np.float32(rest).view(np.uint32) & np.uint32(0xFFFFF000)).view(np.float32))
                rest -= part
                step(dve.scalar_tensor_tensor(out=ang[:], in0=turns[:], scalar=-part, in1=ang[:], op0=ALU.mult, op1=ALU.add))
            step(dve.tensor_scalar(ang[:, 0], ang[:, 0], float(np.pi / 2), None, ALU.add))
            dve.tensor_scalar(ang[:], ang[:], 3.1415925, -3.1415925, ALU.min, ALU.max).then_inc(ang_ok, 1)

            dve.wait_ge(trig_ok, 1)
            dve.tensor_scalar(nsin[:, :, :], trig[:, 1], -1.0, None, ALU.mult).then_inc(nsin_ok, 1)
            dve.wait_ge(nsin_ok, 1)
            dve.wait_ge(z_ok, 2)
            step(rotate(z_kv[:, :, 2 * HD:3 * HD].unsqueeze(2)[:, :, :, 0:ROT], 1, ROT // 2, 2))
            step(dve.tensor_scalar(w_idx[:, :, :], z_kv[:, :, 3 * HD:3 * HD + HEADS], HEADS ** -0.5, None, ALU.mult))
            step(dve.tensor_copy(kk[:, :, :, :], z_kv[:, :, 2 * HD:3 * HD].unsqueeze(2).to_broadcast([P, TT, 2, HD])))
            dve.wait_ge(z_ok, 4)
            rotate(z_qi[:, :, :].rearrange("p t (h d) -> p t h d", h=HEADS)[:, :, :, 0:ROT], HEADS, ROT // 2, 2).then_inc(qi_rot, 1)
            dve.wait_ge(bgu_ps, 1)
            dve.tensor_copy(bias_gu[:, :, :], B[7][:, :].rearrange("p (j e) -> p e j", e=EXPERTS)).then_inc(bgu_ok, 1)
            dve.wait_ge(small_in, SMALL)
            dve.tensor_tensor(rw[:, :, :], rw[:, :, :], g_ffn[:, :].unsqueeze(2).to_broadcast([P, KC, EXPERTS]),
                              ALU.mult).then_inc(rw_ok, 1)
            for b in range(6):
                t, heads = BATCHES[b]
                w = P * (t + 1)
                dve.wait_ge(idx_rl, b + 1)
                for m, h in enumerate(heads):
                    src = prob[:, b % 2, m * w:(m + 1) * w]
                    if h == 0:
                        ins = dve.tensor_scalar(score[:, t, 0:w], src, w_idx[:, t, h:h + 1], None, ALU.mult)
                    else:
                        ins = dve.scalar_tensor_tensor(out=score[:, t, 0:w], in0=src, scalar=w_idx[:, t, h:h + 1],
                                                       in1=score[:, t, 0:w], op0=ALU.mult, op1=ALU.add)
                    if m < len(heads) - 1:
                        step(ins)
                ins.then_inc(idx_ac, 1)
                dve.wait_ge(idx_ac, b + 1)
            for t in range(TT):
                last = dve.tensor_tensor(score[:, t, t * P:(t + 1) * P], score[:, t, t * P:(t + 1) * P], const("causal"), ALU.add)
            step(last)

            def topk():
                for t in range(TT):
                    w = P * (t + 1)
                    sc, wk = score[:, t, 0:w], work[:, t, 0:w]
                    for r in range(TOPK // 8):
                        step(dve.max(top8[:, t, :], sc if r == 0 else wk))
                        if r < TOPK // 8 - 1:
                            step(dve.match_replace(wk, top8[:, t, :], sc if r == 0 else wk, REMOVED))
                        if r % 3 == 2:
                            yield
                    over, same, count = (pick[:, j, 0:w] for j in range(3))
                    thr = top8[:, t, 7:8]
                    dve.tensor_scalar(over, sc, thr, 0.0, ALU.is_gt, ALU.add, accum_out=cnt[:, t:t + 1])
                    step(dve.tensor_scalar(same, sc, thr, None, ALU.is_equal))
                    dve.tensor_tensor_scan(count, same, same, 0.0, ALU.add, ALU.max)
                    step(dve.tensor_scalar(cnt[:, t:t + 1], cnt[:, t:t + 1], -1.0, float(TOPK), ALU.mult, ALU.add))
                    step(dve.scalar_tensor_tensor(out=same, in0=count, scalar=cnt[:, t:t + 1], in1=same, op0=ALU.is_le, op1=ALU.mult))
                    step(dve.tensor_tensor(over, over, same, ALU.add))
                    step(dve.tensor_scalar(allow[:, t, 0:w], over, -1.0, -NEG, ALU.add, ALU.mult))
                    step(dve.tensor_tensor(allow[:, t, t * P:(t + 1) * P], allow[:, t, t * P:(t + 1) * P], const("causal"), ALU.add))
                    yield

            dve.wait_ge(c_sq, 1)
            step(dve.tensor_scalar(stat[:, 7:9], stat[:, 7:9], 1.0 / Q_LORA, EPS, ALU.mult, ALU.add))
            dve.tensor_scalar(stat[:, 9:11], stat[:, 9:11], 1.0 / KV_LORA, EPS, ALU.mult, ALU.add).then_inc(c_ms, 1)
            for c in range(2):
                dve.wait_ge(c_ps, 1)
                last = dve.tensor_scalar(c_qT[:, c, :], TB[0][:, c * TOKENS:(c + 1) * TOKENS], g_q[:, c:c + 1], None, ALU.mult)
            last.then_inc(c_ok, 1)
            dve.wait_ge(c_ps, 2)
            dve.tensor_scalar(c_kvT[:, :], TB[1][:, 0:TOKENS], g_kv[:, 0:1], None, ALU.mult).then_inc(c_ok, 1)
            dve.wait_ge(c_rt, 1)
            dve.reciprocal(stat[:, 11:15], stat[:, 7:11]).then_inc(c_rs, 1)
            dve.wait_ge(c_rs, 1)
            parts = topk()
            for _ in range(3):
                next(parts)
            for t in range(TT):
                dve.wait_ge(up_ps, 2 * t + 2)
                dve.wait_ge(up_a, 4 * t + 4)
                for j in range(2):
                    src = VB[j][:, :].rearrange("p (h d) -> p h d", h=4)
                    dve.tensor_scalar(v_ml[:, t, 4 * j:4 * j + 4, :], src[:, :, NOPE:NOPE + V_DIM],
                                      stat[:, 13 + t:14 + t], None, ALU.mult).then_inc(up_d, 1)
            for j in range(4):
                dve.wait_ge(mT_ps, 2 * j + 2)
                dve.tensor_copy(kmT[:, 2 * j:2 * j + 2, :].rearrange("p h t -> p (h t)"), TURN[(2 * j + 1) % 4][0:QK, :]).then_inc(mk_ok, 1)

            def masked(b):
                t, heads = BATCHES[b % 6]
                w, n = P * (t + 1), len(heads)
                scale = (QK if b < 6 else HD) ** -0.5
                src = SB[b % 2][:, :].rearrange("p (h k) -> p h k", h=n)
                pr = prob[:, b % 2, :].rearrange("p (h k) -> p h k", h=n)
                dve.wait_ge(s_ps, b + 1)
                if b >= 2:
                    dve.wait_ge(pT_ps, b - 1)
                if b >= 6:
                    mask = allow[:, t, 0:w].unsqueeze(1).to_broadcast([P, n, w])
                    step(dve.scalar_tensor_tensor(out=pr, in0=src, scalar=scale, in1=mask, op0=ALU.mult, op1=ALU.add))
                else:
                    if t:
                        dve.tensor_scalar(pr[:, :, 0:P], src[:, :, 0:P], scale, None, ALU.mult)
                    mask = const("causal").unsqueeze(1).to_broadcast([P, n, P])
                    step(dve.scalar_tensor_tensor(out=pr[:, :, t * P:w], in0=src[:, :, t * P:w], scalar=scale, in1=mask,
                                                  op0=ALU.mult, op1=ALU.add))
                step(dve.tensor_reduce(mx[:, b % 2, 0:n], pr, AXX, ALU.max))
                dve.tensor_scalar(mx[:, b % 2, 0:n], mx[:, b % 2, 0:n], -1.0, None, ALU.mult).then_inc(s_mx, 1)

            def normalised(b):
                t, heads = BATCHES[b % 6]
                w, n = P * (t + 1), len(heads)
                pr = prob[:, b % 2, :].rearrange("p (h k) -> p h k", h=n)
                dve.wait_ge(p_ex, b + 1)
                step(dve.reciprocal(den[:, b % 2, 0:n], den[:, b % 2, 0:n]))
                dve.tensor_tensor(pr, pr, den[:, b % 2, 0:n].unsqueeze(2).to_broadcast([P, n, w]), ALU.mult).then_inc(p_ok, 1)

            masked(0)
            for b in range(12):
                if b == 5:
                    for _ in parts:
                        pass
                if b < 11:
                    masked(b + 1)
                normalised(b)
                next(parts, None)
            for mc in range(KC):
                dve.wait_ge(br_ps, mc + 1)
                dve.wait_ge(sig_ok, mc // 2 + 1)
                sg = sgT[:, mc, :, :].rearrange("p a t -> p (a t)")
                dve.tensor_tensor(sg, sg, SB[mc % 2][:, :], ALU.mult).then_inc(br_ok, 1)
                dve.wait_ge(br_ok, 2 * mc + 1)
                dve.tensor_tensor(mT[:, mc, :], sg[:, 0:TOKENS], sg[:, TOKENS:2 * TOKENS], ALU.add).then_inc(br_ok, 1)
            def low(i, p):
                dve.wait_ge(hi_ok, PIECES * i + (p + 1))
                dve.tensor_tensor(lo[:, p % SPLITS, :, :], piece_of(p), hi[:, p % SPLITS, :, :].bitcast(F32),
                                  ALU.subtract).then_inc(lo_ok, 1)

            def residual(t):
                for n in range(2):
                    dve.wait_ge(wo_ps, 2 * t + n + 1)
                    at = slice(n * BLK, (n + 1) * BLK)
                    dve.tensor_tensor(xs[:, t, at], xs[:, t, at], B[2 * t + n][:, :], ALU.add).then_inc(x1_ok, 1)

            def mean(t):
                dve.wait_ge(f_sq, t + 1)
                dve.tensor_scalar(stat[:, 2 + t:3 + t], stat[:, t:t + 1], 1.0 / D, EPS, ALU.mult, ALU.add).then_inc(f_ms, 1)

            def root(t):
                dve.wait_ge(f_rt, t + 1)
                step(dve.reciprocal(stat[:, t:t + 1], stat[:, 4 + t:5 + t]))

            def normed(t):
                dve.scalar_tensor_tensor(out=h2[:, t, :], in0=xs[:, t, :], scalar=stat[:, t:t + 1], in1=gain[:, :],
                                         op0=ALU.mult, op1=ALU.mult).then_inc(h2_ok, 1)

            def route(t):
                step(dve.scalar_tensor_tensor(out=lg[:, t, :], in0=B[3 * t][:, 0:EXPERTS],
                                              scalar=stat[:, t:t + 1], in1=rb[:, :], op0=ALU.mult, op1=ALU.add))
                step(dve.max(top8[:, t, :], lg[:, t, :]))
                dve.tensor_scalar(r_s[:, t, 0:1], top8[:, t, 0:1], -1.0, None, ALU.mult).then_inc(lg_mx, 1)
                thr = top8[:, t, EXP_K - 1:EXP_K]
                dve.tensor_scalar(sel[:, t, :], lg[:, t, :], thr, 0.0, ALU.is_gt, ALU.add, accum_out=r_s[:, t, 1:2])
                step(dve.tensor_scalar(r_a[:, t, :], lg[:, t, :], thr, None, ALU.is_equal))
                dve.tensor_tensor_scan(pm[:, t, :], r_a[:, t, :], r_a[:, t, :], 0.0, ALU.add, ALU.max)
                step(dve.tensor_scalar(r_s[:, t, 1:2], r_s[:, t, 1:2], -1.0, float(EXP_K), ALU.mult, ALU.add))
                step(dve.scalar_tensor_tensor(out=r_a[:, t, :], in0=pm[:, t, :], scalar=r_s[:, t, 1:2], in1=r_a[:, t, :],
                                              op0=ALU.is_le, op1=ALU.mult))
                dve.tensor_tensor(sel[:, t, :], sel[:, t, :], r_a[:, t, :], ALU.add).then_inc(sel_ok, 1)

            residual(0)
            dve.wait_ge(gain_in, 32)
            mean(0)
            root(0)
            normed(0)
            for p in range(SPLITS):
                low(0, p)
            residual(1)
            dve.wait_ge(x1T_ps, 4)
            dve.tensor_copy(x1T[:, 4:8, P:2 * P], B[7][:, :].rearrange("p (c t) -> p c t", c=4)).then_inc(x1T_last, 1)
            mean(1)
            dve.wait_ge(lg_ps, 1)
            route(0)
            root(1)
            dve.wait_ge(lg_ps, 2)
            route(1)
            normed(1)
            dve.wait_ge(sel_ok, TT)
            dve.wait_ge(lg_ex, TT)
            step(dve.tensor_tensor(r_b[:, :, :], r_b[:, :, :], sel[:, :, :], ALU.mult))
            step(dve.tensor_reduce(r_s[:, :, 2:3], r_b[:, :, :], AXX, ALU.add))
            step(dve.reciprocal(r_s[:, :, 3:4], r_s[:, :, 2:3]))
            dve.tensor_tensor(gate[:, :, :], r_b[:, :, :], r_s[:, :, 3:4].to_broadcast([P, TT, EXPERTS]), ALU.mult).then_inc(gate_ok, 1)
            dve.wait_ge(gate_ok, 1)
            dve.tensor_copy(gates[:, :, :].rearrange("p t (c e) -> p t c e", e=EXPERTS),
                            gate[:, :, :].unsqueeze(2).to_broadcast([P, TT, CHUNKS + 1, EXPERTS]))
            dve.wait_ge(pos_ps, 1)
            step(dve.scalar_tensor_tensor(out=pm[:, :, :], in0=B[7][:, 0:64].rearrange("p (t e) -> p t e", t=TT), scalar=1.0,
                                          in1=sel[:, :, :], op0=ALU.add, op1=ALU.mult))
            for c in range(CHUNKS + 1):
                last = dve.tensor_scalar(posc[:, :, c * EXPERTS:(c + 1) * EXPERTS], pm[:, :, :], -1.0 - SLOTS * c, None, ALU.add)
            step(last)
            def prepare(i):
                for t in range(TT):
                    dve.tensor_scalar(onehot[:, t, :], const("slot")[:, 0:SLOTS], posc[:, t, bass.ds(i, 1)], None, ALU.is_equal)
                    last = dve.tensor_scalar(gated[:, t, :], const("slot"), posc[:, t, bass.ds(i, 1)],
                                             gates[:, t, bass.ds(i, 1)], ALU.is_equal, ALU.mult)
                last.then_inc(prep_ok, 1)

            prepare(0)
            step(dve.tensor_reduce(r_s[:, 0, 0:1], B[7][:, 64:96], AXX, ALU.max))
            for c in range(1, CHUNKS):
                last = dve.tensor_scalar(r_s[:, 0, c:c + 1], r_s[:, 0, 0:1], float(SLOTS * c), float(EXPERTS), ALU.is_gt, ALU.mult)
            step(last)
            step(dve.tensor_reduce(r_s[:, 0, 0:1], r_s[:, 0, 1:4], AXX, ALU.add))
            dve.tensor_scalar(n_items[:, :], r_s[:, 0, 0:1], float(EXPERTS), None, ALU.add).then_inc(n_ok, 1)

            def split_x(n):
                dve.wait_ge(xh_ok, n)
                dve.tensor_tensor(xe[:, :, 1, :], PREP[:, :].rearrange("p (c s) -> p c s", c=KC),
                                  xe[:, :, 0, :].bitcast(F32), ALU.subtract).then_inc(xl_ok, 1)

            dve.wait_ge(n_ok, 1)
            dve.memset(stat[:, 12:13], 0.0).then_inc(gub_ok, 1)
            split_x(1)
            items = dve.value_load(n_items[0:1, 0:1], min_val=EXPERTS, max_val=EXPERTS * CHUNKS)

            def item(i, first):
                e = i % EXPERTS if isinstance(i, int) else dve.snap(i % EXPERTS)

                def add_bias(half):
                    dve.wait_ge(ev_used, UNITS * i + (2 + 2 * half + 2))
                    dve.tensor_tensor(gub[:, :, :, :].rearrange("p a c s -> p (a c) s"),
                                      GUT[:, :].rearrange("p (j s) -> p j s", s=SLOTS),
                                      bias_gu[:, bass.ds(e, 1), 8 * half:8 * half + 8].rearrange("p a j -> p (a j)")
                                      .unsqueeze(2).to_broadcast([P, 8, SLOTS]), ALU.add).then_inc(gub_ok, 1)
                    dve.wait_ge(gub_ok, 2 * i + (1 + half + 1))
                    dve.tensor_scalar(glu, glu, LIMIT, None, ALU.min).then_inc(glu_ok, 1)
                    dve.tensor_scalar(lin, lin, LIMIT, -LIMIT, ALU.min, ALU.max).then_inc(lin_ok, 1)

                def product(half):
                    dve.wait_ge(lin_ok, 2 * i + (half + 1))
                    dve.scalar_tensor_tensor(out=lin, in0=lin, scalar=1.0, in1=glu,
                                             op0=ALU.add, op1=ALU.mult).then_inc(prod_ok, 1)

                def low_act(half):
                    dve.wait_ge(ah_ok, 2 * i + (half + 1))
                    dve.tensor_tensor(ae[:, 4 * half:4 * half + 4, 1, :], sig[:, :, :],
                                      ae[:, 4 * half:4 * half + 4, 0, :].bitcast(F32), ALU.subtract).then_inc(al_ok, 1)

                before = 6 if first else 5
                for p in range(SPLITS if first else 0, before):
                    low(i, p)
                dve.wait_ge(sc_ok, i + 1)
                prepare(i + 1)
                for p in range(before, 7):
                    low(i, p)
                add_bias(0)
                product(0)
                low(i, 7)
                low_act(0)
                low(i, 8)
                low(i, 9)
                add_bias(1)
                product(1)
                low(i, 10)
                low_act(1)
                low(i, 11)
                split_x(i + 2)

            item(0, True)
            with dve.Fori(1, items) as i:
                item(i, False)
            dve.wait_ge(final_in, 32)
            for n in range(2):
                dve.wait_ge(ev_used, UNITS * items + (1 + n))
                for t in range(TT):
                    at = slice(n * BLK, (n + 1) * BLK)
                    dve.tensor_tensor(xs[:, t, at], xs[:, t, at], ACC[2 * t + n][:, :], ALU.add).then_inc(y_ok, 1)
            for t in range(TT):
                dve.wait_ge(y_sq, t + 1)
                dve.tensor_scalar(stat[:, 2 + t:3 + t], stat[:, t:t + 1], 1.0 / D, EPS, ALU.mult, ALU.add).then_inc(y_ms, 1)
                dve.wait_ge(y_rt, t + 1)
                dve.reciprocal(stat[:, t:t + 1], stat[:, 4 + t:5 + t]).then_inc(fin_r, 1)
                dve.wait_ge(fin_r, t + 1)
                for n in range(2):
                    at = slice(n * BLK, (n + 1) * BLK)
                    dve.scalar_tensor_tensor(out=xs[:, t, at], in0=xs[:, t, at], scalar=stat[:, t:t + 1], in1=gain[:, at],
                                             op0=ALU.mult, op1=ALU.mult).then_inc(o_ok, 1)

        @block.gpsimd
        def _(pool):
            step = stepper(pool, pool_step)

            def rotate(view, heads, half, every):
                ta, tb = (x[:, :, 0:heads, 0:2 * half] for x in (ropc, ropd))
                shape = [P, TT, heads, half]
                cos = trig[:, 0, :, 0:16:every].unsqueeze(2).to_broadcast(shape)
                sin = trig[:, 1, :, 0:16:every].unsqueeze(2).to_broadcast(shape)
                neg = nsin[:, :, 0:16:every].unsqueeze(2).to_broadcast(shape)
                x1, x2 = view[:, :, :, 0:half], view[:, :, :, half:2 * half]
                pool.tensor_tensor(ta[:, :, :, 0:half], x1, cos, ALU.mult)
                pool.tensor_tensor(ta[:, :, :, half:2 * half], x2, cos, ALU.mult)
                pool.tensor_tensor(tb[:, :, :, 0:half], x2, neg, ALU.mult)
                step(pool.tensor_tensor(tb[:, :, :, half:2 * half], x1, sin, ALU.mult))
                return pool.tensor_tensor(view, ta, tb, ALU.add)

            pool.wait_ge(nsin_ok, 1)
            pool.wait_ge(z_ok, 6)
            step(rotate(z_qb[:, :, :].rearrange("p t (h d) -> p t h d", h=HEADS)[:, :, :, 0:ROT], HEADS, ROT // 2, 2))
            step(rotate(z_kv[:, :, 0:HD].unsqueeze(2)[:, :, :, 0:ROT], 1, ROT // 2, 2))
            pool.wait_ge(qi_ps, 3)
            for t in range(TT):
                last = pool.tensor_copy(kk[:, t, :, :], z_kv[:, t, 0:HD].unsqueeze(1).to_broadcast([P, 2, HD]))
            last.then_inc(qb_rot, 1)
            pool.wait_ge(z_ok, 8)
            pool.wait_ge(c_sq, 1)
            pool.wait_ge(idx_ac, 6)
            step(rotate(z_ml[:, :, Q_LORA + KV_LORA:C_QB].unsqueeze(2), 1, ROPE // 2, 1))
            for t in range(TT):
                last = pool.tensor_copy(k_ml[:, t, :, NOPE:QK],
                                        z_ml[:, t, Q_LORA + KV_LORA:C_QB].unsqueeze(1).to_broadcast([P, HEADS, ROPE]))
            step(last)
            pool.wait_ge(up_a, 8)
            rotate(q_ml[:, :, :, NOPE:QK], HEADS, ROPE // 2, 1).then_inc(ml_rot, 1)

            pool.wait_ge(n_ok, 1)
            items = pool.value_load(n_items[0:1, 0:1], min_val=EXPERTS, max_val=EXPERTS * CHUNKS)
            with pool.Fori(0, items) as i:
                for half in range(2):
                    pool.wait_ge(prod_ok, 2 * i + (half + 1))
                    pool.wait_ge(sig2_ok, 2 * i + (half + 1))
                    pool.tensor_tensor(sig[:, :, :], lin, sig[:, :, :], ALU.mult).then_inc(actv_ok, 1)


_INS = ['x', 'positions', 'attn_norm_g', 'w_in', 'mla_q_norm_g', 'mla_w_uq', 'mla_kv_norm_g', 'mla_w_ukv',
        'w_branch_mla', 'w_branch_dsa', 'w_out', 'ffn_norm_g', 'router_w', 'router_b',
        'w_gate_up', 'b_gate_up', 'w_down', 'b_down', 'final_norm_g']


def kernel(**inputs):
    import concourse.bacc as _bacc
    from concourse.bass_utils import run_bass_kernel_spmd as _run

    nc = _bacc.Bacc("TRN2", target_bir_lowering=False, num_devices=1)
    arrays, args = {}, []
    for name in _INS + ['consts']:
        a = constants() if name == 'consts' else np.ascontiguousarray(inputs[name])
        arrays[f"in_{name}"] = a
        args.append(nc.dram_tensor(f"in_{name}", a.shape, mybir.dt.from_np(a.dtype), kind="ExternalInput").ap())
    args.append(nc.dram_tensor("out_y", (1, TOKENS, D), F32, kind="ExternalOutput").ap())
    build(nc, *args)
    r = _run(nc, [arrays], core_ids=[0])
    return r.results[0]["out_y"]
```
